# Optimizing a Trainium2 kernel written in Bass

```python
import math
import jax, jax.numpy as jnp
from jax import lax
import numpy as np
import jax
import jax.numpy as jnp

D_MODEL = 1024
BATCH = 1
SEQ = 512
DEPTH = 1

HEAD_DIM = 64
N_ATTN_HEADS = 8
N_HGRN_HEADS = 8
ATTN_WIDTH = N_ATTN_HEADS * HEAD_DIM
HGRN_WIDTH = N_HGRN_HEADS * HEAD_DIM
MIX_WIDTH = ATTN_WIDTH + HGRN_WIDTH
IN_PROJ_WIDTH = 3 * ATTN_WIDTH + 4 * HGRN_WIDTH
DILATED_CONFIGS = ((128, 1), (512, 4), (2048, 16))
ATTN_BLOCK = 128
HGRN_CHUNK = 32
N_GROUPS = 4
EXPERTS_PER_GROUP = 8
N_EXPERTS = N_GROUPS * EXPERTS_PER_GROUP
EXPERT_TOP_K = 2
D_EXPERT = 512
MOE_BLOCK = 128
EPS = 1e-6


def rmsnorm(x, g):
    xf = x.astype(jnp.float32)
    y = xf * lax.rsqrt(jnp.mean(xf * xf, axis=-1, keepdims=True) + EPS)
    return (y * g.astype(jnp.float32)).astype(x.dtype)

def alibi_slopes(n_heads):
    return 2.0 ** (-8.0 * jnp.arange(1, n_heads + 1, dtype=jnp.float32) / n_heads)

def dilated_branch(q, k, v, slopes, window, dilation):
    B, S, H, Dh = q.shape
    n_keys = window // dilation
    assert n_keys <= ATTN_BLOCK
    U = S // dilation
    nb = -(-U // ATTN_BLOCK)
    Up = nb * ATTN_BLOCK

    def to_blocks(t):
        t = t.reshape(B, U, dilation, H, Dh).transpose(0, 2, 1, 3, 4)
        t = jnp.pad(t, ((0, 0), (0, 0), (0, Up - U), (0, 0), (0, 0)))
        return t.reshape(B, dilation, nb, ATTN_BLOCK, H, Dh)

    def from_blocks(t):
        rest = t.shape[4:]
        t = t.reshape((B, dilation, Up) + rest)[:, :, :U]
        return jnp.swapaxes(t, 1, 2).reshape((B, S) + rest)

    def with_prev(t):
        prev = jnp.pad(t, ((0, 0), (0, 0), (1, 0), (0, 0), (0, 0), (0, 0)))[:, :, :-1]
        return jnp.concatenate([prev, t], axis=3)

    qb = to_blocks(q)
    kk = with_prev(to_blocks(k))
    vv = with_prev(to_blocks(v))
    scores = jnp.einsum('bgnqhd,bgnkhd->bgnhqk', qb, kk,
                        preferred_element_type=jnp.float32) / math.sqrt(Dh)
    qi = jnp.arange(ATTN_BLOCK)[:, None]
    ki = jnp.arange(2 * ATTN_BLOCK)[None, :]
    sub_dist = qi + ATTN_BLOCK - ki
    band = (sub_dist >= 0) & (sub_dist <= n_keys)
    key_pos = jnp.arange(nb)[:, None, None] * ATTN_BLOCK + ki[None] - ATTN_BLOCK
    valid = band[None] & (key_pos >= 0)
    bias = -slopes[:, None, None] * (sub_dist * dilation).astype(jnp.float32)[None]
    scores = jnp.where(valid[None, None, :, None], scores + bias[None, None, None], -jnp.inf)
    lse = jax.nn.logsumexp(scores, axis=-1)
    p = jnp.exp(scores - lse[..., None])
    o = jnp.einsum('bgnhqk,bgnkhd->bgnqhd', p, vv.astype(jnp.float32))
    return from_blocks(o), from_blocks(jnp.swapaxes(lse, -1, -2))

def dilated_attention(q, k, v):
    slopes = alibi_slopes(q.shape[2])
    outs, lses = [], []
    for window, dilation in DILATED_CONFIGS:
        o_c, lse_c = dilated_branch(q, k, v, slopes, window, dilation)
        outs.append(o_c)
        lses.append(lse_c)
    w = jax.nn.softmax(jnp.stack(lses, axis=0), axis=0)
    return jnp.sum(w[..., None] * jnp.stack(outs, axis=0), axis=0)

def hgrn2(q, f_raw, i_in, lb):
    B, S, H, Dk = q.shape
    Dv = i_in.shape[-1]
    C = HGRN_CHUNK
    nC = S // C
    f32 = jnp.float32
    q, f_raw, i_in = q.astype(f32), f_raw.astype(f32), i_in.astype(f32)
    lb = lb.reshape(H, Dk)
    log_f = jnp.log(lb + (1.0 - lb) * jax.nn.sigmoid(f_raw))
    key = (1.0 - lb) * jax.nn.sigmoid(-f_raw)
    q = jax.nn.silu(q)
    rs = lambda t: t.reshape(B, nC, C, H, t.shape[-1])
    qc, kc, vc, lfc = rs(q), rs(key), rs(i_in), rs(log_f)
    b = jnp.cumsum(lfc, axis=2)
    b_last = b[:, :, -1:]
    q_in = qc * jnp.exp(b)
    k_in = kc * jnp.exp(-b)
    k_end = kc * jnp.exp(b_last - b)
    causal = jnp.tril(jnp.ones((C, C), dtype=bool))
    A = jnp.where(causal, jnp.einsum('bnthk,bnshk->bnhts', q_in, k_in), 0.0)
    o_intra = jnp.einsum('bnhts,bnshv->bnthv', A, vc)
    dS = jnp.einsum('bnshk,bnshv->bnhkv', k_end, vc)
    decay = jnp.exp(b_last[:, :, 0])

    def step(S_prev, inp):
        dec, ds = inp
        return dec[..., None] * S_prev + ds, S_prev

    S0 = jnp.zeros((B, H, Dk, Dv), f32)
    _, S_prevs = lax.scan(step, S0, (jnp.swapaxes(decay, 0, 1), jnp.swapaxes(dS, 0, 1)))
    S_prevs = jnp.swapaxes(S_prevs, 0, 1)
    o_inter = jnp.einsum('bnthk,bnhkv->bnthv', q_in, S_prevs)
    return (o_intra + o_inter).reshape(B, S, H, Dv)

def hier_moe(h, w_group, b_group, w_router, b_router, w_gate, w_up, w_down):
    B, S, D = h.shape
    N = B * S
    f32 = jnp.float32
    xf = h.reshape(N, D)
    grp_logits = (xf @ w_group).astype(f32) + b_group.astype(f32)
    p_grp = jax.nn.softmax(grp_logits, axis=-1)
    g_sel = jnp.argmax(grp_logits, axis=-1).astype(jnp.int32)
    w_g = jnp.take_along_axis(p_grp, g_sel[:, None], axis=1)
    exp_logits = ((xf @ w_router).astype(f32) + b_router.astype(f32)).reshape(N, N_GROUPS, EXPERTS_PER_GROUP)
    sel_logits = jnp.take_along_axis(exp_logits, g_sel[:, None, None], axis=1)[:, 0]
    top_vals, top_idx = lax.top_k(sel_logits, EXPERT_TOP_K)
    gate = w_g * jax.nn.softmax(top_vals, axis=-1)
    eid = (g_sel[:, None] * EXPERTS_PER_GROUP + top_idx).reshape(-1).astype(jnp.int32)
    tok = jnp.repeat(jnp.arange(N, dtype=jnp.int32), EXPERT_TOP_K)
    A_n = N * EXPERT_TOP_K
    order = jnp.argsort(eid)
    eid_s, tok_s, gate_s = eid[order], tok[order], gate.reshape(-1)[order]
    counts = jnp.bincount(eid, length=N_EXPERTS).astype(jnp.int32)
    starts = jnp.cumsum(counts) - counts
    padded = ((counts + MOE_BLOCK - 1) // MOE_BLOCK) * MOE_BLOCK
    pad_ends = jnp.cumsum(padded)
    pad_starts = pad_ends - padded
    dest = pad_starts[eid_s] + jnp.arange(A_n, dtype=jnp.int32) - starts[eid_s]
    P = (-(-A_n // MOE_BLOCK)) * MOE_BLOCK + N_EXPERTS * MOE_BLOCK
    n_blocks = P // MOE_BLOCK
    buf_tok = jnp.full((P,), N, jnp.int32).at[dest].set(tok_s)
    buf_gate = jnp.zeros((P,), f32).at[dest].set(gate_s)
    block_expert = jnp.minimum(
        jnp.searchsorted(pad_ends, jnp.arange(n_blocks, dtype=jnp.int32) * MOE_BLOCK, side='right'),
        N_EXPERTS - 1).astype(jnp.int32)
    x_pad = jnp.concatenate([xf, jnp.zeros((1, D), xf.dtype)], axis=0)

    def run_block(args):
        e, toks, gts = args
        xb = x_pad[toks]
        hid = jax.nn.silu(xb @ w_gate[e]) * (xb @ w_up[e])
        return ((hid @ w_down[e]) * gts[:, None].astype(xb.dtype)).astype(h.dtype)

    y = lax.map(run_block, (block_expert, buf_tok.reshape(n_blocks, MOE_BLOCK),
                            buf_gate.reshape(n_blocks, MOE_BLOCK)))
    out = jnp.zeros((N + 1, D), h.dtype).at[buf_tok].add(y.reshape(P, D))[:N]
    return out.reshape(B, S, D)

def first_inputs(seed: int = 0) -> dict:
    key = jax.random.key(seed)
    ks = jax.random.split(key, 16)
    f32 = jnp.float32
    nrm = lambda k, shape, scale: jax.random.normal(k, shape, f32) * scale
    L = DEPTH
    return {
        "x": jax.random.normal(ks[0], (BATCH, SEQ, D_MODEL), f32),
        "norm1_g": 1.0 + nrm(ks[1], (L, D_MODEL), 0.05),
        "w_in": nrm(ks[2], (L, D_MODEL, IN_PROJ_WIDTH), D_MODEL ** -0.5),
        "attn_norm_g": 1.0 + nrm(ks[3], (L, ATTN_WIDTH), 0.05),
        "hgrn_gamma": nrm(ks[4], (L + 1, HGRN_WIDTH), 0.1),
        "hgrn_norm_g": 1.0 + nrm(ks[5], (L, HGRN_WIDTH), 0.05),
        "w_out": nrm(ks[6], (L, MIX_WIDTH, D_MODEL), MIX_WIDTH ** -0.5),
        "norm2_g": 1.0 + nrm(ks[7], (L, D_MODEL), 0.05),
        "w_group": nrm(ks[8], (L, D_MODEL, N_GROUPS), D_MODEL ** -0.5),
        "b_group": nrm(ks[9], (L, N_GROUPS), 0.01),
        "w_router": nrm(ks[10], (L, D_MODEL, N_EXPERTS), D_MODEL ** -0.5),
        "b_router": nrm(ks[11], (L, N_EXPERTS), 0.01),
        "w_gate": nrm(ks[12], (L, N_EXPERTS, D_MODEL, D_EXPERT), D_MODEL ** -0.5),
        "w_up": nrm(ks[13], (L, N_EXPERTS, D_MODEL, D_EXPERT), D_MODEL ** -0.5),
        "w_down": nrm(ks[14], (L, N_EXPERTS, D_EXPERT, D_MODEL), D_EXPERT ** -0.5),
        "norm_f_g": 1.0 + nrm(ks[15], (D_MODEL,), 0.05),
    }

def first_block(x, norm1_g, w_in, attn_norm_g, hgrn_gamma, hgrn_norm_g, w_out, norm2_g,
              w_group, b_group, w_router, b_router, w_gate, w_up, w_down, norm_f_g):
    B, S, _ = x.shape
    split_at = [ATTN_WIDTH, 2 * ATTN_WIDTH, 3 * ATTN_WIDTH,
                3 * ATTN_WIDTH + HGRN_WIDTH, 3 * ATTN_WIDTH + 2 * HGRN_WIDTH,
                3 * ATTN_WIDTH + 3 * HGRN_WIDTH]
    lower_bounds = jnp.cumsum(jax.nn.softmax(hgrn_gamma.astype(jnp.float32), axis=0), axis=0)
    for layer in range(DEPTH):
        h = rmsnorm(x, norm1_g[layer])
        proj = h @ w_in[layer]
        qa, ka, va, qh, fh, ih, gh = jnp.split(proj, split_at, axis=-1)
        heads = lambda t, n: t.reshape(B, S, n, HEAD_DIM)
        o_attn = dilated_attention(heads(qa, N_ATTN_HEADS), heads(ka, N_ATTN_HEADS),
                                   heads(va, N_ATTN_HEADS)).reshape(B, S, ATTN_WIDTH)
        y_attn = rmsnorm(o_attn, attn_norm_g[layer])
        o_h = hgrn2(heads(qh, N_HGRN_HEADS), heads(fh, N_HGRN_HEADS), heads(ih, N_HGRN_HEADS),
                    lower_bounds[layer])
        o_h = rmsnorm(o_h, hgrn_norm_g[layer].reshape(N_HGRN_HEADS, HEAD_DIM)).reshape(B, S, HGRN_WIDTH)
        y_hgrn = o_h * jax.nn.silu(gh.astype(jnp.float32))
        mixed = jnp.concatenate([y_attn, y_hgrn], axis=-1).astype(x.dtype)
        x = x + mixed @ w_out[layer]
        h2 = rmsnorm(x, norm2_g[layer])
        x = x + hier_moe(h2, w_group[layer], b_group[layer], w_router[layer], b_router[layer],
                         w_gate[layer], w_up[layer], w_down[layer])
    return rmsnorm(x, norm_f_g)


DEPTH_2 = 2

GRID_W = 64
CTX_LEN = 256
N_EVEN = (DEPTH_2 + 1) // 2
N_ODD = DEPTH_2 // 2
D_FF = 4 * D_MODEL
N_MOD = 6
F32 = jnp.float32

MLA_HEADS = 8
MLA_NOPE = 64
MLA_ROPE = 32
MLA_V = 64
MLA_QK = MLA_NOPE + MLA_ROPE
MLA_Q_RANK = 3 * D_MODEL // 8
MLA_KV_RANK = D_MODEL // 4
ROPE_THETA = 10000.0
Q_BLOCK = 128

GLA_HEADS = 4
GLA_DK = 64
GLA_DV = 128
GLA_GATE_RANK = 16
GLA_GATE_NORM = 16.0
GLA_CHUNK = 64

GDN_HEADS = 8
GDN_DK = 64
GDN_DV = 128
GDN_CONV = 3
GDN_CHUNK = 64

EVEN_SPLITS = (MLA_Q_RANK, MLA_KV_RANK, MLA_ROPE,
               GLA_HEADS * GLA_DK, GLA_HEADS * GLA_DK, GLA_HEADS * GLA_DV, GLA_HEADS * GLA_DV,
               2 * GLA_GATE_RANK)
EVEN_IN = 2240
MIX_WIDTH_2 = MLA_HEADS * MLA_V + GLA_HEADS * GLA_DV
GDN_QKV = 2 * GDN_HEADS * GDN_DK + GDN_HEADS * GDN_DV
ODD_SPLITS = (GDN_QKV, GDN_HEADS * GDN_DV, 2 * GDN_HEADS, 2 * GDN_HEADS)
ODD_IN = 3104
GDN_WIDTH = GDN_HEADS * GDN_DV


def rms_norm(x, w):
    xf = x.astype(F32)
    y = xf * lax.rsqrt(jnp.mean(xf * xf, axis=-1, keepdims=True) + EPS)
    return (y * w.astype(F32)).astype(x.dtype)

def l2norm(t):
    tf = t.astype(F32)
    return (tf * lax.rsqrt(jnp.sum(tf * tf, axis=-1, keepdims=True) + EPS)).astype(t.dtype)

def split_cols(y, sizes):
    out, start = [], 0
    for s in sizes:
        out.append(y[..., start:start + s])
        start += s
    return out

def modulate(h, shift, scale):
    return h * (1.0 + scale) + shift

def flip_seq(ts):
    return tuple(jnp.flip(t, axis=2) for t in ts)

def axial_rope_tables(n_tokens):
    rows = n_tokens // GRID_W
    row = jnp.repeat(jnp.arange(rows, dtype=F32), GRID_W)
    col = jnp.tile(jnp.arange(GRID_W, dtype=F32), rows)
    axis_dim = MLA_ROPE // 2
    inv_freq = ROPE_THETA ** (-jnp.arange(0, axis_dim, 2, dtype=F32) / axis_dim)
    ang = jnp.concatenate([row[:, None] * inv_freq, col[:, None] * inv_freq], axis=-1)
    return jnp.cos(ang), jnp.sin(ang)

def apply_axial_rope(x, cos, sin):
    shp = x.shape
    nf = MLA_ROPE // 4
    xf = x.astype(F32).reshape(shp[:-1] + (2, 2, nf))
    x1, x2 = xf[..., 0, :], xf[..., 1, :]
    cos = cos.reshape(-1, 2, nf)
    sin = sin.reshape(-1, 2, nf)
    out = jnp.stack([x1 * cos - x2 * sin, x2 * cos + x1 * sin], axis=-2)
    return out.reshape(shp).astype(x.dtype)

def mla_attend(q, k, v):
    B, H, Lq, D = q.shape
    scale = MLA_QK ** -0.5
    nb = Lq // Q_BLOCK
    qb = jnp.moveaxis(q.reshape(B, H, nb, Q_BLOCK, D), 2, 0)

    def one(qblk):
        s = jnp.einsum('bhqd,bhkd->bhqk', qblk, k).astype(F32) * scale
        p = jax.nn.softmax(s, axis=-1).astype(v.dtype)
        return jnp.einsum('bhqk,bhkv->bhqv', p, v)

    o = lax.map(one, qb)
    return jnp.moveaxis(o, 0, 2).reshape(B, H, Lq, v.shape[-1])

def gla_chunked(q, k, v, logg, s0):
    out_dtype = v.dtype
    q, k, v, logg = (t.astype(F32) for t in (q, k, v, logg))
    B, H, L, DK = q.shape
    DV = v.shape[-1]
    C = GLA_CHUNK
    n = L // C
    q = q.reshape(B, H, n, C, DK) * DK ** -0.5
    k = k.reshape(B, H, n, C, DK)
    v = v.reshape(B, H, n, C, DV)
    b = jnp.cumsum(logg.reshape(B, H, n, C, DK), axis=3)
    q_dec = q * jnp.exp(b)
    k_inv = k * jnp.exp(-b)
    k_end = k * jnp.exp(b[..., -1:, :] - b)
    g_end = jnp.exp(b[..., -1, :])
    incl = jnp.tril(jnp.ones((C, C), bool))
    a = jnp.where(incl, jnp.einsum('bhnid,bhnjd->bhnij', q_dec, k_inv), 0.0)
    o_intra = jnp.einsum('bhnij,bhnjv->bhniv', a, v)

    def step(s, xs):
        qd_c, ke_c, v_c, ge_c = xs
        o = jnp.einsum('bhcd,bhdv->bhcv', qd_c, s)
        s = s * ge_c[..., None] + jnp.einsum('bhcd,bhcv->bhdv', ke_c, v_c)
        return s, o

    xs = tuple(jnp.moveaxis(t, 2, 0) for t in (q_dec, k_end, v, g_end))
    s_fin, o_inter = lax.scan(step, s0, xs)
    o = o_intra + jnp.moveaxis(o_inter, 0, 2)
    return o.reshape(B, H, L, DV).astype(out_dtype), s_fin

def gdn_chunked(q, k, v, log_a, beta, s0):
    out_dtype = v.dtype
    q, k, v, log_a, beta = (t.astype(F32) for t in (q, k, v, log_a, beta))
    B, H, L, DK = q.shape
    DV = v.shape[-1]
    C = GDN_CHUNK
    n = L // C
    q = q.reshape(B, H, n, C, DK) * DK ** -0.5
    k = k.reshape(B, H, n, C, DK)
    v = v.reshape(B, H, n, C, DV)
    beta = beta.reshape(B, H, n, C)[..., None]
    g = jnp.cumsum(log_a.reshape(B, H, n, C), axis=-1)
    incl = jnp.tril(jnp.ones((C, C), bool))
    strict = jnp.tril(jnp.ones((C, C), bool), -1)
    diff = g[..., :, None] - g[..., None, :]
    decay = jnp.where(incl, jnp.exp(jnp.where(incl, diff, 0.0)), 0.0)
    kb = k * beta
    a_mat = jnp.where(strict, jnp.einsum('bhnid,bhnjd->bhnij', kb, k) * decay, 0.0) + jnp.eye(C, dtype=F32)
    rhs = jnp.concatenate([v * beta, kb * jnp.exp(g)[..., None]], axis=-1)
    sol = lax.linalg.triangular_solve(a_mat, rhs, left_side=True, lower=True)
    u, w = sol[..., :DV], sol[..., DV:]
    qk = jnp.einsum('bhnid,bhnjd->bhnij', q, k) * decay
    q_dec = q * jnp.exp(g)[..., None]
    k_end = k * jnp.exp(g[..., -1:] - g)[..., None]
    g_end = jnp.exp(g[..., -1])

    def step(s, xs):
        qk_c, qd_c, w_c, u_c, ke_c, ge_c = xs
        v_new = u_c - jnp.einsum('bhcd,bhdv->bhcv', w_c, s)
        o = jnp.einsum('bhcd,bhdv->bhcv', qd_c, s) + jnp.einsum('bhcs,bhsv->bhcv', qk_c, v_new)
        s = s * ge_c[..., None, None] + jnp.einsum('bhcd,bhcv->bhdv', ke_c, v_new)
        return s, o

    xs = tuple(jnp.moveaxis(t, 2, 0) for t in (qk, q_dec, w, u, k_end, g_end))
    s_fin, o = lax.scan(step, s0, xs)
    o = jnp.moveaxis(o, 0, 2).reshape(B, H, L, DV)
    return o.astype(out_dtype), s_fin

def bidir_scan(scan_fn, ctx_f, ctx_b, lat_f, lat_b, s0):
    o_cf, s_f = scan_fn(*ctx_f, s0)
    o_cb, s_b = scan_fn(*flip_seq(ctx_b), s0)
    o_lf, _ = scan_fn(*lat_f, s_f)
    o_lb, _ = scan_fn(*flip_seq(lat_b), s_b)
    return o_lf + jnp.flip(o_lb, axis=2), (o_cf, o_cb)

def even_project(y, q_norm, w_uq, kv_norm, w_ukv, gate_up, gate_bias, rope):
    cq, ckv, kpe, gq, gk, gv, gg, glow = split_cols(y, EVEN_SPLITS)
    B, L, _ = y.shape
    q = (rms_norm(cq, q_norm) @ w_uq).reshape(B, L, MLA_HEADS, MLA_QK).transpose(0, 2, 1, 3)
    q_nope, q_pe = q[..., :MLA_NOPE], q[..., MLA_NOPE:]
    kv = (rms_norm(ckv, kv_norm) @ w_ukv).reshape(B, L, MLA_HEADS, MLA_NOPE + MLA_V).transpose(0, 2, 1, 3)
    k_nope, mv = kv[..., :MLA_NOPE], kv[..., MLA_NOPE:]
    if rope is not None:
        q_pe = apply_axial_rope(q_pe, *rope)
        kpe = apply_axial_rope(kpe, *rope)
    mq = jnp.concatenate([q_nope, q_pe], axis=-1)
    mk = jnp.concatenate([k_nope, jnp.broadcast_to(kpe[:, None], (B, MLA_HEADS, L, MLA_ROPE))], axis=-1)
    glow = glow.reshape(B, L, 2, GLA_GATE_RANK)
    logit = jnp.einsum('blzr,zrk->zblk', glow, gate_up) + gate_bias[:, None, None, :]
    logg = jax.nn.log_sigmoid(logit.astype(F32)) / GLA_GATE_NORM
    logg = logg.reshape(2, B, L, GLA_HEADS, GLA_DK).transpose(0, 1, 3, 2, 4)
    heads = lambda t, d: t.reshape(B, L, -1, d).transpose(0, 2, 1, 3)
    return (mq, mk, mv, heads(gq, GLA_DK), heads(gk, GLA_DK), heads(gv, GLA_DV), gg, logg[0], logg[1])

def even_merge(att, gla, gg, o_norm, w_out):
    B, _, L, _ = att.shape
    att = att.transpose(0, 2, 1, 3).reshape(B, L, MLA_HEADS * MLA_V)
    gla = rms_norm(gla.transpose(0, 2, 1, 3), o_norm) * jax.nn.silu(gg.reshape(B, L, GLA_HEADS, GLA_DV))
    return jnp.concatenate([att, gla.reshape(B, L, GLA_HEADS * GLA_DV)], axis=-1) @ w_out

def even_mixer(a_lat, a_ctx, w_in, q_norm, w_uq, kv_norm, w_ukv, gate_up, gate_bias, o_norm, w_out, rope, need_ctx):
    mq_l, mk_l, mv_l, gq_l, gk_l, gv_l, gg_l, lf_l, lb_l = even_project(
        a_lat @ w_in, q_norm, w_uq, kv_norm, w_ukv, gate_up, gate_bias, rope)
    mq_c, mk_c, mv_c, gq_c, gk_c, gv_c, gg_c, lf_c, lb_c = even_project(
        a_ctx @ w_in, q_norm, w_uq, kv_norm, w_ukv, gate_up, gate_bias, None)
    att_l = mla_attend(mq_l, jnp.concatenate([mk_l, mk_c], axis=2), jnp.concatenate([mv_l, mv_c], axis=2))
    B = a_lat.shape[0]
    s0 = jnp.zeros((B, GLA_HEADS, GLA_DK, GLA_DV), F32)
    gla_l, (o_cf, o_cb) = bidir_scan(gla_chunked, (gq_c, gk_c, gv_c, lf_c), (gq_c, gk_c, gv_c, lb_c),
                                     (gq_l, gk_l, gv_l, lf_l), (gq_l, gk_l, gv_l, lb_l), s0)
    o_lat = even_merge(att_l, gla_l, gg_l, o_norm, w_out)
    o_ctx = None
    if need_ctx:
        att_c = mla_attend(mq_c, mk_c, mv_c)
        o_ctx = even_merge(att_c, o_cf + jnp.flip(o_cb, axis=2), gg_c, o_norm, w_out)
    return o_lat, o_ctx

def short_conv(x, w):
    ch = x.shape[-1]
    y = lax.conv_general_dilated(x, w[:, None, :], window_strides=(1,),
                                 padding=[((GDN_CONV - 1) // 2, GDN_CONV // 2)],
                                 dimension_numbers=('NWC', 'WIO', 'NWC'), feature_group_count=ch)
    return jax.nn.silu(y)

def odd_project(a, w_in, conv_w, a_log, dt_bias):
    B, L, _ = a.shape
    qkv, g, a_in, b_in = split_cols(a @ w_in, ODD_SPLITS)
    q, k, v = split_cols(short_conv(qkv, conv_w), (GDN_HEADS * GDN_DK, GDN_HEADS * GDN_DK, GDN_HEADS * GDN_DV))
    heads = lambda t, d: t.reshape(B, L, GDN_HEADS, d).transpose(0, 2, 1, 3)
    q = l2norm(heads(q, GDN_DK))
    k = l2norm(heads(k, GDN_DK))
    v = heads(v, GDN_DV)
    a_in = a_in.reshape(B, L, 2, GDN_HEADS).astype(F32)
    log_a = -jnp.exp(a_log.astype(F32)) * jax.nn.softplus(a_in + dt_bias.astype(F32))
    beta = jax.nn.sigmoid(b_in.reshape(B, L, 2, GDN_HEADS).astype(F32))
    return q, k, v, g, log_a.transpose(2, 0, 3, 1), beta.transpose(2, 0, 3, 1)

def odd_merge(o, g, o_norm, w_out):
    B, _, L, _ = o.shape
    o = rms_norm(o.transpose(0, 2, 1, 3), o_norm) * jax.nn.silu(g.reshape(B, L, GDN_HEADS, GDN_DV))
    return o.reshape(B, L, GDN_WIDTH) @ w_out

def odd_mixer(a_lat, a_ctx, w_in, conv_w, a_log, dt_bias, o_norm, w_out, need_ctx):
    lq, lk, lv, lg, lla, lbe = odd_project(a_lat, w_in, conv_w, a_log, dt_bias)
    cq, ck, cv, cg, cla, cbe = odd_project(a_ctx, w_in, conv_w, a_log, dt_bias)
    B = a_lat.shape[0]
    s0 = jnp.zeros((B, GDN_HEADS, GDN_DK, GDN_DV), F32)
    o_l, (o_cf, o_cb) = bidir_scan(gdn_chunked, (cq, ck, cv, cla[0], cbe[0]), (cq, ck, cv, cla[1], cbe[1]),
                                   (lq, lk, lv, lla[0], lbe[0]), (lq, lk, lv, lla[1], lbe[1]), s0)
    o_lat = odd_merge(o_l, lg, o_norm, w_out)
    o_ctx = None
    if need_ctx:
        o_ctx = odd_merge(o_cf + jnp.flip(o_cb, axis=2), cg, o_norm, w_out)
    return o_lat, o_ctx

def sq_relu_mlp(h, w1, w2):
    return jnp.square(jax.nn.relu(h @ w1)) @ w2

def second_inputs(seed: int = 0) -> dict:
    key = jax.random.key(seed)
    ks = iter(jax.random.split(key, 40))
    nrm = lambda shape, scale: jax.random.normal(next(ks), shape, F32) * scale
    gain = lambda shape: 1.0 + 0.05 * jax.random.normal(next(ks), shape, F32)
    d = D_MODEL
    dt = jnp.exp(jax.random.uniform(next(ks), (N_ODD, 2, GDN_HEADS), F32, np.log(1e-3), np.log(1e-1)))
    return {
        "x": nrm((BATCH, SEQ, d), 1.0),
        "c": nrm((BATCH, d), 1.0),
        "ctx": nrm((BATCH, CTX_LEN, d), 1.0),
        "c_ctx": nrm((d,), 1.0),
        "ada_w": nrm((DEPTH_2, d, N_MOD * d), 0.5 * d ** -0.5),
        "ada_b": nrm((DEPTH_2, N_MOD * d), 0.02),
        "norm1_w": gain((DEPTH_2, d)),
        "norm2_w": gain((DEPTH_2, d)),
        "mlp_w1": nrm((DEPTH_2, d, D_FF), d ** -0.5),
        "mlp_w2": nrm((DEPTH_2, D_FF, d), D_FF ** -0.5),
        "even_w_in": nrm((N_EVEN, d, EVEN_IN), d ** -0.5),
        "mla_q_norm": gain((N_EVEN, MLA_Q_RANK)),
        "mla_w_uq": nrm((N_EVEN, MLA_Q_RANK, MLA_HEADS * MLA_QK), MLA_Q_RANK ** -0.5),
        "mla_kv_norm": gain((N_EVEN, MLA_KV_RANK)),
        "mla_w_ukv": nrm((N_EVEN, MLA_KV_RANK, MLA_HEADS * (MLA_NOPE + MLA_V)), MLA_KV_RANK ** -0.5),
        "gla_gate_up": nrm((N_EVEN, 2, GLA_GATE_RANK, GLA_HEADS * GLA_DK), GLA_GATE_RANK ** -0.5),
        "gla_gate_bias": nrm((N_EVEN, 2, GLA_HEADS * GLA_DK), 0.1),
        "gla_o_norm": gain((N_EVEN, GLA_DV)),
        "even_w_out": nrm((N_EVEN, MIX_WIDTH_2, d), MIX_WIDTH_2 ** -0.5),
        "gdn_w_in": nrm((N_ODD, d, ODD_IN), d ** -0.5),
        "gdn_conv_w": nrm((N_ODD, GDN_CONV, GDN_QKV), GDN_CONV ** -0.5),
        "gdn_a_log": jnp.log(jax.random.uniform(next(ks), (N_ODD, 2, GDN_HEADS), F32, 1.0, 16.0)),
        "gdn_dt_bias": dt + jnp.log(-jnp.expm1(-dt)),
        "gdn_o_norm": gain((N_ODD, GDN_DV)),
        "gdn_w_out": nrm((N_ODD, GDN_WIDTH, d), GDN_WIDTH ** -0.5),
        "final_norm": gain((d,)),
    }

def second_block(x, c, ctx, c_ctx, ada_w, ada_b, norm1_w, norm2_w, mlp_w1, mlp_w2,
              even_w_in, mla_q_norm, mla_w_uq, mla_kv_norm, mla_w_ukv, gla_gate_up, gla_gate_bias,
              gla_o_norm, even_w_out, gdn_w_in, gdn_conv_w, gdn_a_log, gdn_dt_bias, gdn_o_norm,
              gdn_w_out, final_norm):
    rope = axial_rope_tables(x.shape[1])
    h_lat, h_ctx = x, ctx
    for layer in range(DEPTH_2):
        need_ctx = layer < DEPTH_2 - 1
        ml = [m[:, None, :] for m in jnp.split(jax.nn.silu(c) @ ada_w[layer] + ada_b[layer], N_MOD, axis=-1)]
        mc = jnp.split(jax.nn.silu(c_ctx) @ ada_w[layer] + ada_b[layer], N_MOD, axis=-1)
        a_lat = modulate(rms_norm(h_lat, norm1_w[layer]), ml[0], ml[1])
        a_ctx = modulate(rms_norm(h_ctx, norm1_w[layer]), mc[0], mc[1])
        i = layer // 2
        if layer % 2 == 0:
            o_lat, o_ctx = even_mixer(a_lat, a_ctx, even_w_in[i], mla_q_norm[i], mla_w_uq[i], mla_kv_norm[i],
                                      mla_w_ukv[i], gla_gate_up[i], gla_gate_bias[i], gla_o_norm[i],
                                      even_w_out[i], rope, need_ctx)
        else:
            o_lat, o_ctx = odd_mixer(a_lat, a_ctx, gdn_w_in[i], gdn_conv_w[i], gdn_a_log[i], gdn_dt_bias[i],
                                     gdn_o_norm[i], gdn_w_out[i], need_ctx)
        h_lat = h_lat + ml[2] * o_lat
        h_lat = h_lat + ml[5] * sq_relu_mlp(modulate(rms_norm(h_lat, norm2_w[layer]), ml[3], ml[4]),
                                            mlp_w1[layer], mlp_w2[layer])
        if need_ctx:
            h_ctx = h_ctx + mc[2] * o_ctx
            h_ctx = h_ctx + mc[5] * sq_relu_mlp(modulate(rms_norm(h_ctx, norm2_w[layer]), mc[3], mc[4]),
                                                mlp_w1[layer], mlp_w2[layer])
    return rms_norm(h_lat, final_norm)


def setup_inputs(seed=0):
    out = dict(first_inputs(seed))
    for name, value in second_inputs(seed + 1).items():
        if name != "x":
            out[name + "_2"] = value
    return out


def reference(
    x, norm1_g, w_in, attn_norm_g, hgrn_gamma, hgrn_norm_g, w_out, norm2_g, w_group, b_group,
    w_router, b_router, w_gate, w_up, w_down, norm_f_g, c_2, ctx_2, c_ctx_2, ada_w_2, ada_b_2,
    norm1_w_2, norm2_w_2, mlp_w1_2, mlp_w2_2, even_w_in_2, mla_q_norm_2, mla_w_uq_2,
    mla_kv_norm_2, mla_w_ukv_2, gla_gate_up_2, gla_gate_bias_2, gla_o_norm_2, even_w_out_2,
    gdn_w_in_2, gdn_conv_w_2, gdn_a_log_2, gdn_dt_bias_2, gdn_o_norm_2, gdn_w_out_2,
    final_norm_2,
):
    x = first_block(
        x, norm1_g, w_in, attn_norm_g, hgrn_gamma, hgrn_norm_g, w_out, norm2_g, w_group,
        b_group, w_router, b_router, w_gate, w_up, w_down, norm_f_g,
    )
    return second_block(
        x, c_2, ctx_2, c_ctx_2, ada_w_2, ada_b_2, norm1_w_2, norm2_w_2, mlp_w1_2, mlp_w2_2,
        even_w_in_2, mla_q_norm_2, mla_w_uq_2, mla_kv_norm_2, mla_w_ukv_2, gla_gate_up_2,
        gla_gate_bias_2, gla_o_norm_2, even_w_out_2, gdn_w_in_2, gdn_conv_w_2, gdn_a_log_2,
        gdn_dt_bias_2, gdn_o_norm_2, gdn_w_out_2, final_norm_2,
    )


_drawn_inputs = setup_inputs


def setup_inputs(seed=0):
    import zlib

    import numpy as np

    out = dict(_drawn_inputs(seed))
    spreads = {}
    factors = {'b_group': 4.838,
     'b_router': 4.939,
     'norm1_w_2': 2.678,
     'mla_q_norm_2': 8.0,
     'mla_w_uq_2': 3.189,
     'mla_kv_norm_2': 8.0,
     'gla_gate_bias_2': 8.0,
     'gla_o_norm_2': 7.632,
     'gdn_o_norm_2': 27.261,
     'norm2_w_2': 5.972}
    for name, (base, spread) in spreads.items():
        noise = np.random.default_rng([zlib.crc32(name.encode()), seed]).standard_normal(out[name].shape)
        drawn = base * np.exp(spread * noise) if base else spread * noise
        out[name] = jnp.asarray(drawn.astype(out[name].dtype))
    for name, factor in factors.items():
        out[name] = (out[name] * factor).astype(out[name].dtype)
    return out
```

```python
from contextlib import ExitStack

import numpy as np
import concourse.bass as bass
from concourse import mybir

class Parts:
    pass


P = 128
D = 1024
KT = D // P
S = 512
CTX = 256
TT = S + CTX
BANK = 512
EPS = 1e-6
HEADS = 8
FP = mybir.dt.float32
ACT = mybir.ActivationFunctionType
ALU = mybir.AluOpType
AX = mybir.AxisListType

VEC_ROWS = [("norm1_g", 8), ("attn_norm_g", 4), ("hgrn_gamma", 8), ("hgrn_norm_g", 4), ("norm2_g", 8),
            ("norm_f_g", 8), ("norm1_w_2", 16), ("norm2_w_2", 16), ("mla_q_norm_2", 3), ("mla_kv_norm_2", 2),
            ("gla_gate_bias_2", 4), ("gla_o_norm_2", 1), ("gdn_o_norm_2", 1), ("final_norm_2", 8), ("c_2", 8),
            ("c_ctx_2", 8), ("ada_b_2", 96), ("gdn_conv_w_2", 48)]
VEC_AT = {}
_at = 0
for _name, _rows in VEC_ROWS:
    VEC_AT[_name] = _at
    _at += _rows
N_VEC = _at

CST = [("ident", 128), ("ones", 128), ("blk64", 128), ("hg_mask", 128), ("fwd64", 128), ("bwd64", 128),
       ("dist", 512), ("mult", 512), ("reset32", 512), ("reset64", 768), ("cos", 768), ("sin", 768),
       ("rot", 32), ("levels", 6 * 2 * 128), ("iota", 32), ("iota64", 64), ("before", 128)]
CST_AT = {}
_at = 0
for _name, _w in CST:
    CST_AT[_name] = (_at, _w)
    _at += _w
N_CST = _at


def constants():
    c = {}
    i = np.arange(P)
    c["ident"] = np.eye(P)
    c["ones"] = np.ones((P, P))
    same = lambda n: (i[:, None] // n) == (i[None, :] // n)
    c["blk64"] = same(64)
    c["hg_mask"] = same(32) & (i[:, None] <= i[None, :])
    c["fwd64"] = same(64) & (i[:, None] <= i[None, :])
    c["bwd64"] = same(64) & (i[:, None] >= i[None, :])
    dist = 384 + i[:, None] - np.arange(512)[None, :]
    mult = ((dist >= 0) & (dist <= 128)) * 1.0 + ((dist >= 0) & (dist % 4 == 0)) + ((dist >= 0) & (dist % 16 == 0))
    c["dist"] = np.where(mult > 0, dist, 1e32)
    c["mult"] = mult
    c["reset32"] = np.broadcast_to(np.arange(512) % 32 != 0, (P, 512))
    c["reset64"] = np.broadcast_to(np.arange(768) % 64 != 0, (P, 768))
    t = np.arange(S)
    inv = 10000.0 ** (-np.arange(0, 16, 2, dtype=np.float32) / np.float32(16))
    row, col = (t // 64).astype(np.float32), (t % 64).astype(np.float32)
    ang = np.stack([row[None, :] * inv[:, None].astype(np.float32), col[None, :] * inv[:, None].astype(np.float32)])
    cos, sin = np.ones((P, TT)), np.zeros((P, TT))
    rot = np.zeros((P, 32))
    for axis in range(2):
        for half in range(2):
            for f in range(8):
                r = 16 * axis + 8 * half + f
                cos[64 + r, :S] = np.cos(ang[axis, f])
                sin[64 + r, :S] = np.sin(ang[axis, f])
                rot[64 + (r + 8 if half == 0 else r - 8), r] = -1.0 if half == 0 else 1.0
    c["cos"], c["sin"], c["rot"] = cos, sin, rot
    lv = []
    for b in (1, 2, 4, 8, 16, 32):
        pair = ((i[:, None] // (2 * b)) == (i[None, :] // (2 * b))) & ((i[:, None] // b) != (i[None, :] // b))
        lv += [pair & (i[:, None] < i[None, :]), pair & (i[:, None] > i[None, :])]
    c["levels"] = np.concatenate(lv, axis=1)
    c["iota"] = np.broadcast_to(np.arange(32) % 8, (P, 32))
    c["iota64"] = np.broadcast_to(np.arange(64), (P, 64))
    c["before"] = i[:, None] < i[None, :]
    return np.concatenate([np.asarray(c[n], np.float32) for n, _ in CST], axis=1).astype(np.float32)


def setup(nc, ctx, d):
    E = Parts()
    E.nc, E.d = nc, d
    E.ps = ctx.enter_context(nc.psum_tensor("ps", [P, 8 * BANK], FP))
    E.bank = lambda b, w=BANK, p=P: E.ps[0:p, b * BANK:b * BANK + w]
    E.hT = ctx.enter_context(nc.sbuf_tensor("hT", [P, KT, TT], FP))
    E.aT = ctx.enter_context(nc.sbuf_tensor("aT", [P, KT, TT], FP))
    E.vcol = ctx.enter_context(nc.sbuf_tensor("vcol", [P, 256], FP))
    E.base = ctx.enter_context(nc.sbuf_tensor("base", [P, 3 * P], FP))
    E.ident, E.ones, E.blk64 = (E.base[:, i * P:(i + 1) * P] for i in range(3))
    E.mod = ctx.enter_context(nc.sbuf_tensor("mod", [P, 2, 6 * KT, 2], FP))
    E.nw = ctx.enter_context(nc.sbuf_tensor("norm_weights", [P, 2, 2, KT, 2], FP))
    E.v = lambda name, i: E.vcol[:, VEC_AT[name] + i:VEC_AT[name] + i + 1]

    def sem(name):
        return nc.alloc_semaphore(name=name)
    E.sem = sem
    E.cst = lambda name: d["cst"][:, CST_AT[name][0]:CST_AT[name][0] + CST_AT[name][1]]
    loaded, turned, copied = sem("vec_loaded"), sem("vec_turned"), sem("vec_copied")
    rows = (P, N_VEC - P)
    with nc.sbuf_tensor("vec_rows", [P, 2, P], FP) as vrow, nc.Block() as block:
        @block.sync
        def _(sp):
            sp.dma_start(E.base[:], d["cst"][:, 0:3 * P]).then_inc(loaded, 16)
            for i in range(2):
                sp.dma_start(vrow[0:rows[i], i, :], d["vec"][i * P:i * P + rows[i], :]).then_inc(loaded, 16)

        @block.tensor
        def _(pe):
            pe.wait_ge(loaded, 48)
            for i in range(2):
                last = pe.transpose(E.bank(0, P)[:, 0:rows[i]] if i == 0 else E.bank(1, P)[:, 0:rows[i]],
                                    vrow[0:rows[i], i, :], E.ident[0:rows[i], 0:rows[i]])
            last.then_inc(turned, 1)

        @block.vector
        def _(dve):
            dve.wait_ge(turned, 1)
            for i in range(2):
                dve.tensor_copy(E.vcol[:, i * P:i * P + rows[i]], E.bank(i, rows[i])).then_inc(copied, 1)
    return E


def gemm(E, name, jobs, slots=2, banks=8):
    nc, sem = E.nc, E.sem
    loaded = [sem(f"{name}_w_loaded{i}") for i in range(slots)]
    full = sem(f"{name}_bank_full")
    ends, at = [], 0
    for job in jobs:
        at += len(job["units"])
        ends.append(at)
    freed = {"act": sem(f"{name}_act_freed"), "dve": sem(f"{name}_dve_freed")}
    units = [(j, u) for j, job in enumerate(jobs) for u in job["units"]]
    count, freed_at = {"act": 0, "dve": 0}, []
    for _, (_, who, _) in units:
        count[who] += 1
        freed_at.append((who, count[who]))
    width = max(job["w"].shape[1] * job["w"].shape[2] for job in jobs)
    with nc.sbuf_tensor(f"{name}_ring", [P, slots, width], FP) as ring, nc.Block() as block:
        def tile(j):
            kt, cols = jobs[j]["w"].shape[1:]
            return ring[:, j % slots, 0:kt * cols].rearrange("p (k n) -> p k n", k=kt)

        @block.sync
        def _(sp):
            for j, job in enumerate(jobs):
                if j >= slots:
                    sp.wait_ge(full, ends[j - slots])
                sp.dma_start(tile(j), job["w"]).then_inc(loaded[j % slots], 16)

        @block.tensor
        def _(pe):
            before = -1
            for u, (j, (mms, _, _)) in enumerate(units):
                if j != before:
                    pe.wait_ge(loaded[j % slots], 16 * (j // slots + 1))
                before = j
                if u >= banks:
                    who, n = freed_at[u - banks]
                    pe.wait_ge(freed[who], n)
                steps = mms(tile(j), u % banks)
                for i, (out, lhsT, rhs) in enumerate(steps):
                    last = pe.matmul(out, lhsT, rhs, start=(i == 0), stop=(i == len(steps) - 1))
                last.then_inc(full, 1)

        def evacuate(eng, me):
            for u, (j, (_, who, ev)) in enumerate(units):
                if who == me:
                    eng.wait_ge(full, u + 1)
                    ev(eng, u % banks).then_inc(freed[me], 1)

        @block.scalar
        def _(act):
            evacuate(act, "act")

        @block.vector
        def _(dve):
            evacuate(dve, "dve")


def kn(w):
    return w.rearrange("(k p) n -> p k n", p=P)


def feature_unit(E, x, n0, m, t0, t1, who, ev, kt=KT):
    def mms(w, b):
        return [(E.bank(b, t1 - t0, m), w[:, k, n0:n0 + m], x[:, k, t0:t1]) for k in range(kt)]
    return (mms, who, lambda eng, b: ev(eng, E.bank(b, t1 - t0, m)))


def token_unit(E, x, t0, n, who, ev, kt=KT, pick=None):
    def mms(w, b):
        return [(E.bank(b, n), x[:, k, t0:t0 + P], pick(w, k) if pick else w[:, k, 0:n]) for k in range(kt)]
    return (mms, who, lambda eng, b: ev(eng, E.bank(b, n)))


def act_copy(dst, func=ACT.Copy, scale=1.0):
    return lambda eng, ps: eng.activation(dst, ps, func, scale=scale)


def dve_copy(dst):
    return lambda eng, ps: eng.tensor_copy(dst, ps)


def norm(E, name, src, dst, kt, width, T, scale, shift=None, segs=None):
    nc, sem = E.nc, E.sem
    segs = segs or [(0, T)]
    parts = [(0, min(T, BANK))] + ([(BANK, T)] if T > BANK else [])
    squared, summed, rooted, scaled = (sem(f"{name}_{x}") for x in ("squared", "summed", "rooted", "scaled"))
    with nc.sbuf_tensor(f"{name}_sq", [P, 2, T], FP) as sq, nc.sbuf_tensor(f"{name}_rstd", [P, T], FP) as rstd, \
            nc.Block() as block:
        @block.scalar
        def _(act):
            for k in range(kt):
                if k >= 2:
                    act.wait_ge(summed, k - 1)
                act.activation(sq[:, k % 2, :], src[:, k, 0:T], ACT.Square).then_inc(squared, 1)
            act.wait_ge(summed, kt)
            act.activation(rstd[:], E.ps[:, 0:T], ACT.Ln, scale=1.0 / width, bias=EPS).then_inc(rooted, 1)
            act.wait_ge(rooted, 1)
            act.activation(rstd[:], rstd[:], ACT.Exp, scale=-0.5).then_inc(rooted, 1)
            if shift:
                for k in range(kt):
                    act.wait_ge(scaled, (k + 1) * len(segs))
                    for s, (a, b) in enumerate(segs):
                        act.activation(dst[:, k, a:b], dst[:, k, a:b], ACT.Identity, bias=shift(k, s))

        @block.tensor
        def _(pe):
            for k in range(kt):
                pe.wait_ge(squared, k + 1)
                for a, b in parts:
                    last = pe.matmul(E.ps[:, a:b], E.ones, sq[:, k % 2, a:b], start=(k == 0), stop=(k == kt - 1))
                last.then_inc(summed, 1)

        @block.vector
        def _(dve):
            dve.wait_ge(rooted, 2)
            for k in range(kt):
                for s, (a, b) in enumerate(segs):
                    dve.scalar_tensor_tensor(out=dst[:, k, a:b], in0=src[:, k, a:b], scalar=scale(k, s),
                                             in1=rstd[:, a:b], op0=ALU.mult, op1=ALU.mult).then_inc(scaled, 1)


def gated_norm(E, name, o, dst, tiles, T, width, summer, scale, gate, gate_T=None):
    nc, sem = E.nc, E.sem
    squared, summed, rooted, scaled = (sem(f"{name}_{x}") for x in ("squared", "summed", "rooted", "scaled"))
    per = -(-T // BANK)
    parts = [(0, min(T, BANK))] + ([(BANK, T)] if T > BANK else [])
    with nc.sbuf_tensor(f"{name}_sq", [P, 2, T], FP) as sq, nc.sbuf_tensor(f"{name}_rstd", [P, tiles, T], FP) as rstd, \
            nc.Block() as block:
        @block.scalar
        def _(act):
            for k in range(tiles):
                if k >= 2:
                    act.wait_ge(summed, k - 1)
                act.activation(sq[:, k % 2, :], o[:, k, 0:T], ACT.Square).then_inc(squared, 1)
            act.wait_ge(summed, tiles)
            for k in range(tiles):
                act.activation(rstd[:, k, :], E.ps[:, k * per * BANK:k * per * BANK + T], ACT.Ln,
                               scale=1.0 / width, bias=EPS).then_inc(rooted, 1)
            act.wait_ge(rooted, tiles)
            for k in range(tiles):
                act.activation(rstd[:, k, :], rstd[:, k, :], ACT.Exp, scale=-0.5).then_inc(rooted, 1)

        @block.tensor
        def _(pe):
            for k in range(tiles):
                pe.wait_ge(squared, k + 1)
                for a, b in parts:
                    last = pe.matmul(E.ps[:, k * per * BANK + a:k * per * BANK + b], summer, sq[:, k % 2, a:b],
                                     start=True, stop=True)
                last.then_inc(summed, 1)

        @block.vector
        def _(dve):
            for k in range(tiles):
                dve.wait_ge(rooted, tiles + k + 1)
                dve.scalar_tensor_tensor(out=dst[:, k, 0:T], in0=o[:, k, 0:T], scalar=scale(k), in1=rstd[:, k, :],
                                         op0=ALU.mult, op1=ALU.mult).then_inc(scaled, 1)

        @block.gpsimd
        def _(pool):
            for k in range(tiles):
                pool.wait_ge(scaled, k + 1)
                pool.tensor_tensor(dst[:, k, 0:T], dst[:, k, 0:T], gate[:, k, 0:T], ALU.mult)


def turn(E, name, jobs):
    turned, act_out, dve_out = (E.sem(f"{name}_{x}") for x in ("turned", "act_out", "dve_out"))
    with E.nc.Block() as block:
        @block.tensor
        def _(pe):
            for u, (srcs, _) in enumerate(jobs):
                if u >= 8:
                    pe.wait_ge(act_out if u % 2 == 0 else dve_out, (u - 8) // 2 + 1)
                for i, s in enumerate(srcs):
                    last = pe.transpose(E.bank(u % 8)[:, i * P:(i + 1) * P], s, E.ident)
                last.then_inc(turned, 1)

        @block.scalar
        def _(act):
            for u, (srcs, dst) in enumerate(jobs):
                if u % 2 == 0:
                    act.wait_ge(turned, u + 1)
                    act.activation(dst, E.bank(u % 8, len(srcs) * P), ACT.Copy).then_inc(act_out, 1)

        @block.vector
        def _(dve):
            for u, (srcs, dst) in enumerate(jobs):
                if u % 2 == 1:
                    dve.wait_ge(turned, u + 1)
                    dve.tensor_copy(dst, E.bank(u % 8, len(srcs) * P)).then_inc(dve_out, 1)


def load(E, name, pairs, eng="sync"):
    done = E.sem(f"{name}_loaded")
    with E.nc.Block() as block:
        @block.sync
        def _(sp):
            for dst, src in pairs:
                sp.dma_start(dst, src).then_inc(done, 16)
            sp.wait_ge(done, 16 * len(pairs))


def attention_and_hgrn(E):
    nc, d, sem = E.nc, E.d, E.sem
    hT, aT = E.hT, E.aT
    with nc.sbuf_tensor("x_rows", [P, 4, D], FP) as xr:
        load(E, "x", [(xr[:], d["x"][0].rearrange("(t p) n -> p t n", p=P))])
        turn(E, "xturn", [([xr[:, t, k * P:(k + 1) * P] for t in range(4)], hT[:, k, 0:S]) for k in range(KT)])
    norm(E, "n1", hT, aT, KT, D, S, lambda k, s: E.v("norm1_g", k))

    with ExitStack() as c:
        sb = lambda n, s: c.enter_context(nc.sbuf_tensor(n, s, FP))
        qT, kT, V = sb("a_qT", [P, 4, S]), sb("a_kT", [P, 4, S]), sb("a_V", [P, 4, S])
        hq, hf, hi, hg = sb("h_q", [P, 4, S]), sb("h_f", [P, 4, S]), sb("h_i", [P, 4, S]), sb("h_gate", [P, 4, S])
        w = d["w_in"][0]

        def group(g, kind, dst, ev):
            units = []
            for n in range(4):
                who = "act" if ev else ("act" if n % 2 else "dve")
                e = ev(dst[:, n, :]) if ev else (act_copy(dst[:, n, :]) if n % 2 else dve_copy(dst[:, n, :]))
                units.append(feature_unit(E, aT, n * P, P, 0, S, who, e) if kind == "f"
                             else token_unit(E, aT, n * P, S, who, e))
            return dict(w=kn(w[:, g * S:(g + 1) * S]), units=units)
        silu = lambda dst: act_copy(dst, ACT.Silu)
        gemm(E, "proj1", [group(0, "f", qT, lambda dst: act_copy(dst, scale=0.125)), group(1, "f", kT, None),
                          group(2, "t", V, None), group(3, "f", hq, silu), group(4, "f", hf, None),
                          group(5, "t", hi, None), group(6, "f", hg, silu)])
        dilated(E, qT, kT, V)
        hgrn(E, hq, hf, hi, hg)
    resid_gemm(E, "wout1", d["w_out"][0], aT, S, None)


def resid_gemm(E, name, w, x, T, gate):
    segs = [(0, S)] + ([(S, T)] if T > S else [])

    def ev(n, s, a, b):
        def run(dve, ps):
            if gate is None:
                return dve.tensor_tensor(E.hT[:, n, a:b], E.hT[:, n, a:b], ps, ALU.add)
            return dve.scalar_tensor_tensor(out=E.hT[:, n, a:b], in0=ps, scalar=gate(n, s), in1=E.hT[:, n, a:b],
                                            op0=ALU.mult, op1=ALU.add)
        return run
    gemm(E, name, [dict(w=kn(w[:, g * 512:(g + 1) * 512]),
                        units=[feature_unit(E, x, n * P, P, a, b, "dve", ev(4 * g + n, s, a, b))
                               for n in range(4) for s, (a, b) in enumerate(segs)]) for g in range(2)])


def dilated(E, qT, kT, V):
    nc = E.nc
    with ExitStack() as c:
        sb = lambda nm, s: c.enter_context(nc.sbuf_tensor(nm, s, FP))
        O = sb("dil_o", [P, 4, 512])
        dilated_units(E, qT, kT, V, O)
        oT = sb("dil_oT", [P, 4, 512])
        turn(E, "dil_oturn", [([O[:, i, k * P:(k + 1) * P] for i in range(4)], oT[:, k, :]) for k in range(4)])
        norm(E, "dil_norm", oT, E.aT, 4, 512, S, lambda k, s: E.v("attn_norm_g", k))


def dilated_units(E, qT, kT, V, O):
    nc, d, sem = E.nc, E.d, E.sem
    units = [(h, i) for h in range(HEADS) for i in range(4)]
    n = len(units)
    cst_in, scored, biased, maxed, exped, weighted, turned, evac, summed, done = (
        sem(f"dil_{x}") for x in ("cst", "scored", "biased", "maxed", "exped", "weighted", "turned", "evac",
                                  "summed", "done"))
    with ExitStack() as c:
        sb = lambda nm, s: c.enter_context(nc.sbuf_tensor(nm, s, FP))
        dist, mult = sb("dist", [P, 512]), sb("mult", [P, 512])
        sc, pr, pm, pT = (sb(x, [P, 2, 512]) for x in ("dil_sc", "dil_pr", "dil_pm", "dil_pT"))
        neg, tot, inv = (sb(x, [P, n]) for x in ("dil_neg", "dil_tot", "dil_inv"))
        block = c.enter_context(nc.Block())

        @block.sync
        def _(sp):
            sp.dma_start(dist[:], E.cst("dist")).then_inc(cst_in, 16)
            sp.dma_start(mult[:], E.cst("mult")).then_inc(cst_in, 16)

        @block.tensor
        def _(pe):
            for t in range(n + 2):
                if t < n:
                    h, i = units[t]
                    if t >= 2:
                        pe.wait_ge(biased, t - 1)
                    lo = 64 * (h % 2)
                    pe.matmul(E.bank(t % 2, (i + 1) * P), qT[lo:lo + 64, h // 2, i * P:(i + 1) * P],
                              kT[lo:lo + 64, h // 2, 0:(i + 1) * P], start=True, stop=True).then_inc(scored, 1)
                if 1 <= t <= n:
                    u = t - 1
                    h, i = units[u]
                    pe.wait_ge(weighted, u + 1)
                    if u >= 2:
                        pe.wait_ge(evac, u - 1)
                    for j in range(i + 1):
                        last = pe.transpose(E.bank(2 + u % 2)[:, j * P:(j + 1) * P], pm[:, u % 2, j * P:(j + 1) * P],
                                            E.ident)
                    last.then_inc(turned, 1)
                if t >= 2:
                    u = t - 2
                    h, i = units[u]
                    pe.wait_ge(evac, u + 1)
                    if u >= 2:
                        pe.wait_ge(done, u - 1)
                    for j in range(i + 1):
                        last = pe.matmul(E.bank(4 + u % 2, 64), pT[:, u % 2, j * P:(j + 1) * P],
                                         V[:, j, h * 64:(h + 1) * 64], start=(j == 0), stop=(j == i))
                    last.then_inc(summed, 1)

        @block.scalar
        def _(act):
            for t in range(n + 1):
                if t < n:
                    L = (units[t][1] + 1) * P
                    act.wait_ge(maxed, t + 1)
                    if t >= 2:
                        act.wait_ge(weighted, t - 1)
                    act.activation(pr[:, t % 2, 0:L], sc[:, t % 2, 0:L], ACT.Exp, bias=neg[:, t:t + 1]).then_inc(exped, 1)
                if t >= 1:
                    u = t - 1
                    L = (units[u][1] + 1) * P
                    act.wait_ge(turned, u + 1)
                    if u >= 2:
                        act.wait_ge(summed, u - 1)
                    act.activation(pT[:, u % 2, 0:L], E.bank(2 + u % 2, L), ACT.Copy).then_inc(evac, 1)

        @block.vector
        def _(dve):
            dve.wait_ge(cst_in, 32)
            for t in range(n + 3):
                if t < n:
                    h, i = units[t]
                    L, off = (i + 1) * P, (3 - i) * P
                    dve.wait_ge(scored, t + 1)
                    if t >= 2:
                        dve.wait_ge(exped, t - 1)
                    dve.scalar_tensor_tensor(out=sc[:, t % 2, 0:L], in0=dist[:, off:512], scalar=-2.0 ** -(h + 1),
                                             in1=E.bank(t % 2, L), op0=ALU.mult, op1=ALU.add).then_inc(biased, 1)
                    dve.wait_ge(biased, t + 1)
                    dve.tensor_reduce(neg[:, t:t + 1], sc[:, t % 2, 0:L], AX.X, ALU.max, negate=True).then_inc(maxed, 1)
                if 1 <= t <= n:
                    u = t - 1
                    h, i = units[u]
                    L, off = (i + 1) * P, (3 - i) * P
                    dve.wait_ge(exped, u + 1)
                    if u >= 2:
                        dve.wait_ge(turned, u - 1)
                    dve.tensor_tensor_reduce(pm[:, u % 2, 0:L], pr[:, u % 2, 0:L], mult[:, off:512], 1.0, 0.0,
                                             ALU.mult, ALU.add, tot[:, u:u + 1]).then_inc(weighted, 1)
                    dve.wait_ge(weighted, u + 1)
                    dve.reciprocal(inv[:, u:u + 1], tot[:, u:u + 1])
                if t >= 3:
                    u = t - 3
                    h, i = units[u]
                    dve.wait_ge(summed, u + 1)
                    dve.tensor_scalar(O[:, i, h * 64:(h + 1) * 64], E.bank(4 + u % 2, 64), inv[:, u:u + 1], None,
                                      ALU.mult).then_inc(done, 1)


def hgrn(E, hq, hf, hi, gate):
    nc, d, sem = E.nc, E.d, E.sem
    C, NC = 32, S // 32
    pt = [P, 4, S]
    with ExitStack() as c:
        sb = lambda nm, s: c.enter_context(nc.sbuf_tensor(nm, s, FP))
        reset, mask, lb, omlb, dec = sb("hg_reset", [P, S]), sb("hg_mask", [P, P]), sb("hg_lb", [P, 4]), \
            sb("hg_omlb", [P, 4]), sb("hg_dec", [P, 4, NC])
        key, b, e1, k_in, k_end = sb("hg_key", pt), sb("hg_b", pt), sb("hg_e", pt), sb("hg_k_in", pt), sb("hg_k_end", pt)
        cst_in, a, v = sem("hg_cst"), sem("hg_act"), sem("hg_dve")
        with nc.Block() as block:
            @block.sync
            def _(sp):
                sp.dma_start(reset[:], E.cst("reset32")).then_inc(cst_in, 16)
                sp.dma_start(mask[:], E.cst("hg_mask")).then_inc(cst_in, 16)

            @block.scalar
            def _(act):
                act.activation(e1[:], hf[:], ACT.Exp, scale=-1.0).then_inc(a, 1)
                act.activation(key[:], hf[:], ACT.Exp).then_inc(a, 1)
                act.wait_ge(v, 1)
                act.activation(lb[:], lb[:], ACT.Exp).then_inc(a, 1)
                act.wait_ge(v, 8)
                act.activation(e1[:], e1[:], ACT.Ln).then_inc(a, 1)
                act.wait_ge(v, 15)
                act.activation(k_in[:], b[:], ACT.Exp, scale=-1.0).then_inc(a, 1)
                act.activation(b[:], b[:], ACT.Exp).then_inc(a, 1)
                act.activation(k_end[:], k_end[:], ACT.Exp).then_inc(a, 1)
                act.activation(dec[:], dec[:], ACT.Exp).then_inc(a, 1)

            @block.vector
            def _(dve):
                g = VEC_AT["hgrn_gamma"]
                dve.tensor_tensor(lb[:], E.vcol[:, g + 4:g + 8], E.vcol[:, g:g + 4], ALU.subtract).then_inc(v, 1)
                dve.wait_ge(a, 3)
                dve.tensor_scalar(lb[:], lb[:], 1.0, None, ALU.add).then_inc(v, 1)
                dve.tensor_scalar(e1[:], e1[:], 1.0, None, ALU.add).then_inc(v, 1)
                dve.wait_ge(v, 2)
                dve.reciprocal(lb[:], lb[:]).then_inc(v, 1)
                dve.wait_ge(v, 4)
                dve.tensor_scalar(omlb[:], lb[:], -1.0, 1.0, ALU.mult, ALU.add).then_inc(v, 1)
                dve.reciprocal(e1[:], e1[:]).then_inc(v, 1)
                dve.tensor_scalar(key[:], key[:], 1.0, None, ALU.add).then_inc(v, 1)
                dve.wait_ge(v, 7)
                for j in range(4):
                    ins = dve.tensor_scalar(e1[:, j, :], e1[:, j, :], omlb[:, j:j + 1], lb[:, j:j + 1], ALU.mult, ALU.add)
                ins.then_inc(v, 1)
                dve.reciprocal(key[:], key[:]).then_inc(v, 1)
                dve.wait_ge(v, 9)
                for j in range(4):
                    ins = dve.tensor_scalar(key[:, j, :], key[:, j, :], omlb[:, j:j + 1], None, ALU.mult)
                ins.then_inc(v, 1)
                dve.wait_ge(cst_in, 32)
                dve.wait_ge(a, 4)
                for j in range(4):
                    dve.tensor_tensor_scan(b[:, j, :], reset[:], e1[:, j, :], 0.0, ALU.mult, ALU.add).then_inc(v, 1)
                dve.wait_ge(v, 14)
                bc = b[:].rearrange("p j (c t) -> p (j c) t", t=C)
                dve.tensor_copy(dec[:].rearrange("p j c -> p (j c)"), bc[:, :, C - 1])
                dve.tensor_tensor(k_end[:].rearrange("p j (c t) -> p (j c) t", t=C),
                                  bc[:, :, C - 1:C].to_broadcast([P, 4 * NC, C]), bc, ALU.subtract).then_inc(v, 1)
                dve.wait_ge(a, 7)
                dve.tensor_tensor(k_in[:], k_in[:], key[:], ALU.mult)
                dve.tensor_tensor(k_end[:], k_end[:], key[:], ALU.mult)
                dve.tensor_tensor(hq[:], hq[:], b[:], ALU.mult)
        kt = key
        turn(E, "hg_kturn", [([k_end[:, j, i * P:(i + 1) * P] for j in range(4)],
                              kt[:, i, :]) for i in range(4)])
        Sall = sb("hg_states", [P, 4, 64, NC])
        dS, decx = sb("hg_dS", [P, 64, NC]), sb("hg_decx", [P, 64, NC])
        gains, out, decd, scanned = (sem(f"hg_{x}") for x in ("gains", "gains_out", "decay_spread", "scanned"))
        with nc.Block() as block:
            @block.tensor
            def _(pe):
                for j in range(4):
                    if j >= 2:
                        pe.wait_ge(out, j - 1)
                    for ch in range(NC):
                        t, r = ch // 4, ch % 4
                        for h2 in range(2):
                            col, at = (2 * j + h2) * 64, (4 * (j % 2) + r) * BANK + 64 * t
                            last = pe.matmul(E.ps[64 * h2:64 * h2 + 64, at:at + 64], kt[32 * r:32 * r + 32, t, col:col + 64],
                                             hi[32 * r:32 * r + 32, t, col:col + 64], start=True, stop=True)
                    last.then_inc(gains, 1)

            @block.scalar
            def _(act):
                for j in range(4):
                    if j >= 1:
                        act.wait_ge(scanned, j)
                    act.wait_ge(gains, j + 1)
                    for r in range(4):
                        last = act.activation(dS[:].rearrange("p v (t r) -> p r t v", r=4)[:, r],
                                              E.bank(4 * (j % 2) + r, 256).rearrange("p (t v) -> p t v", v=64), ACT.Copy)
                    last.then_inc(out, 1)

            @block.vector
            def _(dve):
                for j in range(4):
                    dve.tensor_copy(decx[:], dec[:, j:j + 1, :].to_broadcast([P, 64, NC])).then_inc(decd, 1)
                    dve.wait_ge(decd, 2 * j + 1)
                    dve.memset(decx[:, :, 0:1], 0.0).then_inc(decd, 1)
                    dve.wait_ge(decd, 2 * j + 2)
                    dve.wait_ge(out, j + 1)
                    dve.tensor_tensor_scan(Sall[:, j].rearrange("p v c -> p (v c)"), decx[:].rearrange("p v c -> p (v c)"),
                                           dS[:].rearrange("p v c -> p (v c)"), 0.0, ALU.mult, ALU.add).then_inc(scanned, 1)
                    dve.wait_ge(scanned, j + 1)
        AT = sb("hg_AT", [P, 2, 2, P])
        oT = k_end
        scored, masked, summed, taken = (sem(f"hg_{x}") for x in ("scored", "masked", "summed", "taken"))
        with nc.Block() as block:
            units = [(j, t) for j in range(4) for t in range(4)]

            @block.tensor
            def _(pe):
                for n in range(17):
                    if n < 16:
                        j, t = units[n]
                        if n >= 2:
                            pe.wait_ge(masked, n - 1)
                        for h2 in range(2):
                            lo = 64 * h2
                            last = pe.matmul(E.bank(2 * (n % 2) + h2, P), k_in[lo:lo + 64, j, t * P:(t + 1) * P],
                                             hq[lo:lo + 64, j, t * P:(t + 1) * P], start=True, stop=True)
                        last.then_inc(scored, 1)
                    if n >= 1:
                        j, t = units[n - 1]
                        pe.wait_ge(masked, n)
                        if n >= 3:
                            pe.wait_ge(taken, n - 2)
                        for h2 in range(2):
                            lo, col = 64 * h2, (2 * j + h2) * 64
                            o = E.ps[lo:lo + 64, (4 + (n - 1) % 2) * BANK:(4 + (n - 1) % 2) * BANK + P]
                            pe.matmul(o, hi[:, t, col:col + 64], AT[:, (n - 1) % 2, h2, :], start=True, stop=False,
                                      skip_group_check=True)
                            for ci in range(4):
                                ch = 4 * t + ci
                                if ch:
                                    last = pe.matmul(o[:, 32 * ci:32 * ci + 32], Sall[lo:lo + 64, j, :, ch - 1],
                                                     hq[lo:lo + 64, j, 32 * ch:32 * ch + 32], start=False, stop=(ci == 3),
                                                     skip_group_check=True)
                        last.then_inc(summed, 1)

            @block.vector
            def _(dve):
                for n in range(16):
                    dve.wait_ge(scored, n + 1)
                    if n >= 2:
                        dve.wait_ge(summed, n - 1)
                    for h2 in range(2):
                        last = dve.tensor_tensor(AT[:, n % 2, h2, :], mask[:], E.bank(2 * (n % 2) + h2, P), ALU.mult)
                    last.then_inc(masked, 1)

            @block.scalar
            def _(act):
                for n in range(16):
                    j, t = units[n]
                    act.wait_ge(summed, n + 1)
                    act.activation(oT[:, j, t * P:(t + 1) * P], E.bank(4 + n % 2, P), ACT.Copy).then_inc(taken, 1)
        gated_norm(E, "hg_norm", oT, E.aT[:, 4:8, :], 4, S, 64, E.blk64, lambda k: E.v("hgrn_norm_g", k), gate)


N_EXP, N_GRP, D_EXP = 32, 4, 512


SLOTS = 64
PAIRS = N_EXP // 2


def route(E, R):
    nc, d, sem = E.nc, E.d, E.sem
    with ExitStack() as c:
        sb = lambda n, s, dt=FP: c.enter_context(nc.sbuf_tensor(n, s, dt))
        wr, brow = sb("r_w", [P, KT, 36]), sb("r_bias", [1, 36])
        L, grp, m8, g8, iota = sb("r_L", [P, 4, 36]), sb("r_grp", [P, 4, 8]), sb("r_m8", [P, 4, 8]), sb("r_g8", [P, 4, 8]), \
            sb("r_iota", [P, 8])
        idx, idf = sb("r_idx", [P, 4, 8], mybir.dt.uint32), sb("r_idf", [P, 4, 8])
        m8b, idxb, idfb = sb("r_m8b", [P, 4, 8]), sb("r_idxb", [P, 4, 8], mybir.dt.uint32), sb("r_idfb", [P, 4, 8])
        ex, ohg, sel, tmp = sb("r_ex", [P, 4, 4]), sb("r_ohg", [P, 4, 4]), sb("r_sel", [P, 4, 8]), sb("r_tmp", [P, 4, 8])
        s1, s2, s3, s4 = (sb(f"r_s{i}", [P, 4, 1]) for i in range(4))
        Gt, mem, before = R.gate, sb("r_mem", [P, 4, 32]), sb("r_before", [P, P])
        mem8, fullest, need = sb("r_mem8", [P, 4, 8]), sb("r_fullest", [P, 1]), sb("r_need", [P, 8])
        loaded, logits, v, a, ranked = (sem(f"route_{x}") for x in ("loaded", "logits", "dve", "act", "ranked"))
        with nc.Block() as block:
            @block.sync
            def _(sp):
                sp.dma_start(wr[:, :, 0:4], kn(d["w_group"][0])).then_inc(loaded, 16)
                sp.dma_start(wr[:, :, 4:36], kn(d["w_router"][0])).then_inc(loaded, 16)
                sp.dma_start(brow[:, 0:4], d["b_group"]).then_inc(loaded, 16)
                sp.dma_start(brow[:, 4:36], d["b_router"]).then_inc(loaded, 16)
                sp.dma_start(iota[:], E.cst("iota")[:, 0:8]).then_inc(loaded, 16)
                sp.dma_start(before[:], E.cst("before")).then_inc(loaded, 16)
                sp.dma_start(R.slot[:], E.cst("iota64")).then_inc(loaded, 16)

            @block.tensor
            def _(pe):
                pe.wait_ge(loaded, 112)
                for t in range(4):
                    pe.matmul(E.bank(t, 36), E.ones[0:1, :], brow[0:1, :], start=True, stop=False)
                    for k in range(KT):
                        last = pe.matmul(E.bank(t, 36), E.aT[:, k, t * P:(t + 1) * P], wr[:, k, :], start=False,
                                         stop=(k == KT - 1))
                    last.then_inc(logits, 1)
                pe.wait_ge(v, 99)
                for t in range(4):
                    for i in range(t):
                        pe.matmul(E.bank(4, P)[:, 32 * t:32 * t + 32], E.ones, mem[:, i, :], start=(i == 0), stop=False)
                    pe.matmul(E.bank(4, P)[:, 32 * t:32 * t + 32], before[:], mem[:, t, :], start=(t == 0), stop=True)
                for t in range(4):
                    last = pe.matmul(E.bank(5, 32), E.ones, mem[:, t, :], start=(t == 0), stop=(t == 3))
                last.then_inc(ranked, 1)

            @block.scalar
            def _(act):
                act.wait_ge(v, 11)
                act.activation(ex[:], ex[:], ACT.Exp).then_inc(a, 1)
                act.wait_ge(v, 25)
                act.activation(s2[:], s2[:], ACT.Exp).then_inc(a, 1)

            @block.vector
            def _(dve):
                n = [0]

                def done(ins, upto=None):
                    k = (upto or n[0] + 1) - n[0]
                    ins.then_inc(v, k)
                    n[0] += k
                    dve.wait_ge(v, n[0])
                dve.wait_ge(logits, 4)
                dve.wait_ge(loaded, 112)
                done(dve.memset(grp[:], -3e38))
                done(dve.tensor_copy(L[:], E.ps[:].rearrange("p (b n) -> p b n", n=BANK)[:, 0:4, 0:36]))
                done(dve.tensor_copy(grp[:, :, 0:4], L[:, :, 0:4]))
                for t in range(4):
                    last = dve.max(m8[:, t, :], grp[:, t, :])
                done(last)
                for t in range(4):
                    last = dve.max_index(idx[:, t, :], m8[:, t, :], grp[:, t, :])
                done(last)
                done(dve.tensor_copy(idf[:], idx[:]))
                done(dve.tensor_tensor(ohg[:], iota[:, 0:4].unsqueeze(1).to_broadcast([P, 4, 4]),
                                       idf[:, :, 0:1].to_broadcast([P, 4, 4]), ALU.is_equal))
                done(dve.tensor_tensor(ex[:], L[:, :, 0:4], m8[:, :, 0:1].to_broadcast([P, 4, 4]), ALU.subtract), 11)
                done(dve.tensor_tensor(sel[:], L[:, :, 4:12], ohg[:, :, 0:1].to_broadcast([P, 4, 8]), ALU.mult))
                for g in range(1, 4):
                    done(dve.tensor_tensor(tmp[:], L[:, :, 4 + 8 * g:12 + 8 * g], ohg[:, :, g:g + 1].to_broadcast([P, 4, 8]),
                                           ALU.mult))
                    done(dve.tensor_tensor(sel[:], sel[:], tmp[:], ALU.add))
                for t in range(4):
                    last = dve.max(m8b[:, t, :], sel[:, t, :])
                done(last)
                for t in range(4):
                    last = dve.max_index(idxb[:, t, :], m8b[:, t, :], sel[:, t, :])
                done(last)
                done(dve.tensor_copy(idfb[:], idxb[:]))
                done(dve.tensor_tensor(s2[:], m8b[:, :, 1:2], m8b[:, :, 0:1], ALU.subtract), 25)
                dve.wait_ge(a, 2)
                done(dve.tensor_reduce(s1[:], ex[:], AX.X, ALU.add))
                done(dve.tensor_scalar(s3[:], s2[:], 1.0, None, ALU.add))
                done(dve.tensor_tensor(s1[:], s1[:], s3[:], ALU.mult))
                done(dve.reciprocal(s1[:], s1[:]))
                done(dve.tensor_tensor(s2[:], s2[:], s1[:], ALU.mult))
                iob = iota[:, 0:8].unsqueeze(1).to_broadcast([P, 4, 8])
                for which, g in ((0, s1), (1, s2)):
                    done(dve.tensor_tensor(tmp[:], iob, idfb[:, :, which:which + 1].to_broadcast([P, 4, 8]), ALU.is_equal))
                    if which == 0:
                        done(dve.tensor_copy(mem8[:], tmp[:]))
                        done(dve.tensor_tensor(g8[:], tmp[:], g[:].to_broadcast([P, 4, 8]), ALU.mult))
                    else:
                        done(dve.tensor_tensor(mem8[:], mem8[:], tmp[:], ALU.add))
                        done(dve.tensor_tensor(tmp[:], tmp[:], g[:].to_broadcast([P, 4, 8]), ALU.mult))
                done(dve.tensor_tensor(g8[:], g8[:], tmp[:], ALU.add))
                for g in range(4):
                    of_group = ohg[:, :, g:g + 1].to_broadcast([P, 4, 8])
                    dve.tensor_tensor(Gt[:, :, 8 * g:8 * g + 8], g8[:], of_group, ALU.mult)
                    last = dve.tensor_tensor(mem[:, :, 8 * g:8 * g + 8], mem8[:], of_group, ALU.mult)
                done(last, 99)
                dve.wait_ge(ranked, 1)
                done(dve.tensor_scalar(R.key[:].rearrange("p t e -> p (t e)"), E.bank(4, P), 1.0, None, ALU.add))
                done(dve.tensor_tensor(R.key[:], R.key[:], mem[:], ALU.mult))
                done(dve.tensor_scalar(R.key[:], R.key[:], -1.0, None, ALU.add))
                done(dve.tensor_reduce(fullest[:], E.bank(5, 32), AX.X, ALU.max))
                done(dve.tensor_scalar(need[:], iota[:], float(SLOTS), None, ALU.mult))
                done(dve.tensor_tensor(need[:], need[:], fullest[:].to_broadcast([P, 8]), ALU.is_lt))
                done(dve.tensor_reduce(fullest[:], need[:], AX.X, ALU.add))
                done(dve.tensor_copy(R.passes[:], fullest[:]))


def token_rows(E, R):
    turned, high, low = (E.sem(f"rows_{x}") for x in ("turned", "high", "low"))
    with E.nc.Block() as block:
        units = [(t, half) for t in range(4) for half in range(2)]

        @block.tensor
        def _(pe):
            for u, (t, half) in enumerate(units):
                for i in range(4):
                    last = pe.transpose(E.bank(u)[:, i * P:(i + 1) * P], E.aT[:, 4 * half + i, t * P:(t + 1) * P], E.ident)
                last.then_inc(turned, 1)

        @block.scalar
        def _(act):
            for u, (t, half) in enumerate(units):
                act.wait_ge(turned, u + 1)
                act.activation(R.xh[:, t, half * BANK:(half + 1) * BANK], E.bank(u), ACT.Copy).then_inc(high, 1)

        @block.vector
        def _(dve):
            for u, (t, half) in enumerate(units):
                dve.wait_ge(high, u + 1)
                cols = slice(half * BANK, (half + 1) * BANK)
                dve.tensor_tensor(R.xl[:, t, cols], E.bank(u), R.xh[:, t, cols].bitcast(FP), ALU.subtract).then_inc(low, 1)


def experts(E, R):
    nc, d, sem = E.nc, E.d, E.sem
    FT = D_EXP // P
    FR = mybir.dt.float32r
    with ExitStack() as c:
        sb = lambda n, s, dt=FP: c.enter_context(nc.sbuf_tensor(n, s, dt))
        sel, selg, back = sb("e_sel", [P, 4, P], FR), sb("e_selg", [P, 4, P]), sb("e_back", [P, S])
        xg, sg, hid = sb("e_xg", [P, KT, P]), sb("e_silu", [P, 2, FT * SLOTS]), sb("e_hid", [P, 2, FT * SLOTS])
        yT, y = sb("e_yT", [P, KT, P]), sb("e_y", [P, D])
        wg, wu, wd, in_gu, in_d = R.wg, R.wu, R.wd, R.in_gu, R.in_d
        (gathered, scattered, hidden_in, downs, sel_turned, y_turned, xg_act, xg_dve, silus, hids, y_out, y_act, y_dve,
         back_out, added, selected, weighted, keyed) = (sem(f"exp_{n}") for n in (
             "gathered", "scattered", "gate_up", "down", "sel_turned", "y_turned", "xg_act", "xg_dve", "silu", "hidden",
             "y_out", "y_act", "y_dve", "back_out", "added", "selected", "weighted", "keyed"))

        def fetch_gu(act, i, s):
            act.dma_start(wg[:, s], expert(d["w_gate"], 2 * i + s)).then_inc(in_gu[s], 16)
            act.dma_start(wu[:, s], expert(d["w_up"], 2 * i + s)).then_inc(in_gu[s], 16)

        def fetch_d(act, i, s):
            act.dma_start(wd[:, s], expert(d["w_down"], 2 * i + s)).then_inc(in_d[s], 16)

        with nc.Block() as block:
            @block.tensor
            def _(pe):
                n_pass = pe.value_load(R.passes[0:1, 0:1], min_val=1, max_val=S // SLOTS)
                with pe.Fori(0, n_pass) as p, pe.Fori(0, PAIRS) as i:
                    q = pe.snap(p * PAIRS + i)

                    def scatter(n):
                        pe.wait_ge(added, 8 * q + n + 1)
                        pe.matmul(E.bank(6 + n % 2), y[:, n * P:(n + 1) * P], back[:], start=True, stop=True)\
                          .then_inc(scattered, 1)
                    pe.wait_ge(y_act, q + 1)
                    pe.wait_ge(y_dve, q + 1)
                    pe.wait_ge(back_out, q + 1)
                    for n in range(6):
                        scatter(n)
                    pe.wait_ge(selected, q + 1)
                    pe.wait_ge(y_out, 2 * q + 1)
                    for k in range(KT):
                        for t in range(4):
                            for x in (R.xh, R.xl):
                                last = pe.matmul(E.bank(4 + k // 4)[:, (k % 4) * P:(k % 4 + 1) * P], x[:, t, k * P:(k + 1) * P],
                                                 sel[:, t, :], start=(t == 0 and x is R.xh), stop=(t == 3 and x is R.xl))
                    last.then_inc(gathered, 1)
                    scatter(6)
                    scatter(7)
                    pe.wait_ge(xg_act, q + 1)
                    pe.wait_ge(xg_dve, q + 1)
                    for s in range(2):
                        pe.wait_ge(in_gu[s], 32 * q + 32)
                        pe.wait_ge(hids, 2 * q + s + 1)
                        for j, w in enumerate((wg, wu)):
                            for f in range(FT):
                                at = (j * FT + f) * SLOTS
                                for k in range(KT):
                                    last = pe.matmul(E.bank(2 + s)[:, at:at + SLOTS], w[:, s, k, f * P:(f + 1) * P],
                                                     xg[:, k, s * SLOTS:(s + 1) * SLOTS], start=(k == 0), stop=(k == KT - 1))
                        last.then_inc(hidden_in, 1)
                    for s in range(2):
                        pe.wait_ge(in_d[s], 16 * q + 16)
                        pe.wait_ge(hids, 2 * q + s + 3)
                        for n in range(KT):
                            for f in range(FT):
                                last = pe.matmul(E.bank(4 + s)[:, n * SLOTS:(n + 1) * SLOTS], wd[:, s, f, n * P:(n + 1) * P],
                                                 hid[:, s, f * SLOTS:(f + 1) * SLOTS], start=(f == 0), stop=(f == FT - 1))
                        last.then_inc(downs, 1)
                    pe.wait_ge(weighted, q + 2)
                    for t in range(4):
                        last = pe.transpose(E.bank(2)[:, t * P:(t + 1) * P], selg[:, t, :], E.ident)
                    last.then_inc(sel_turned, 1)
                    pe.wait_ge(y_out, 2 * q + 3)
                    for n in range(KT):
                        last = pe.transpose(E.ps[:, n * P:(n + 1) * P], yT[:, n, :], E.ident)
                    last.then_inc(y_turned, 1)

            @block.scalar
            def _(act):
                n_pass = act.value_load(R.passes[0:1, 0:1], min_val=1, max_val=S // SLOTS)
                act.wait_ge(keyed, 1)
                act.sem_inc(y_act, 1)
                act.sem_inc(y_out, 1)

                def turn_(q, i):
                    act.wait_ge(gathered, q + 1)
                    act.activation(xg[:, 0:4, :], E.bank(4).rearrange("p (k n) -> p k n", k=4), ACT.Copy).then_inc(xg_act, 1)
                    for s in range(2):
                        act.wait_ge(hidden_in, 2 * q + s + 1)
                        act.activation(sg[:, s], E.bank(2 + s, FT * SLOTS), ACT.Silu).then_inc(silus, 1)
                        if i is not None:
                            fetch_gu(act, i + 1, s)
                    for s in range(2):
                        act.wait_ge(downs, 2 * q + s + 1)
                        act.activation(yT[:, :, s * SLOTS:(s + 1) * SLOTS],
                                       E.bank(4 + s).rearrange("p (k n) -> p k n", k=KT), ACT.Copy).then_inc(y_out, 1)
                        if i is not None:
                            fetch_d(act, i + 1, s)
                    act.wait_ge(y_turned, q + 1)
                    act.activation(y[:, 0:BANK], E.bank(0), ACT.Copy).then_inc(y_act, 1)
                with act.Fori(0, n_pass) as p:
                    with act.Fori(0, PAIRS - 1) as i:
                        turn_(act.snap(p * PAIRS + i), i)
                    turn_(act.snap(p * PAIRS + PAIRS - 1), None)
                    with act.If(p + 1 < n_pass):
                        for s in range(2):
                            fetch_gu(act, 0, s)
                            fetch_d(act, 0, s)
                    act.nop()

            @block.vector
            def _(dve):
                n_pass = dve.value_load(R.passes[0:1, 0:1], min_val=1, max_val=S // SLOTS)
                dve.memset(back[:], 0.0)
                dve.memset(y[:], 0.0).then_inc(keyed, 1)
                dve.wait_ge(keyed, 1)
                dve.sem_inc(y_dve, 1)
                dve.sem_inc(back_out, 1)
                dve.sem_inc(added, 2)
                dve.sem_inc(hids, 2)
                with dve.Fori(0, n_pass) as p:
                    with dve.Fori(0, PAIRS) as i:
                        q = dve.snap(p * PAIRS + i)

                        def add(n):
                            dve.wait_ge(scattered, 8 * q + n + 1)
                            dve.tensor_tensor(E.hT[:, n, 0:S], E.hT[:, n, 0:S], E.bank(6 + n % 2), ALU.add).then_inc(added, 1)
                        dve.wait_ge(weighted, q + 1)
                        dve.wait_ge(keyed, p + 1)
                        dve.tensor_tensor(sel[:].rearrange("p t (e s) -> p t e s", e=2),
                                          R.slot[:].unsqueeze(1).unsqueeze(1).to_broadcast([P, 4, 2, SLOTS]),
                                          R.key[:, :, bass.ds(2 * i, 2)].unsqueeze(3).to_broadcast([P, 4, 2, SLOTS]),
                                          ALU.is_equal).then_inc(selected, 1)
                        for n in range(6):
                            add(n)
                        dve.wait_ge(gathered, q + 1)
                        dve.tensor_copy(xg[:, 4:8, :], E.bank(5).rearrange("p (k n) -> p k n", k=4)).then_inc(xg_dve, 1)
                        add(6)
                        add(7)
                        for s in range(2):
                            dve.wait_ge(silus, 2 * q + s + 1)
                            dve.tensor_tensor(hid[:, s], sg[:, s], E.bank(2 + s)[:, FT * SLOTS:2 * FT * SLOTS], ALU.mult)\
                               .then_inc(hids, 1)
                        dve.wait_ge(sel_turned, q + 1)
                        dve.tensor_copy(back[:], E.bank(2)).then_inc(back_out, 1)
                        dve.wait_ge(y_turned, q + 1)
                        dve.tensor_copy(y[:, BANK:D], E.bank(1)).then_inc(y_dve, 1)
                    dve.wait_ge(selected, p * PAIRS + PAIRS)
                    dve.tensor_scalar(R.key[:], R.key[:], -float(SLOTS), None, ALU.add).then_inc(keyed, 1)

            @block.gpsimd
            def _(pool):
                n_pass = pool.value_load(R.passes[0:1, 0:1], min_val=1, max_val=S // SLOTS)
                pool.sem_inc(weighted, 1)
                with pool.Fori(0, n_pass) as p, pool.Fori(0, PAIRS) as i:
                    q = pool.snap(p * PAIRS + i)
                    pool.wait_ge(selected, q + 1)
                    pool.wait_ge(back_out, q + 1)
                    pool.tensor_tensor(selg[:].rearrange("p t (e s) -> p t e s", e=2),
                                       sel[:].bitcast(FP).rearrange("p t (e s) -> p t e s", e=2),
                                       R.gate[:, :, bass.ds(2 * i, 2)].unsqueeze(3).to_broadcast([P, 4, 2, SLOTS]),
                                       ALU.mult).then_inc(weighted, 1)
        last_in, last_out = sem("exp_last_scattered"), sem("exp_last_added")
        with nc.Block() as block:
            @block.tensor
            def _(pe):
                for n in range(KT):
                    pe.matmul(E.bank(n), y[:, n * P:(n + 1) * P], back[:], start=True, stop=True).then_inc(last_in, 1)

            @block.vector
            def _(dve):
                for n in range(KT):
                    dve.wait_ge(last_in, n + 1)
                    dve.tensor_tensor(E.hT[:, n, 0:S], E.hT[:, n, 0:S], E.bank(n), ALU.add).then_inc(last_out, 1)


def expert(w, e):
    return w[0][bass.ds(e, 1)].rearrange("o (k p) n -> p (o k) n", p=P)


def moe(E):
    nc, d, sem = E.nc, E.d, E.sem
    with ExitStack() as c:
        sb = lambda n, s, dt=FP: c.enter_context(nc.sbuf_tensor(n, s, dt))
        R = Parts()
        R.wg, R.wu, R.wd = sb("e_wg", [P, 2, KT, D_EXP]), sb("e_wu", [P, 2, KT, D_EXP]), sb("e_wd", [P, 2, D_EXP // P, D])
        R.in_gu, R.in_d = ([sem(f"exp_{n}_loaded{i}") for i in range(2)] for n in ("gate_up", "down"))
        with nc.Block() as block:
            @block.scalar
            def _(act):
                for s in range(2):
                    act.dma_start(R.wg[:, s], expert(d["w_gate"], s)).then_inc(R.in_gu[s], 16)
                    act.dma_start(R.wu[:, s], expert(d["w_up"], s)).then_inc(R.in_gu[s], 16)
                    act.dma_start(R.wd[:, s], expert(d["w_down"], s)).then_inc(R.in_d[s], 16)
        norm(E, "n2", E.hT, E.aT, KT, D, S, lambda k, s: E.v("norm2_g", k))
        R.gate, R.key, R.slot = sb("r_gate", [P, 4, N_EXP]), sb("r_key", [P, 4, N_EXP]), sb("r_slot", [P, SLOTS])
        R.passes = sb("r_passes", [P, 1], mybir.dt.int32)
        route(E, R)
        R.xh, R.xl = sb("e_xh", [P, 4, D], mybir.dt.float32r), sb("e_xl", [P, 4, D], mybir.dt.float32r)
        token_rows(E, R)
        experts(E, R)
    norm(E, "nf", E.hT, E.hT, KT, D, S, lambda k, s: E.v("norm_f_g", k))


N_MOD, D_FF = 6, 4 * D


def modulation(E):
    nc, d, sem = E.nc, E.d, E.sem
    turns = N_MOD * D // 512 // 2
    loaded = [sem(f"ada_w_loaded{i}") for i in range(2)]
    silus, full, biased, scaled = (sem(f"ada_{x}") for x in ("silu", "full", "biased", "scaled"))
    with nc.sbuf_tensor("ada_c", [P, KT, 2], FP) as cs, nc.sbuf_tensor("ada_ring", [P, 2, KT, 512], FP) as ring, \
            nc.Block() as block:
        ada = [d["ada_w_2"][l].rearrange("(k p) (g n) -> g p k n", p=P, n=512) for l in range(2)]
        b0 = VEC_AT["ada_b_2"]

        @block.scalar
        def _(act):
            for s, name in enumerate(("c_2", "c_ctx_2")):
                last = act.activation(cs[:, :, s], E.vcol[:, VEC_AT[name]:VEC_AT[name] + KT], ACT.Silu)
            last.then_inc(silus, 1)
            for s in range(2):
                act.dma_start(ring[:, s], ada[0][s]).then_inc(loaded[s], 16)
            for layer in range(2):
                with act.Fori(0, turns - 1) as i:
                    for s in range(2):
                        act.wait_ge(full, 2 * i + 2 * turns * layer + s + 1)
                        act.dma_start(ring[:, s], ada[layer][bass.ds(2 * i + s + 2, 1)].rearrange("o p k n -> p (o k) n"))\
                           .then_inc(loaded[s], 16)
                if layer == 0:
                    for s in range(2):
                        act.wait_ge(full, 2 * (turns - 1) + s + 1)
                        act.dma_start(ring[:, s], ada[1][s]).then_inc(loaded[s], 16)

        @block.tensor
        def _(pe):
            pe.wait_ge(silus, 1)
            with pe.Fori(0, 2 * turns) as i:
                for s in range(2):
                    pe.wait_ge(loaded[s], 16 * i + 16)
                    pe.wait_ge(biased, 2 * i + 1)
                    for n in range(4):
                        for k in range(KT):
                            last = pe.matmul(E.bank(s)[:, 2 * n:2 * n + 2], ring[:, s, k, n * P:(n + 1) * P], cs[:, k, :],
                                             start=(k == 0), stop=(k == KT - 1))
                    last.then_inc(full, 1)

        @block.vector
        def _(dve):
            flat = E.mod[:].rearrange("p l m s -> p (l m) s")
            dve.sem_inc(biased, 1)
            with dve.Fori(0, 2 * turns) as i:
                for s in range(2):
                    dve.wait_ge(full, 2 * i + s + 1)
                    dve.tensor_tensor(flat[:, bass.ds(8 * i + 4 * s, 4), :], E.bank(s, 8).rearrange("p (n s) -> p n s", s=2),
                                      E.vcol[:, bass.ds(8 * i + b0 + 4 * s, 4)].unsqueeze(2).to_broadcast([P, 4, 2]), ALU.add)\
                       .then_inc(biased, 1)
            dve.wait_ge(biased, 4 * turns + 1)
            for layer in range(2):
                for which, (name, m) in enumerate((("norm1_w_2", 1), ("norm2_w_2", 4))):
                    w = E.vcol[:, VEC_AT[name] + 8 * layer:VEC_AT[name] + 8 * layer + 8].unsqueeze(2).to_broadcast([P, 8, 2])
                    dve.scalar_tensor_tensor(out=E.nw[:, layer, which], in0=E.mod[:, layer, 8 * m:8 * m + 8, :], scalar=1.0,
                                             in1=w, op0=ALU.add, op1=ALU.mult)


def modulated_norm(E, name, layer, which, T):
    segs = [(0, S)] + ([(S, T)] if T > S else [])
    m = 0 if which == 0 else 3
    norm(E, name, E.hT, E.aT, KT, D, T, lambda k, s: E.nw[:, layer, which, k, s:s + 1],
         shift=lambda k, s: E.mod[:, layer, 8 * m + k, s:s + 1], segs=segs)


def mlp(E, layer, T):
    nc, d, sem = E.nc, E.d, E.sem
    name = f"mlp{layer}"
    modulated_norm(E, f"{name}_norm", layer, 1, T)
    FF = D_FF // P
    segs = [(0, S)] + ([(S, T)] if T > S else [])
    ns = len(segs)
    w1 = d["mlp_w1_2"][layer].rearrange("(k p) (g n) -> g p k n", p=P, n=512)
    w2 = [kn(d["mlp_w2_2"][layer][1024 * (j % 4):1024 * (j % 4 + 1), 512 * (j // 4):512 * (j // 4 + 1)]) for j in range(8)]
    U = 4 * ns
    with ExitStack() as c:
        sb = lambda n, s: c.enter_context(nc.sbuf_tensor(n, s, FP))
        h1, ring = sb(f"{name}_h1", [P, FF, T]), sb(f"{name}_ring", [P, 2, KT, 512])
        in1 = [sem(f"{name}_w1_loaded{i}") for i in range(2)]
        in2 = [sem(f"{name}_w2_loaded{i}") for i in range(2)]
        full, relus, full2, taken, added = (sem(f"{name}_{x}") for x in ("full", "relu", "chunk_done", "full2", "added"))
        unit = [(n, s, a, b) for n in range(4) for s, (a, b) in enumerate(segs)]
        with nc.Block() as block:
            @block.scalar
            def _(act):
                act.sem_inc(relus, 1)
                for s in range(2):
                    act.dma_start(ring[:, s], w1[s]).then_inc(in1[s], 16)

                def relu(i, s):
                    for u, (n, _, a, b) in enumerate(unit):
                        act.wait_ge(full, 2 * U * i + U * s + u + 1)
                        act.activation(h1[:, bass.ds(8 * i + 4 * s + n, 1), a:b], E.bank((U * s + u) % 8, b - a).unsqueeze(1),
                                       ACT.Relu).then_inc(relus, 1)
                with act.Fori(0, 3) as i:
                    for s in range(2):
                        relu(i, s)
                        act.dma_start(ring[:, s], w1[bass.ds(2 * i + s + 2, 1)].rearrange("o p k n -> p (o k) n"))\
                           .then_inc(in1[s], 16)
                for s in range(2):
                    relu(3, s)
                    act.dma_start(ring[:, s], w2[s]).then_inc(in2[s], 16)

            @block.tensor
            def _(pe):
                with pe.Fori(0, 4) as i:
                    for s in range(2):
                        pe.wait_ge(in1[s], 16 * i + 16)
                        for u, (n, _, a, b) in enumerate(unit):
                            q = U * s + u
                            if q == 0:
                                pe.wait_ge(relus, 2 * U * i + 1)
                            if q >= 8:
                                pe.wait_ge(relus, 2 * U * i + q - 6)
                            for k in range(KT):
                                last = pe.matmul(E.bank((U * s + u) % 8, b - a), ring[:, s, k, n * P:(n + 1) * P],
                                                 E.aT[:, k, a:b], start=(k == 0), stop=(k == KT - 1))
                            last.then_inc(full, 1)

            @block.vector
            def _(dve):
                with dve.Fori(0, 4) as i:
                    for s in range(2):
                        for u, (n, _, a, b) in enumerate(unit):
                            dve.wait_ge(relus, 2 * U * i + U * s + u + 2)
                            hh = h1[:, bass.ds(8 * i + 4 * s + n, 1), a:b]
                            dve.tensor_tensor(hh, hh, hh, ALU.mult)
        with nc.Block() as block:
            @block.scalar
            def _(act):
                for j in range(2, 8):
                    half, chunk = (j - 2) // 4, (j - 2) % 4
                    act.wait_ge(full2, 3 * half + chunk + 1) if chunk < 3 else act.wait_ge(taken, U * (half + 1))
                    act.dma_start(ring[:, j % 2], w2[j]).then_inc(in2[j % 2], 16)

            @block.tensor
            def _(pe):
                with pe.Fori(0, 2) as g:
                    pe.wait_ge(added, U * g + 1)
                    for j in range(4):
                        pe.wait_ge(in2[j % 2], 32 * g + 16 * (j // 2) + 16)
                        for u, (n, _, a, b) in enumerate(unit):
                            for f in range(8):
                                last = pe.matmul(E.bank(u, b - a), ring[:, j % 2, f, n * P:(n + 1) * P],
                                                 h1[:, 8 * j + f, a:b], start=(j == 0 and f == 0),
                                                 stop=(j == 3 and f == 7))
                            if j == 3:
                                last.then_inc(taken, 1)
                        if j < 3:
                            last.then_inc(full2, 1)

            @block.vector
            def _(dve):
                dve.sem_inc(added, 1)
                for g in range(2):
                    for u, (n, s, a, b) in enumerate(unit):
                        dve.wait_ge(taken, U * g + u + 1)
                        k = 4 * g + n
                        dve.scalar_tensor_tensor(out=E.hT[:, k, a:b], in0=E.bank(u, b - a),
                                                 scalar=E.mod[:, layer, 40 + k, s:s + 1], in1=E.hT[:, k, a:b],
                                                 op0=ALU.mult, op1=ALU.add).then_inc(added, 1)


def even_mixer(E):
    nc, d, sem = E.nc, E.d, E.sem
    w = d["even_w_in_2"][0]
    aT = E.aT
    segs = [(0, S), (S, TT)]
    modulated_norm(E, "even_norm", 0, 0, TT)
    with ExitStack() as c:
        sb = lambda n, s: c.enter_context(nc.sbuf_tensor(n, s, FP))
        cq, ckv, kpe = sb("cq", [P, 3, TT]), sb("ckv", [P, 2, TT]), sb("kpe", [P, TT])
        gq, gk, gv, gg, glow = sb("gq", [P, 2, TT]), sb("gk", [P, 2, TT]), sb("gv", [P, 6, 512]), sb("gg", [P, 4, TT]), \
            sb("glow", [32, TT])

        def feats(n0, tiles, dst, func=ACT.Copy, scale=1.0):
            return [feature_unit(E, aT, n0 + n * P, P, a, b, "act", act_copy(dst[:, n, a:b], func, scale))
                    if func != ACT.Copy or n % 2 or scale != 1.0 else
                    feature_unit(E, aT, n0 + n * P, P, a, b, "dve", dve_copy(dst[:, n, a:b]))
                    for n in range(tiles) for a, b in segs]

        def kpe_unit(a, b):
            def mms(wt, bank):
                return [(E.ps[64:96, bank * BANK:bank * BANK + b - a], wt[:, k, 256:288], aT[:, k, a:b]) for k in range(KT)]
            return (mms, "dve", lambda eng, bank: eng.tensor_copy(kpe[64:96, a:b], E.ps[64:96, bank * BANK:bank * BANK + b - a]))
        gemm(E, "proj2", [
            dict(w=kn(w[:, 0:384]), units=feats(0, 3, cq)),
            dict(w=kn(w[:, 384:672]), units=feats(0, 2, ckv) + [kpe_unit(a, b) for a, b in segs]),
            dict(w=kn(w[:, 672:1184]), units=feats(0, 2, gq, scale=0.125) + feats(256, 2, gk)),
            dict(w=kn(w[:, 1184:1696]), units=[token_unit(E, aT, t * P, 512, "act" if t % 2 else "dve",
                                                          (act_copy if t % 2 else dve_copy)(gv[:, t, :])) for t in range(6)]),
            dict(w=kn(w[:, 1696:2240]), units=feats(0, 4, gg, func=ACT.Silu) + [
                feature_unit(E, aT, 512, 32, a, b, "dve", dve_copy(glow[:, a:b])) for a, b in segs]),
        ])
        gla(E, gq, gk, gv, gg, glow)
        mla(E, cq, ckv, kpe)
    resid_gemm(E, "wout2", d["even_w_out_2"][0], aT, TT, lambda n, s: E.mod[:, 0, 16 + n, s:s + 1])


def mla(E, cq, ckv, kpe):
    nc, d, sem = E.nc, E.d, E.sem
    segs = [(0, S), (S, TT)]
    norm(E, "cq_norm", cq, cq, 3, 384, TT, lambda k, s: E.v("mla_q_norm_2", k))
    norm(E, "ckv_norm", ckv, ckv, 2, 256, TT, lambda k, s: E.v("mla_kv_norm_2", k))
    QK = 96
    with ExitStack() as c:
        sb = lambda n, s: c.enter_context(nc.sbuf_tensor(n, s, FP))
        O = sb("mla_o", [P, 6, 512])
        with ExitStack() as c2:
            sb2 = lambda n, s: c2.enter_context(nc.sbuf_tensor(n, s, FP))
            qh, kh, V = sb2("mla_q", [P, HEADS, TT]), sb2("mla_k", [P, HEADS, TT]), sb2("mla_v", [P, 6, 512])
            gemm(E, "mla_up", [
                dict(w=kn(d["mla_w_uq_2"][0]), units=[
                    feature_unit(E, cq, QK * h, QK, a, b, "act", act_copy(qh[0:QK, h, a:b], scale=QK ** -0.5), kt=3)
                    for h in range(HEADS) for a, b in segs]),
                dict(w=kn(d["mla_w_ukv_2"][0]), units=[
                    feature_unit(E, ckv, P * h, 64, a, b, "dve", dve_copy(kh[0:64, h, a:b]), kt=2)
                    for h in range(HEADS) for a, b in segs] + [
                    token_unit(E, ckv, t * P, 512, "act", act_copy(V[:, t, :]), kt=2,
                               pick=lambda wt, k: wt[:, k, :].rearrange("p (h x) -> p h x", x=P)[:, :, 64:128])
                    for t in range(6)])])
            rope(E, qh, kh, kpe)
            mla_units(E, qh, kh, V, O)
        turn(E, "mla_oturn", [([O[:, i, k * P:(k + 1) * P] for i in ts], E.aT[:, k, ts[0] * P:(ts[-1] + 1) * P])
                              for k in range(4) for ts in ((0, 1, 2, 3), (4, 5))])


def rope(E, qh, kh, kpe):
    nc, sem = E.nc, E.sem
    with ExitStack() as c:
        sb = lambda n, s: c.enter_context(nc.sbuf_tensor(n, s, FP))
        cos, sin, rot, part = sb("cos", [P, S]), sb("sin", [P, S]), sb("rot", [P, 32]), sb("rope_part", [P, 2, S])
        loaded, swapped, own, part_s, done = (sem(f"rope_{x}") for x in ("loaded", "swapped", "own", "partner", "done"))
        items = [kpe[64:96, 0:S]] + [qh[64:96, h, 0:S] for h in range(HEADS)]
        with nc.Block() as block:
            @block.sync
            def _(sp):
                sp.dma_start(cos[64:96, :], E.cst("cos")[64:96, 0:S]).then_inc(loaded, 16)
                sp.dma_start(sin[64:96, :], E.cst("sin")[64:96, 0:S]).then_inc(loaded, 16)
                sp.dma_start(rot[64:96, :], E.cst("rot")[64:96, :]).then_inc(loaded, 16)

            @block.tensor
            def _(pe):
                pe.wait_ge(loaded, 48)
                for i, x in enumerate(items):
                    if i >= 2:
                        pe.wait_ge(part_s, i - 1)
                    pe.matmul(E.ps[64:96, (i % 2) * BANK:(i % 2) * BANK + S], rot[64:96, :], x, start=True, stop=True)\
                      .then_inc(swapped, 1)

            @block.vector
            def _(dve):
                dve.wait_ge(loaded, 48)
                for i, x in enumerate(items):
                    dve.wait_ge(swapped, i + 1)
                    dve.tensor_tensor(part[64:96, i % 2, :], sin[64:96, :], E.ps[64:96, (i % 2) * BANK:(i % 2) * BANK + S],
                                      ALU.mult).then_inc(part_s, 1)
                    dve.tensor_tensor(x, x, cos[64:96, :], ALU.mult).then_inc(own, 1)
                    dve.wait_ge(own, i + 1)
                    dve.wait_ge(part_s, i + 1)
                    dve.tensor_tensor(x, x, part[64:96, i % 2, :], ALU.add).then_inc(done, 1)

            @block.scalar
            def _(act):
                act.wait_ge(done, 1)
                for h in range(HEADS):
                    act.activation(kh[64:96, h, :], kpe[64:96, :], ACT.Copy)


def mla_units(E, qh, kh, V, O):
    nc, sem = E.nc, E.sem
    QK = 96
    units = [(h, i, 0, TT) if i < 4 else (h, i, S, TT) for h in range(HEADS) for i in range(6)]
    n = len(units)
    scored, maxed, exped, turned, evac_a, evac_v, summed, done = (
        sem(f"mla_{x}") for x in ("scored", "maxed", "exped", "turned", "evac_a", "evac_v", "summed", "done"))
    with ExitStack() as c:
        sb = lambda nm, s: c.enter_context(nc.sbuf_tensor(nm, s, FP))
        pr, pT = sb("mla_pr", [P, 2, TT]), sb("mla_pT", [P, 2, TT])
        neg, tot, inv = (sb(x, [P, n]) for x in ("mla_neg", "mla_tot", "mla_inv"))
        block = c.enter_context(nc.Block())
        score = lambda u, L: E.ps[:, (u % 2) * 2 * BANK:(u % 2) * 2 * BANK + L]

        @block.tensor
        def _(pe):
            for t in range(n + 2):
                if t < n:
                    h, i, k0, k1 = units[t]
                    if t >= 2:
                        pe.wait_ge(exped, t - 1)
                    for a in range(0, k1 - k0, BANK):
                        b = min(a + BANK, k1 - k0)
                        last = pe.matmul(score(t, b)[:, a:b], qh[0:QK, h, i * P:(i + 1) * P], kh[0:QK, h, k0 + a:k0 + b],
                                         start=True, stop=True)
                    last.then_inc(scored, 1)
                if 1 <= t <= n:
                    u = t - 1
                    h, i, k0, k1 = units[u]
                    pe.wait_ge(exped, u + 1)
                    if u >= 1:
                        pe.wait_ge(evac_a, u)
                        pe.wait_ge(evac_v, u)
                    for j in range((k1 - k0) // P):
                        last = pe.transpose(E.ps[:, 4 * BANK + j * P:4 * BANK + (j + 1) * P], pr[:, u % 2, j * P:(j + 1) * P],
                                            E.ident)
                    last.then_inc(turned, 1)
                if t >= 2:
                    u = t - 2
                    h, i, k0, k1 = units[u]
                    pe.wait_ge(evac_a, u + 1)
                    pe.wait_ge(evac_v, u + 1)
                    if u >= 2:
                        pe.wait_ge(done, u - 1)
                    J = (k1 - k0) // P
                    for j in range(J):
                        last = pe.matmul(E.bank(6 + u % 2, 64), pT[:, u % 2, j * P:(j + 1) * P],
                                         V[:, k0 // P + j, h * 64:(h + 1) * 64], start=(j == 0), stop=(j == J - 1))
                    last.then_inc(summed, 1)

        @block.scalar
        def _(act):
            for t in range(n + 1):
                if t < n:
                    L = units[t][3] - units[t][2]
                    act.wait_ge(maxed, t + 1)
                    if t >= 2:
                        act.wait_ge(turned, t - 1)
                    act.activation(pr[:, t % 2, 0:L], score(t, L), ACT.Exp, bias=neg[:, t:t + 1],
                                   accum_out=tot[:, t:t + 1]).then_inc(exped, 1)
                if t >= 1:
                    u = t - 1
                    L = min(BANK, units[u][3] - units[u][2])
                    act.wait_ge(turned, u + 1)
                    if u >= 2:
                        act.wait_ge(summed, u - 1)
                    act.activation(pT[:, u % 2, 0:L], E.bank(4, L), ACT.Copy).then_inc(evac_a, 1)

        @block.vector
        def _(dve):
            for t in range(n + 3):
                if t < n:
                    L = units[t][3] - units[t][2]
                    dve.wait_ge(scored, t + 1)
                    dve.tensor_reduce(neg[:, t:t + 1], score(t, L), AX.X, ALU.max, negate=True).then_inc(maxed, 1)
                if 1 <= t <= n:
                    u = t - 1
                    L = units[u][3] - units[u][2]
                    dve.wait_ge(turned, u + 1)
                    if u >= 2:
                        dve.wait_ge(summed, u - 1)
                    if L > BANK:
                        dve.tensor_copy(pT[:, u % 2, BANK:L], E.bank(5, L - BANK)).then_inc(evac_v, 1)
                        dve.reciprocal(inv[:, u:u + 1], tot[:, u:u + 1])
                    else:
                        dve.reciprocal(inv[:, u:u + 1], tot[:, u:u + 1]).then_inc(evac_v, 1)
                if t >= 3:
                    u = t - 3
                    h, i, _, _ = units[u]
                    dve.wait_ge(summed, u + 1)
                    dve.tensor_scalar(O[:, i, h * 64:(h + 1) * 64], E.bank(6 + u % 2, 64), inv[:, u:u + 1], None,
                                      ALU.mult).then_inc(done, 1)


GLA_C = 64
NCH = TT // GLA_C


def step_of(z, ch):
    return (ch + 4 if ch < 8 else ch - 8) if z == 0 else 11 - ch


def gla(E, gq, gk, gv, gg, glow):
    nc, d, sem = E.nc, E.d, E.sem
    C = GLA_C
    full = [P, 4, TT]
    with ExitStack() as c:
        sb = lambda n, s: c.enter_context(nc.sbuf_tensor(n, s, FP))
        gate_up, reset, masks = sb("gla_gate_up", [32, 2, 256]), sb("gla_reset", [P, TT]), sb("gla_masks", [P, 2, P])
        dec = sb("gla_dec", [P, 4, NCH])
        lg, B, qd, ki = sb("gla_lg", full), sb("gla_B", full), sb("gla_qd", full), sb("gla_ki", full)
        zeroed, loaded, logits, biased, a, v = (sem(f"gla_{x}") for x in ("zeroed", "loaded", "logits", "biased", "act", "dve"))
        with nc.Block() as block:
            @block.gpsimd
            def _(pool):
                pool.memset(gate_up[:], 0.0).then_inc(zeroed, 1)

            @block.sync
            def _(sp):
                sp.dma_start(reset[:], E.cst("reset64")).then_inc(loaded, 16)
                sp.dma_start(masks[:, 0, :], E.cst("fwd64")).then_inc(loaded, 16)
                sp.dma_start(masks[:, 1, :], E.cst("bwd64")).then_inc(loaded, 16)
                sp.wait_ge(zeroed, 1)
                for z in range(2):
                    sp.dma_start(gate_up[16 * z:16 * z + 16, z, :], d["gla_gate_up_2"][0, z]).then_inc(loaded, 16)

            @block.tensor
            def _(pe):
                pe.wait_ge(loaded, 80)
                for q in range(4):
                    for b, (t0, t1) in enumerate(((0, S), (S, TT))):
                        last = pe.matmul(E.bank(2 * q + b, t1 - t0), gate_up[:, q // 2, (q % 2) * P:(q % 2 + 1) * P],
                                         glow[:, t0:t1], start=True, stop=True)
                    last.then_inc(logits, 1)

            @block.scalar
            def _(act):
                for q in range(4):
                    act.wait_ge(logits, q + 1)
                    act.activation(lg[:, q, :], E.ps[:, 2 * q * BANK:2 * q * BANK + TT], ACT.Identity,
                                   bias=E.v("gla_gate_bias_2", q)).then_inc(biased, 1)
                act.wait_ge(v, 1)
                act.activation(B[:], B[:], ACT.Exp).then_inc(a, 1)
                act.wait_ge(a, 1)
                act.activation(B[:], B[:], ACT.Ln, bias=1.0).then_inc(a, 1)
                act.wait_ge(v, 7)
                act.activation(qd[:], B[:], ACT.Exp, scale=1 / 16).then_inc(a, 1)
                act.activation(ki[:], B[:], ACT.Exp, scale=-1 / 16).then_inc(a, 1)
                act.wait_ge(v, 8)
                act.activation(lg[:], lg[:], ACT.Exp, scale=1 / 16).then_inc(a, 1)
                act.activation(dec[:], dec[:], ACT.Exp, scale=1 / 16).then_inc(a, 1)

            @block.vector
            def _(dve):
                dve.wait_ge(biased, 4)
                dve.scalar_tensor_tensor(out=B[:], in0=lg[:], scalar=-1.0, in1=lg[:], op0=ALU.mult, op1=ALU.min).then_inc(v, 1)
                dve.wait_ge(a, 2)
                dve.scalar_tensor_tensor(out=lg[:], in0=lg[:], scalar=0.0, in1=B[:], op0=ALU.min, op1=ALU.subtract)\
                   .then_inc(v, 1)
                dve.wait_ge(loaded, 80)
                dve.wait_ge(v, 2)
                for q in range(4):
                    last = dve.tensor_tensor_scan(B[:, q, :], reset[:], lg[:, q, :], 0.0, ALU.mult, ALU.add)
                last.then_inc(v, 1)
                dve.wait_ge(v, 3)
                ch = lambda x: x.rearrange("p q (c t) -> p q c t", t=C)
                flat = lambda x: x.rearrange("p q (c t) -> p (q c) t", t=C)
                dve.tensor_copy(dec[:], ch(B[:])[:, :, :, C - 1]).then_inc(v, 1)
                dve.wait_ge(v, 4)
                tot = dec[:].rearrange("p q c -> p (q c)").unsqueeze(2)
                dve.tensor_tensor(lg[:, 2:4, :], lg[:, 2:4, :], B[:, 2:4, :], ALU.subtract).then_inc(v, 1)
                dve.wait_ge(v, 5)
                dve.tensor_tensor(flat(B[:, 2:4, :]), flat(lg[:, 2:4, :]), tot[:, 24:48].to_broadcast([P, 24, C]), ALU.add)\
                   .then_inc(v, 2)
                dve.wait_ge(v, 7)
                dve.tensor_tensor(flat(lg[:]), tot.to_broadcast([P, 48, C]), flat(B[:]), ALU.subtract).then_inc(v, 1)
                dve.wait_ge(a, 5)
                for z in range(2):
                    dve.tensor_tensor(qd[:, 2 * z:2 * z + 2, :], qd[:, 2 * z:2 * z + 2, :], gq[:], ALU.mult)
                    dve.tensor_tensor(ki[:, 2 * z:2 * z + 2, :], ki[:, 2 * z:2 * z + 2, :], gk[:], ALU.mult)
                    dve.tensor_tensor(lg[:, 2 * z:2 * z + 2, :], lg[:, 2 * z:2 * z + 2, :], gk[:], ALU.mult)
        kt = B[:].rearrange("p q t -> p (q t)").rearrange("p (i n) -> p i n", n=512)
        turn(E, "gla_kturn", [([lg[:, q, i * P:(i + 1) * P] for q in range(4)], kt[:, i, :]) for i in range(6)])
        St = sb("gla_states", [P, 4, P, NCH])
        gains, out, decd, scanned = (sem(f"gla_{x}") for x in ("gains", "gains_out", "decay_spread", "scanned"))
        with ExitStack() as c2:
            dS, decx = (c2.enter_context(nc.sbuf_tensor(n, [P, P, NCH], FP)) for n in ("gla_dS", "gla_decx"))
            block = c2.enter_context(nc.Block())

            def place(z, t):
                return (0, t if z == 0 else 3 - t) if t < 4 else (1, t - 4 if z == 0 else 5 - t)

            @block.tensor
            def _(pe):
                for q in range(4):
                    z, j = q // 2, q % 2
                    if q >= 2:
                        pe.wait_ge(out, q - 1)
                    for t in range(6):
                        for r in range(2):
                            half, slot = place(z, t)
                            at = (4 * (q % 2) + 2 * r + half) * BANK + P * slot
                            for h2 in range(2):
                                last = pe.matmul(E.ps[64 * h2:64 * h2 + 64, at:at + P],
                                                 kt[64 * r:64 * r + 64, t, q * P + 64 * h2:q * P + 64 * h2 + 64],
                                                 gv[64 * r:64 * r + 64, t, (2 * j + h2) * P:(2 * j + h2 + 1) * P],
                                                 start=True, stop=True)
                    last.then_inc(gains, 1)

            @block.scalar
            def _(act):
                for q in range(4):
                    z = q // 2
                    act.wait_ge(gains, q + 1)
                    if q >= 1:
                        act.wait_ge(scanned, q)
                    for r in range(2):
                        for half, n, first in ((0, 4, 4 + r if z == 0 else 5 - r), (1, 2, r if z == 0 else 1 - r)):
                            last = act.activation(dS[:, :, first:first + 2 * n - 1:2].rearrange("p v s -> p s v"),
                                                  E.bank(4 * (q % 2) + 2 * r + half, n * P).rearrange("p (s v) -> p s v", v=P),
                                                  ACT.Copy)
                    last.then_inc(out, 1)

            @block.vector
            def _(dve):
                m = 0
                for q in range(4):
                    for ch in range(NCH):
                        last = dve.tensor_copy(decx[:, :, step_of(q // 2, ch):step_of(q // 2, ch) + 1],
                                               dec[:, q:q + 1, ch:ch + 1].to_broadcast([P, P, 1]))
                    last.then_inc(decd, 1)
                    dve.wait_ge(decd, 2 * q + 1)
                    dve.memset(decx[:, :, 0:1], 0.0).then_inc(decd, 1)
                    dve.wait_ge(decd, 2 * q + 2)
                    dve.wait_ge(out, q + 1)
                    dve.tensor_tensor_scan(St[:, q].rearrange("p v s -> p (v s)"), decx[:].rearrange("p v s -> p (v s)"),
                                           dS[:].rearrange("p v s -> p (v s)"), 0.0, ALU.mult, ALU.add).then_inc(scanned, 1)
                    dve.wait_ge(scanned, q + 1)
        AT = sb("gla_AT", [P, 2, 2, P])
        oT = lg
        scored, masked, summed, taken = (sem(f"gla_{x}") for x in ("scored", "masked", "summed", "taken"))
        units = [(h, t) for h in range(4) for t in range(6)]
        n = len(units)
        with nc.Block() as block:
            @block.tensor
            def _(pe):
                for u in range(n + 1):
                    if u < n:
                        h, t = units[u]
                        lo, j = 64 * (h % 2), h // 2
                        if u >= 2:
                            pe.wait_ge(masked, u - 1)
                        for z in range(2):
                            last = pe.matmul(E.bank(u % 2, 2 * P)[:, z * P:(z + 1) * P], ki[lo:lo + 64, 2 * z + j, t * P:(t + 1) * P],
                                             qd[lo:lo + 64, 2 * z + j, t * P:(t + 1) * P], start=True, stop=True)
                        last.then_inc(scored, 1)
                    if u >= 1:
                        w = u - 1
                        h, t = units[w]
                        lo, j = 64 * (h % 2), h // 2
                        pe.wait_ge(masked, w + 1)
                        if w >= 2:
                            pe.wait_ge(taken, w - 1)
                        o = E.bank(2 + w % 2, P)
                        for z in range(2):
                            last = pe.matmul(o, gv[:, t, h * P:(h + 1) * P], AT[:, w % 2, z, :], start=(z == 0), stop=False,
                                             skip_group_check=True)
                        for z in range(2):
                            for r in range(2):
                                st = step_of(z, 2 * t + r)
                                if st:
                                    last = pe.matmul(o[:, 64 * r:64 * r + 64], St[lo:lo + 64, 2 * z + j, :, st - 1],
                                                     qd[lo:lo + 64, 2 * z + j, (2 * t + r) * 64:(2 * t + r + 1) * 64],
                                                     start=False, stop=(z == 1 and r == 1), skip_group_check=True)
                        last.then_inc(summed, 1)

            @block.vector
            def _(dve):
                for u in range(n):
                    dve.wait_ge(scored, u + 1)
                    if u >= 2:
                        dve.wait_ge(summed, u - 1)
                    dve.tensor_tensor(AT[:, u % 2], masks[:], E.bank(u % 2, 2 * P).rearrange("p (z t) -> p z t", z=2),
                                      ALU.mult).then_inc(masked, 1)

            @block.scalar
            def _(act):
                for u, (h, t) in enumerate(units):
                    act.wait_ge(summed, u + 1)
                    act.activation(oT[:, h, t * P:(t + 1) * P], E.bank(2 + u % 2, P), ACT.Copy).then_inc(taken, 1)
        gated_norm(E, "gla_norm", oT, E.aT[:, 4:8, :], 4, TT, P, E.ones, lambda k: E.v("gla_o_norm_2", 0), gg)


def odd_mixer(E):
    nc, d, sem = E.nc, E.d, E.sem
    modulated_norm(E, "odd_norm", 1, 0, TT)
    w = d["gdn_w_in_2"][0]
    gate_dram = nc.dram_tensor("gdn_gate", [P, KT, S], FP).ap()
    ab_dram = nc.dram_tensor("gdn_ab", [2, 16, TT], FP).ap()
    with ExitStack() as c:
        sb = lambda n, s: c.enter_context(nc.sbuf_tensor(n, s, FP))
        gate, la, be = sb("gdn_gate_sb", [P, KT, S]), sb("gdn_la_rows", [16, TT]), sb("gdn_be_rows", [16, TT])
        silu = lambda dst: act_copy(dst, ACT.Silu)
        gemm(E, "proj3", [dict(w=kn(w[:, 2048 + 512 * g:2560 + 512 * g]),
                               units=[feature_unit(E, E.aT, n * P, P, 0, S, "act", silu(gate[:, 4 * g + n, :]))
                                      for n in range(4)]) for g in range(2)] + [
            dict(w=kn(w[:, 3072:3104]), units=[feature_unit(E, E.aT, 16 * i, 16, a, b, "dve", dve_copy(x[:, a:b]))
                                               for i, x in enumerate((la, be)) for a, b in ((0, S), (S, TT))])])
        decay_and_beta(E, gate, la, be, gate_dram, ab_dram)
    with ExitStack() as c:
        sb = lambda n, s: c.enter_context(nc.sbuf_tensor(n, s, FP))
        G = Parts()
        G.KT, G.QT, G.V = sb("gdn_KT", [P, NCH, 4, P]), sb("gdn_QT", [P, 8, 4, P]), sb("gdn_V", [P, NCH, 4, P])
        G.K = E.aT[:].rearrange("p k t -> p (k t)").rearrange("p (c q n) -> p c q n", c=NCH, q=4)
        G.LA, G.BE, G.GC, G.EGL, G.GE, G.BEG = (sb(f"gdn_{n}", [P, 2, 4, NCH])
                                                for n in ("LA", "BE", "GC", "EGL", "GE", "BEG"))
        with ExitStack() as c2:
            sb2 = lambda n, s: c2.enter_context(nc.sbuf_tensor(n, s, FP))
            q, k, vc = sb2("gdn_q_raw", [P, 4, S]), sb2("gdn_k_raw", [P, 4, TT]), sb2("gdn_v_raw", [P, 4, NCH, 2, 64])
            short_conv(E, w, q, k, vc)
            l2_blocks(E, G, q, k)
            turn(E, "gdn_vturn", [([vc[:, p, ch].rearrange("a h t -> a (h t)") for p in range(4)],
                                   G.V[:, ch].rearrange("a p n -> a (p n)")) for ch in range(NCH)])
            turn(E, "gdn_kturn2", [([G.KT[:, ch, p, :] for p in range(4)], G.K[:, ch].rearrange("a p n -> a (p n)"))
                                   for ch in range(NCH)])
        chunk_scalars(E, G, ab_dram)
        O = sb("gdn_o", [P, KT, S])
        delta(E, G, O)
        load(E, "gdn_gate_back", [(G.V[:].rearrange("a c p n -> a (c p n)")[:, 0:KT * S],
                                   gate_dram.rearrange("p k t -> p (k t)"))])
        gate = G.V[:].rearrange("a c p n -> a (c p n)")[:, 0:KT * S].rearrange("a (k t) -> a k t", t=S)
        gated_norm(E, "gdn_norm", O, E.aT, KT, S, P, E.ones, lambda k: E.v("gdn_o_norm_2", 0), gate)
    resid_gemm(E, "wout3", d["gdn_w_out_2"][0], E.aT, S, lambda n, s: E.mod[:, 1, 16 + n, s:s + 1])


def decay_and_beta(E, gate, la, be, gate_dram, ab_dram):
    nc, d, sem = E.nc, E.d, E.sem
    with ExitStack() as c:
        col, e = c.enter_context(nc.sbuf_tensor("gdn_cols", [16, 2], FP)), c.enter_context(nc.sbuf_tensor("gdn_e", [16, TT], FP))
        loaded, stored, a, v = (sem(f"ab_{x}") for x in ("loaded", "stored", "act", "dve"))
        with nc.Block() as block:
            @block.sync
            def _(sp):
                sp.dma_start(col[:, 0:1], d["gdn_dt_bias_2"].rearrange("o z (h i) -> (o z h) i", i=1)).then_inc(loaded, 16)
                sp.dma_start(col[:, 1:2], d["gdn_a_log_2"].rearrange("o z (h i) -> (o z h) i", i=1)).then_inc(loaded, 16)
                sp.dma_start(gate_dram, gate[:]).then_inc(stored, 16)
                sp.wait_ge(v, 8)
                sp.dma_start(ab_dram[0], la[:]).then_inc(stored, 16)
                sp.dma_start(ab_dram[1], be[:]).then_inc(stored, 16)
                sp.wait_ge(stored, 48)

            @block.scalar
            def _(act):
                act.wait_ge(loaded, 32)
                act.activation(col[:, 1:2], col[:, 1:2], ACT.Exp).then_inc(a, 1)
                act.activation(be[:], be[:], ACT.Exp, scale=-1.0).then_inc(a, 1)
                act.wait_ge(v, 2)
                act.activation(e[:], e[:], ACT.Exp).then_inc(a, 1)
                act.wait_ge(a, 3)
                act.activation(e[:], e[:], ACT.Ln, bias=1.0).then_inc(a, 1)

            @block.vector
            def _(dve):
                dve.wait_ge(loaded, 32)
                dve.tensor_scalar(la[:], la[:], col[:, 0:1], None, ALU.add).then_inc(v, 1)
                dve.wait_ge(v, 1)
                dve.scalar_tensor_tensor(out=e[:], in0=la[:], scalar=-1.0, in1=la[:], op0=ALU.mult, op1=ALU.min)\
                   .then_inc(v, 1)
                dve.wait_ge(a, 4)
                dve.tensor_scalar(be[:], be[:], 1.0, None, ALU.add).then_inc(v, 1)
                dve.scalar_tensor_tensor(out=la[:], in0=la[:], scalar=0.0, in1=e[:], op0=ALU.max, op1=ALU.add).then_inc(v, 1)
                dve.wait_ge(v, 4)
                dve.reciprocal(be[:], be[:]).then_inc(v, 1)
                dve.tensor_scalar(la[:], la[:], col[:, 1:2], -1.0, ALU.mult, ALU.mult).then_inc(v, 3)


def short_conv(E, w, q, k, vc):
    nc, d, sem = E.nc, E.d, E.sem
    tiles = 16
    cols = 256
    with ExitStack() as c:
        sb = lambda n, s: c.enter_context(nc.sbuf_tensor(n, s, FP))
        ring, x, y = sb("conv_ring", [P, 2, KT, cols]), sb("conv_x", [P, 2, TT + 3]), sb("conv_y", [P, 2, TT + 1])
        loaded = [sem(f"conv_w_loaded{i}") for i in range(2)]
        zeroed, full, padded, v, out = (sem(f"conv_{n}") for n in ("zeroed", "full", "padded", "dve", "out"))
        cw = VEC_AT["gdn_conv_w_2"]
        with nc.Block() as block:
            @block.sync
            def _(sp):
                for g in range(tiles // 2):
                    if g >= 2:
                        sp.wait_ge(full, 2 * (g - 1))
                    sp.dma_start(ring[:, g % 2], kn(w[:, g * cols:(g + 1) * cols])).then_inc(loaded[g % 2], 16)

            @block.tensor
            def _(pe):
                for n in range(tiles):
                    g = n // 2
                    if n % 2 == 0:
                        pe.wait_ge(loaded[g % 2], 16 * (g // 2 + 1))
                    if n >= 4:
                        pe.wait_ge(padded, n - 3)
                    for half, (a, b) in enumerate(((0, S), (S, TT)) if n >= 4 else ((0, S),)):
                        for kk in range(KT):
                            last = pe.matmul(E.bank(2 * (n % 4) + half, b - a), ring[:, g % 2, kk, (n % 2) * P:(n % 2 + 1) * P],
                                             E.aT[:, kk, a:b], start=(kk == 0), stop=(kk == KT - 1))
                    last.then_inc(full, 1)

            @block.scalar
            def _(act):
                act.wait_ge(zeroed, 1)
                for n in range(tiles + 1):
                    if n < tiles:
                        act.wait_ge(full, n + 1)
                        if n >= 2:
                            act.wait_ge(v, 3 * (n - 1))
                        last = act.activation(x[:, n % 2, 1:S + 1], E.bank(2 * (n % 4)), ACT.Copy)
                        if n >= 4:
                            last = act.activation(x[:, n % 2, S + 2:TT + 2], E.bank(2 * (n % 4) + 1, CTX), ACT.Copy)
                        last.then_inc(padded, 1)
                    if n >= 1:
                        m = n - 1
                        act.wait_ge(v, 3 * m + 3)
                        lat, ctx_ = y[:, m % 2, 0:S], y[:, m % 2, S + 1:TT + 1]
                        if m < 4:
                            last = act.activation(q[:, m, :], lat, ACT.Silu)
                        elif m < 8:
                            act.activation(k[:, m - 4, 0:S], lat, ACT.Silu)
                            last = act.activation(k[:, m - 4, S:TT], ctx_, ACT.Silu)
                        else:
                            h = m - 8
                            act.activation(vc[:, h // 2, 0:8, h % 2, :], lat.rearrange("p (c t) -> p c t", t=64), ACT.Silu)
                            last = act.activation(vc[:, h // 2, 8:12, h % 2, :], ctx_.rearrange("p (c t) -> p c t", t=64),
                                                  ACT.Silu)
                        last.then_inc(out, 1)

            @block.gpsimd
            def _(pool):
                pool.memset(x[:], 0.0).then_inc(zeroed, 1)

            @block.vector
            def _(dve):
                for n in range(tiles):
                    dve.wait_ge(padded, n + 1)
                    if n >= 2:
                        dve.wait_ge(out, n - 1)
                    L = TT + 1 if n >= 4 else S
                    xs, ys = x[:, n % 2], y[:, n % 2, 0:L]
                    tap = lambda j: E.vcol[:, cw + 16 * j + n:cw + 16 * j + n + 1]
                    dve.tensor_scalar(ys, xs[:, 1:L + 1], tap(1), None, ALU.mult).then_inc(v, 1)
                    dve.wait_ge(v, 3 * n + 1)
                    dve.scalar_tensor_tensor(out=ys, in0=xs[:, 0:L], scalar=tap(0), in1=ys, op0=ALU.mult, op1=ALU.add)\
                       .then_inc(v, 1)
                    dve.wait_ge(v, 3 * n + 2)
                    dve.scalar_tensor_tensor(out=ys, in0=xs[:, 2:L + 2], scalar=tap(2), in1=ys, op0=ALU.mult, op1=ALU.add)\
                       .then_inc(v, 1)


def l2_blocks(E, G, q, k):
    nc, sem = E.nc, E.sem
    items = [("k", p) for p in range(4)] + [("q", p) for p in range(4)]
    zeroed, squared, summed, rooted, used = (sem(f"l2_{x}") for x in ("zeroed", "squared", "summed", "rooted", "used"))
    with ExitStack() as c:
        sb = lambda n, s: c.enter_context(nc.sbuf_tensor(n, s, FP))
        sq, rstd = sb("l2_sq", [P, 2, TT]), sb("l2_rstd", [P, 4, TT])
        with nc.Block() as block:
            @block.gpsimd
            def _(pool):
                pool.memset(G.KT[:], 0.0)
                pool.memset(G.QT[:], 0.0).then_inc(zeroed, 1)
            @block.scalar
            def _(act):
                for rnd, (x, T, scale) in enumerate(((k, TT, 1.0), (q, S, 64.0))):
                    for p in range(4):
                        n = 4 * rnd + p
                        if n >= 2:
                            act.wait_ge(summed, n - 1)
                        act.activation(sq[:, n % 2, 0:T], x[:, p, 0:T], ACT.Square).then_inc(squared, 1)
                    act.wait_ge(summed, 4 * rnd + 4)
                    for p in range(4):
                        if rnd == 1:
                            act.wait_ge(used, 2 * p + 2)
                        act.activation(rstd[:, p, 0:T], E.ps[:, 2 * p * BANK:2 * p * BANK + T], ACT.Ln, scale=scale,
                                       bias=scale * EPS).then_inc(rooted, 1)
                    act.wait_ge(rooted, 8 * rnd + 4)
                    for p in range(4):
                        act.activation(rstd[:, p, 0:T], rstd[:, p, 0:T], ACT.Exp, scale=-0.5).then_inc(rooted, 1)

            @block.tensor
            def _(pe):
                for rnd, T in enumerate((TT, S)):
                    if rnd == 1:
                        pe.wait_ge(rooted, 4)
                    for p in range(4):
                        n = 4 * rnd + p
                        pe.wait_ge(squared, n + 1)
                        for a, b in ((0, S), (S, TT))[:2 if T == TT else 1]:
                            last = pe.matmul(E.ps[:, 2 * p * BANK + a:2 * p * BANK + b], E.blk64, sq[:, n % 2, a:b],
                                             start=True, stop=True)
                        last.then_inc(summed, 1)

            @block.vector
            def _(dve):
                dve.wait_ge(zeroed, 1)
                for rnd, (x, dst, nch) in enumerate(((k, G.KT, NCH), (q, G.QT, 8))):
                    for p in range(4):
                        dve.wait_ge(rooted, 8 * rnd + 5 + p)
                        for h2 in range(2):
                            lo = 64 * h2
                            ch = lambda t: t.rearrange("a (c t) -> a c t", t=64)
                            dve.tensor_tensor(dst[lo:lo + 64, :, p, lo:lo + 64], ch(x[lo:lo + 64, p, :]),
                                              ch(rstd[lo:lo + 64, p, 0:nch * 64]), ALU.mult).then_inc(used, 1)


def chunk_scalars(E, G, ab_dram):
    nc, sem = E.nc, E.sem
    with ExitStack() as c:
        sb = lambda n, s: c.enter_context(nc.sbuf_tensor(n, s, FP))
        rows, U, G.EG = sb("gdn_rows", [96, 2, P]), sb("gdn_U0", [P, 2, P]), sb("gdn_EG", [P, 96])
        loaded, turned, copied, cum, v, a = (sem(f"sc_{x}") for x in ("loaded", "turned", "copied", "cum", "dve", "act"))
        f = lambda x: x[:].rearrange("a z p c -> a (z p c)")
        with nc.Block() as block:
            @block.sync
            def _(sp):
                for i in range(2):
                    for zp in range(8):
                        sp.dma_start(rows[12 * zp:12 * zp + 12, i, :].rearrange("c (h t) -> c h t", h=2),
                                     ab_dram[i, 2 * zp:2 * zp + 2, :].rearrange("h (c t) -> c h t", t=64)).then_inc(loaded, 16)
                sp.dma_start(U[:, 0, :], E.cst("fwd64")).then_inc(loaded, 16)
                sp.dma_start(U[:, 1, :], E.cst("bwd64")).then_inc(loaded, 16)

            @block.tensor
            def _(pe):
                pe.wait_ge(loaded, 18 * 16)
                for i in range(2):
                    last = pe.transpose(E.bank(i, 96), rows[:, i, :], E.ident[0:96, 0:96])
                last.then_inc(turned, 1)
                pe.wait_ge(copied, 1)
                for z in range(2):
                    pe.matmul(E.bank(2, 96)[:, 48 * z:48 * z + 48], U[:, z, :], f(G.LA)[:, 48 * z:48 * z + 48],
                              start=True, stop=True)
                pe.matmul(E.bank(3, 96), E.blk64, f(G.LA), start=True, stop=True).then_inc(cum, 1)

            @block.vector
            def _(dve):
                dve.wait_ge(turned, 1)
                dve.tensor_copy(f(G.LA), E.bank(0, 96))
                dve.tensor_copy(f(G.BE), E.bank(1, 96)).then_inc(copied, 1)
                dve.wait_ge(cum, 1)
                dve.tensor_copy(f(G.GC), E.bank(2, 96)).then_inc(v, 1)
                dve.wait_ge(v, 1)
                dve.tensor_tensor(f(G.EGL), E.bank(3, 96), f(G.GC), ALU.subtract).then_inc(v, 1)
                dve.wait_ge(a, 3)
                dve.tensor_tensor(f(G.BEG), f(G.BE), G.EG[:], ALU.mult)

            @block.scalar
            def _(act):
                act.wait_ge(v, 2)
                act.activation(f(G.GE), E.bank(3, 96), ACT.Exp).then_inc(a, 1)
                act.activation(f(G.EGL), f(G.EGL), ACT.Exp).then_inc(a, 1)
                act.activation(G.EG[:], f(G.GC), ACT.Exp).then_inc(a, 1)


LEVELS = 6
STEPS = NCH


def chunk_at(z, s):
    return (s + 8 if s < 4 else s - 4) if z == 0 else 11 - s


def steps_of(lat):
    up = [f"{x}{l}" for l in range(1, LEVELS) for x in ("M", "X", "T")][:-1]
    return {
        "pe": ["Gj", "KK"] + (["KQ"] if lat else []) + ["T0"] + up + ["U", "W", "WS"] + (["OS"] if lat else []) + ["DS"] +
              (["O"] if lat else []),
        "act": ["D"] + (["DT", "E"] if lat else []) + [f"{x}{l}" for l in range(1, LEVELS) for x in ("M", "T")][:-1] + ["u", "w"],
        "dve": ["t1", "t2"] + (["t3"] if lat else []) + ["N"] + (["qk"] if lat else []) + [f"T{l}" for l in range(LEVELS)] +
               ["vn", "S"] + (["O"] if lat else []),
        "pool": ["LU", "ke", "Vb", "Kb", "Dbeta"] + (["DTmask", "qd"] if lat else []) + ["N0", "I0"] +
                [f"N{l}" for l in range(1, LEVELS)],
    }


def delta(E, G, O):
    nc, sem = E.nc, E.sem
    sems = {e: [sem(f"delta_{e}{z}_done") for z in range(2)] for e in ("pe", "act", "dve", "pool")}

    def done(e, s, label):
        before = sum(len(steps_of(t >= 4)[e]) for t in range(s))
        return before + steps_of(s >= 4)[e].index(label) + 1

    with ExitStack() as c:
        sb = lambda n, s: c.enter_context(nc.sbuf_tensor(n, s, FP))
        U, lev = sb("gdn_U", [P, 2, P]), sb("gdn_levels", [P, LEVELS, 2, P])
        Z = []
        for z in range(2):
            B = Parts()
            (B.LU, B.t1, B.D, B.DT, B.Na, B.Nb, B.T, B.Tt, B.M, B.Vb, B.Kb, B.ke, B.vn, B.S) = (
                sb(f"gdn{z}_{n}", [P, 4, P]) for n in (
                    "LU", "t1", "D", "DT", "Na", "Nb", "T", "Tt", "M", "Vb", "Kb", "ke", "vn", "S"))
            Z.append(B)
            Z[z].Nl = (Z[z].Na, Z[z].Nb)
        cst_in, ready = sem("delta_cst"), sem("delta_ready")
        bank = lambda z, b: E.bank(4 * z + b).rearrange("a (p n) -> a p n", p=4)
        ident4 = E.ident.unsqueeze(1).to_broadcast([P, 4, P])
        mask4 = lambda m: m.unsqueeze(1).to_broadcast([P, 4, P])
        col4 = lambda x, z, ch: x[:, z, :, ch:ch + 1].to_broadcast([P, 4, P])

        def wait(eng, e, z, s, label):
            if s >= 0:
                eng.wait_ge(sems[e][z], done(e, s, label))

        with nc.Block() as block:
            @block.sync
            def _(sp):
                sp.dma_start(U[:, 0, :], E.cst("fwd64")).then_inc(cst_in, 16)
                sp.dma_start(U[:, 1, :], E.cst("bwd64")).then_inc(cst_in, 16)
                sp.dma_start(lev[:].rearrange("a l z n -> a (l z n)"), E.cst("levels")).then_inc(cst_in, 16)

            @block.tensor
            def _(pe):
                def each(z, b, lhsT, rhs, start=True, stop=True):
                    for p in range(4):
                        last = pe.matmul(bank(z, b)[:, p, :], lhsT(p), rhs(p), start=start, stop=stop, skip_group_check=True)
                    return last
                pe.wait_ge(ready, 1)
                for s in range(STEPS):
                    lat = s >= 4
                    for label in steps_of(lat)["pe"]:
                        for z in range(2):
                            B, ch = Z[z], chunk_at(z, s)
                            w = lambda e, l, t=s: wait(pe, e, z, t, l)
                            if label == "Gj":
                                w("pool", "LU")
                                w("dve", "t1", s - 1)
                                if s > 4:
                                    w("dve", "qk", s - 1)
                                last = pe.matmul(E.bank(4 * z), E.ones, B.LU[:].rearrange("a p n -> a (p n)"),
                                                 start=True, stop=True)
                            elif label == "KK":
                                w("act", "u", s - 1)
                                if s > 4:
                                    w("dve", "O", s - 1)
                                last = each(z, 1, lambda p: G.KT[:, ch, p, :], lambda p: G.KT[:, ch, p, :])
                            elif label == "KQ":
                                w("dve", "t1")
                                w("act", "E")
                                last = each(z, 0, lambda p: G.KT[:, ch, p, :], lambda p: G.QT[:, ch, p, :])
                            elif label == "T0":
                                w("pool", "N0")
                                w("dve", "vn", s - 1)
                                for p in range(4):
                                    last = pe.transpose(bank(z, 2)[:, p, :], B.Nl[0][:, p, :], E.ident)
                            elif label[0] == "M":
                                l = int(label[1])
                                w("pool", f"N{l}")
                                w("dve", f"T{l - 1}")
                                if l > 1:
                                    w("act", f"T{l - 1}")
                                last = each(z, 2, lambda p: B.Nl[l % 2][:, p, :], lambda p: B.Tt[:, p, :])
                            elif label[0] == "X":
                                l = int(label[1])
                                w("act", f"M{l}")
                                w("pool", "I0")
                                if l == 1:
                                    w("dve", "S", s - 1)
                                last = each(z, 3, lambda p: B.T[:, p, :], lambda p: B.M[:, p, :])
                            elif label[0] == "T":
                                w("dve", label)
                                for p in range(4):
                                    last = pe.transpose(bank(z, 2)[:, p, :], B.Tt[:, p, :], E.ident)
                            elif label == "U":
                                w("dve", "T5")
                                w("pool", "Kb")
                                last = each(z, 1, lambda p: B.Tt[:, p, :], lambda p: B.Vb[:, p, :])
                            elif label == "W":
                                last = each(z, 3, lambda p: B.Kb[:, p, :], lambda p: B.Tt[:, p, :])
                            elif label == "WS":
                                w("act", "w")
                                w("dve", "S", s - 1)
                                last = each(z, 2, lambda p: B.Kb[:, p, :], lambda p: B.S[:, p, :])
                            elif label == "OS":
                                w("pool", "qd")
                                for p in range(4):
                                    last = pe.matmul(bank(z, 1)[:, p, :], B.S[:, p, :], B.LU[:, p, :], start=(p == 0),
                                                     stop=False, skip_group_check=True)
                            elif label == "DS":
                                w("dve", "vn")
                                last = each(z, 3, lambda p: B.ke[:, p, :], lambda p: B.vn[:, p, :])
                            elif label == "O":
                                last = each(z, 1, lambda p: B.vn[:, p, :], lambda p: B.DT[:, p, :], start=False)
                            last.then_inc(sems["pe"][z], 1)

            @block.scalar
            def _(act):
                for s in range(STEPS):
                    lat = s >= 4
                    for label in steps_of(lat)["act"]:
                        for z in range(2):
                            B, ch = Z[z], chunk_at(z, s)
                            w = lambda e, l, t=s: wait(act, e, z, t, l)
                            if label == "D":
                                w("dve", "t2")
                                last = act.activation(B.D[:], B.D[:], ACT.Exp, scale=-1.0)
                            elif label == "DT":
                                w("dve", "t3")
                                last = act.activation(B.DT[:], B.DT[:], ACT.Exp)
                            elif label == "E":
                                w("pe", "Gj")
                                last = act.activation(B.t1[:], bank(z, 0), ACT.Exp)
                            elif label[0] == "M":
                                w("pe", label)
                                if label == "M1":
                                    w("pe", "X5", s - 1)
                                last = act.activation(B.M[:], bank(z, 2), ACT.Copy)
                            elif label[0] == "T":
                                w("pe", label)
                                last = act.activation(B.T[:], bank(z, 2), ACT.Copy)
                            elif label == "u":
                                w("pe", "U")
                                last = act.activation(B.Vb[:], bank(z, 1), ACT.Copy)
                            elif label == "w":
                                w("pe", "W")
                                last = act.activation(B.Kb[:], bank(z, 3), ACT.Copy)
                            last.then_inc(sems["act"][z], 1)

            @block.vector
            def _(dve):
                for z in range(2):
                    dve.memset(Z[z].S[:], 0.0)
                dve.memset(O[:], 0.0).then_inc(ready, 1)
                dve.wait_ge(ready, 1)
                for s in range(STEPS):
                    lat = s >= 4
                    for label in steps_of(lat)["dve"]:
                        for z in range(2):
                            B, ch = Z[z], chunk_at(z, s)
                            w = lambda e, l, t=s: wait(dve, e, z, t, l)
                            if label == "t1":
                                w("pe", "Gj")
                                if s > 4:
                                    w("pool", "qd", s - 1)
                                last = dve.tensor_tensor(B.t1[:], bank(z, 0), col4(G.GC, z, ch), ALU.subtract)
                            elif label == "t2":
                                w("dve", "t1")
                                w("pool", "N5", s - 1)
                                last = dve.tensor_scalar(B.D[:], B.t1[:], 0.0, None, ALU.max)
                            elif label == "t3":
                                if s > 4:
                                    w("pe", "O", s - 1)
                                last = dve.tensor_scalar(B.DT[:], B.t1[:], 0.0, None, ALU.min)
                            elif label == "N":
                                w("pool", "Dbeta")
                                w("pe", "KK")
                                last = dve.tensor_tensor(B.D[:], B.D[:], bank(z, 1), ALU.mult)
                            elif label == "qk":
                                w("pool", "DTmask")
                                w("pe", "KQ")
                                last = dve.tensor_tensor(B.DT[:], B.DT[:], bank(z, 0), ALU.mult)
                            elif label == "T0":
                                w("pe", "T0")
                                w("pe", "W", s - 1)
                                last = dve.tensor_tensor(B.Tt[:], ident4, bank(z, 2), ALU.subtract)
                            elif label[0] == "T":
                                w("pe", "X" + label[1])
                                w("dve", f"T{int(label[1]) - 1}")
                                last = dve.tensor_tensor(B.Tt[:], B.Tt[:], bank(z, 3), ALU.subtract)
                            elif label == "vn":
                                w("pe", "WS")
                                w("act", "u")
                                w("pe", "O" if s > 4 else "DS", s - 1)
                                last = dve.tensor_tensor(B.vn[:], B.Vb[:], bank(z, 2), ALU.subtract)
                            elif label == "S":
                                w("pe", "DS")
                                w("dve", "S", s - 1)
                                for p in range(4):
                                    last = dve.scalar_tensor_tensor(out=B.S[:, p, :], in0=B.S[:, p, :],
                                                                    scalar=G.GE[:, z, p, ch:ch + 1], in1=bank(z, 3)[:, p, :],
                                                                    op0=ALU.mult, op1=ALU.add)
                            elif label == "O":
                                w("pe", "O")
                                if z == 1:
                                    wait(dve, "dve", 0, s, "O")
                                elif s > 4:
                                    wait(dve, "dve", 1, s - 1, "O")
                                o = O[:, :, 64 * ch:64 * ch + 64]
                                last = dve.tensor_tensor(o, o, E.bank(4 * z + 1).rearrange("a (h t) -> a h t", t=64), ALU.add)
                            last.then_inc(sems["dve"][z], 1)

            @block.gpsimd
            def _(pool):
                pool.wait_ge(cst_in, 48)
                for s in range(STEPS):
                    lat = s >= 4
                    for label in steps_of(lat)["pool"]:
                        for z in range(2):
                            B, ch = Z[z], chunk_at(z, s)
                            w = lambda e, l, t=s: wait(pool, e, z, t, l)
                            tt = lambda out, a, b: pool.tensor_tensor(out, a, b, ALU.mult)
                            if label == "LU":
                                w("pe", "O" if s > 4 else "Gj", s - 1)
                                last = tt(B.LU[:], mask4(U[:, z, :]), col4(G.LA, z, ch))
                            elif label == "ke":
                                w("pe", "DS", s - 1)
                                last = tt(B.ke[:], G.K[:, ch], col4(G.EGL, z, ch))
                            elif label == "Vb":
                                w("dve", "vn", s - 1)
                                last = tt(B.Vb[:], G.V[:, ch], col4(G.BE, z, ch))
                            elif label == "Kb":
                                w("pe", "WS", s - 1)
                                last = tt(B.Kb[:], G.K[:, ch], col4(G.BEG, z, ch))
                            elif label == "Dbeta":
                                w("act", "D")
                                last = tt(B.D[:], B.D[:], col4(G.BE, z, ch))
                            elif label == "DTmask":
                                w("act", "DT")
                                last = tt(B.DT[:], B.DT[:], mask4(U[:, z, :]))
                            elif label == "qd":
                                w("act", "E")
                                w("pe", "Gj")
                                last = tt(B.LU[:], G.QT[:, ch], B.t1[:])
                            elif label == "I0":
                                w("pool", "N0")
                                w("pe", "X5", s - 1)
                                last = pool.tensor_tensor(B.T[:], ident4, B.Nl[0][:], ALU.subtract)
                            else:
                                l = int(label[1])
                                w("dve", "N")
                                if l == 0:
                                    w("pe", "M4", s - 1)
                                elif l == 1:
                                    w("pe", "M5", s - 1)
                                elif l == 2:
                                    w("pe", "T0")
                                    w("pool", "I0")
                                else:
                                    w("pe", f"M{l - 2}")
                                last = tt(B.Nl[l % 2][:], B.D[:], mask4(lev[:, l, 1 - z, :]))
                            last.then_inc(sems["pool"][z], 1)


def build_program(nc, d, out):
    with ExitStack() as ctx:
        E = setup(nc, ctx, d)
        with nc.sbuf_tensor("ctx_rows", [P, 2, D], FP) as cr:
            load(E, "ctx", [(cr[:], d["ctx_2"][0].rearrange("(t p) n -> p t n", p=P))])
            turn(E, "cturn", [([cr[:, t, k * P:(k + 1) * P] for t in range(2)], E.hT[:, k, S:TT]) for k in range(KT)])
        for part in (lambda: attention_and_hgrn(E), lambda: moe(E), lambda: modulation(E), lambda: even_mixer(E),
                     lambda: mlp(E, 0, TT), lambda: odd_mixer(E), lambda: mlp(E, 1, S), lambda: put_out(E, out)):
            with nc.cleanup_on_exit():
                part()


def put_out(E, out):
    nc = E.nc
    norm(E, "last_norm", E.hT, E.aT, KT, D, S, lambda k, s: E.v("final_norm_2", k))
    with nc.sbuf_tensor("out_rows", [P, 4, D], FP) as rows:
        turn(E, "out_turn", [([E.aT[:, k, t * P:(t + 1) * P] for k in ks], rows[:, t, ks[0] * P:(ks[-1] + 1) * P])
                             for t in range(4) for ks in ((0, 1, 2, 3), (4, 5, 6, 7))])
        stored = E.sem("out_stored")
        with nc.Block() as block:
            @block.sync
            def _(sp):
                sp.dma_start(out[0].rearrange("(t p) n -> p t n", p=P), rows[:]).then_inc(stored, 16)
                sp.wait_ge(stored, 16)


WHOLE = ["x", "w_in", "w_out", "w_group", "b_group", "w_router", "b_router", "w_gate", "w_up", "w_down", "ctx_2",
         "ada_w_2", "mlp_w1_2", "mlp_w2_2", "even_w_in_2", "mla_w_uq_2", "mla_w_ukv_2", "gla_gate_up_2",
         "even_w_out_2", "gdn_w_in_2", "gdn_a_log_2", "gdn_dt_bias_2", "gdn_w_out_2"]


def kernel(**inputs):
    import numpy as _np
    import concourse.bacc as _bacc
    from concourse import mybir as _mybir
    from concourse.bass_utils import run_bass_kernel_spmd as _run

    nc = _bacc.Bacc("TRN2", target_bir_lowering=False, num_devices=1)
    host = {name: _np.ascontiguousarray(inputs[name]) for name in WHOLE}
    host["vec"] = _np.concatenate([_np.asarray(inputs[name]).reshape(-1, P) for name, _ in VEC_ROWS])
    host["cst"] = constants()
    arrays, d = {}, {}
    for name, a in host.items():
        arrays[f"in_{name}_dram"] = a
        d[name] = nc.dram_tensor(f"in_{name}_dram", a.shape, _mybir.dt.from_np(a.dtype), kind="ExternalInput").ap()
    out = nc.dram_tensor("out_0_dram", (1, S, D), FP, kind="ExternalOutput").ap()
    build_program(nc, d, out)
    r = _run(nc, [arrays], core_ids=[0])
    return r.results[0]["out_0_dram"]
```

```python
from contextlib import ExitStack

import numpy as np
import concourse.bass as bass
from concourse import mybir

class Parts:
    pass


P = 128
D = 1024
KT = D // P
S = 512
CTX = 256
TT = S + CTX
BANK = 512
EPS = 1e-6
HEADS = 8
FP = mybir.dt.float32
ACT = mybir.ActivationFunctionType
ALU = mybir.AluOpType
AX = mybir.AxisListType

VEC_ROWS = [("norm1_g", 8), ("attn_norm_g", 4), ("hgrn_gamma", 8), ("hgrn_norm_g", 4), ("norm2_g", 8),
            ("norm_f_g", 8), ("norm1_w_2", 16), ("norm2_w_2", 16), ("mla_q_norm_2", 3), ("mla_kv_norm_2", 2),
            ("gla_gate_bias_2", 4), ("gla_o_norm_2", 1), ("gdn_o_norm_2", 1), ("final_norm_2", 8), ("c_2", 8),
            ("c_ctx_2", 8), ("ada_b_2", 96), ("gdn_conv_w_2", 48)]
VEC_AT = {}
_at = 0
for _name, _rows in VEC_ROWS:
    VEC_AT[_name] = _at
    _at += _rows
N_VEC = _at

CST = [("ident", 128), ("ones", 128), ("blk64", 128), ("fold", 2), ("hg_mask", 128), ("fwd64", 128), ("bwd64", 128),
       ("dist", 512), ("mult", 512), ("reset32", 512), ("reset64", 768), ("cos", 768), ("sin", 768),
       ("rot", 32), ("levels", 6 * 2 * 128), ("iota", 32), ("iota64", 64), ("before", 128)]
CST_AT = {}
_at = 0
for _name, _w in CST:
    CST_AT[_name] = (_at, _w)
    _at += _w
N_CST = _at


def constants():
    c = {}
    i = np.arange(P)
    c["ident"] = np.eye(P)
    c["ones"] = np.ones((P, P))
    same = lambda n: (i[:, None] // n) == (i[None, :] // n)
    c["blk64"] = same(64)
    c["fold"] = (i[:, None] % 32) == np.arange(2)[None, :]
    c["hg_mask"] = same(32) & (i[:, None] <= i[None, :])
    c["fwd64"] = same(64) & (i[:, None] <= i[None, :])
    c["bwd64"] = same(64) & (i[:, None] >= i[None, :])
    dist = 384 + i[:, None] - np.arange(512)[None, :]
    mult = ((dist >= 0) & (dist <= 128)) * 1.0 + ((dist >= 0) & (dist % 4 == 0)) + ((dist >= 0) & (dist % 16 == 0))
    c["dist"] = np.where(mult > 0, dist, 1e32)
    c["mult"] = mult
    c["reset32"] = np.broadcast_to(np.arange(512) % 32 != 0, (P, 512))
    c["reset64"] = np.broadcast_to(np.arange(768) % 64 != 0, (P, 768))
    t = np.arange(S)
    inv = 10000.0 ** (-np.arange(0, 16, 2, dtype=np.float32) / np.float32(16))
    row, col = (t // 64).astype(np.float32), (t % 64).astype(np.float32)
    ang = np.stack([row[None, :] * inv[:, None].astype(np.float32), col[None, :] * inv[:, None].astype(np.float32)])
    cos, sin = np.ones((P, TT)), np.zeros((P, TT))
    rot = np.zeros((P, 32))
    for axis in range(2):
        for half in range(2):
            for f in range(8):
                r = 16 * axis + 8 * half + f
                cos[64 + r, :S] = np.cos(ang[axis, f])
                sin[64 + r, :S] = np.sin(ang[axis, f])
                rot[64 + (r + 8 if half == 0 else r - 8), r] = -1.0 if half == 0 else 1.0
    c["cos"], c["sin"], c["rot"] = cos, sin, rot
    lv = []
    for b in (1, 2, 4, 8, 16, 32):
        pair = ((i[:, None] // (2 * b)) == (i[None, :] // (2 * b))) & ((i[:, None] // b) != (i[None, :] // b))
        lv += [pair & (i[:, None] < i[None, :]), pair & (i[:, None] > i[None, :])]
    c["levels"] = np.concatenate(lv, axis=1)
    c["iota"] = np.broadcast_to(np.arange(32) % 8, (P, 32))
    c["iota64"] = np.broadcast_to(np.arange(64), (P, 64))
    c["before"] = i[:, None] < i[None, :]
    return np.concatenate([np.asarray(c[n], np.float32) for n, _ in CST], axis=1).astype(np.float32)


def setup(nc, ctx, d):
    E = Parts()
    E.nc, E.d = nc, d
    E.ps = ctx.enter_context(nc.psum_tensor("ps", [P, 8 * BANK], FP))
    E.bank = lambda b, w=BANK, p=P: E.ps[0:p, b * BANK:b * BANK + w]
    E.hT = ctx.enter_context(nc.sbuf_tensor("hT", [P, KT, TT], FP))
    E.aT = ctx.enter_context(nc.sbuf_tensor("aT", [P, KT, TT], FP))
    E.vcol = ctx.enter_context(nc.sbuf_tensor("vcol", [P, 256], FP))
    E.base = ctx.enter_context(nc.sbuf_tensor("base", [P, 3 * P + 2], FP))
    E.ident, E.ones, E.blk64 = (E.base[:, i * P:(i + 1) * P] for i in range(3))
    E.fold = E.base[:, 3 * P:3 * P + 2]
    E.mod = ctx.enter_context(nc.sbuf_tensor("mod", [P, 2, 6 * KT, 2], FP))
    E.nw = ctx.enter_context(nc.sbuf_tensor("norm_weights", [P, 2, 2, KT, 2], FP))
    E.v = lambda name, i: E.vcol[:, VEC_AT[name] + i:VEC_AT[name] + i + 1]

    def sem(name):
        return nc.alloc_semaphore(name=name)
    E.sem = sem
    E.cst = lambda name: d["cst"][:, CST_AT[name][0]:CST_AT[name][0] + CST_AT[name][1]]
    loaded, turned, copied = sem("vec_loaded"), sem("vec_turned"), sem("vec_copied")
    rows = (P, N_VEC - P)
    with nc.sbuf_tensor("vec_rows", [P, 2, P], FP) as vrow, nc.Block() as block:
        @block.sync
        def _(sp):
            sp.dma_start(E.base[:], d["cst"][:, 0:3 * P + 2]).then_inc(loaded, 16)
            for i in range(2):
                sp.dma_start(vrow[0:rows[i], i, :], d["vec"][i * P:i * P + rows[i], :]).then_inc(loaded, 16)

        @block.tensor
        def _(pe):
            pe.wait_ge(loaded, 48)
            for i in range(2):
                last = pe.transpose(E.bank(0, P)[:, 0:rows[i]] if i == 0 else E.bank(1, P)[:, 0:rows[i]],
                                    vrow[0:rows[i], i, :], E.ident[0:rows[i], 0:rows[i]])
            last.then_inc(turned, 1)

        @block.vector
        def _(dve):
            dve.wait_ge(turned, 1)
            for i in range(2):
                dve.tensor_copy(E.vcol[:, i * P:i * P + rows[i]], E.bank(i, rows[i])).then_inc(copied, 1)
    return E


def ring_of(E, c, name, ws, slots=2):
    G = Parts()
    width = max(w.shape[1] * w.shape[2] for w in ws)
    G.slots, G.ring = slots, c.enter_context(E.nc.sbuf_tensor(f"{name}_ring", [P, slots, width], FP))
    G.loaded = [E.sem(f"{name}_w_loaded{i}") for i in range(slots)]
    G.tile = lambda j, w: G.ring[:, j % slots, 0:w.shape[1] * w.shape[2]].rearrange("p (k n) -> p k n", k=w.shape[1])
    with E.nc.Block() as block:
        @block.sync
        def _(sp):
            for j, w in enumerate(ws[0:slots]):
                sp.dma_start(G.tile(j, w), w).then_inc(G.loaded[j], 16)
    return G


def gemm(E, name, jobs, banks=8, split=None, ahead=None):
    nc, sem = E.nc, E.sem
    full = sem(f"{name}_bank_full")
    ends, at = [], 0
    for job in jobs:
        at += len(job["units"])
        ends.append(at)
    freed = {"act": sem(f"{name}_act_freed"), "dve": sem(f"{name}_dve_freed")}
    units = [(j, u) for j, job in enumerate(jobs) for u in job["units"]]
    count, freed_at = {"act": 0, "dve": 0}, []
    for _, (_, who, _, _) in units:
        count[who] += 1
        freed_at.append((who, count[who]))
    panels, panel_of = [], []
    for u, (j, (_, _, _, part)) in enumerate(units):
        if split is None or part is None:
            panel_of.append(None)
            continue
        if not panels or panels[-1][0:2] != (j, part[0]):
            panels.append((j, part[0], u + 1))
        panels[-1] = (j, part[0], u + 1)
        panel_of.append(len(panels) - 1)
    with ExitStack() as c:
        G = ahead or ring_of(E, c, name, [job["w"] for job in jobs])
        slots, loaded = G.slots, G.loaded
        if split:
            x, kt, T = split
            xh, xl, wh, wl = (c.enter_context(nc.sbuf_tensor(f"{name}_{n}", shape, mybir.dt.float32r)) for n, shape in (
                ("x_high", [P, kt, T]), ("x_low", [P, kt, T]), ("w_high", [P, 2, kt, P]), ("w_low", [P, 2, kt, P])))
            w_high, w_low, x_high, x_low = (sem(f"{name}_{n}") for n in ("w_high", "w_low", "x_high", "x_low"))
        block = c.enter_context(nc.Block())

        def tile(j):
            return G.tile(j, jobs[j]["w"])

        @block.sync
        def _(sp):
            for j, job in enumerate(jobs):
                if j < slots:
                    continue
                sp.wait_ge(full, ends[j - slots])
                sp.dma_start(tile(j), job["w"]).then_inc(loaded[j % slots], 16)

        @block.tensor
        def _(pe):
            before, panel = -1, -1
            for u, (j, (mms, _, _, part)) in enumerate(units):
                if j != before:
                    pe.wait_ge(loaded[j % slots], 16 * (j // slots + 1))
                before = j
                if u >= banks:
                    who, n = freed_at[u - banks]
                    pe.wait_ge(freed[who], n)
                if panel_of[u] is None:
                    steps = mms(tile(j), u % banks)
                    for i, (out, lhsT, rhs) in enumerate(steps):
                        last = pe.matmul(out, lhsT, rhs, start=(i == 0), stop=(i == len(steps) - 1))
                else:
                    first = panel < 0
                    if panel_of[u] != panel:
                        panel = panel_of[u]
                        pe.wait_ge(w_low, panel + 1)
                    _, t0, t1 = part
                    for k in range(kt):
                        if first:
                            pe.wait_ge(x_low, k + 1)
                        for i, (w, xp) in enumerate(((wh, xh), (wh, xl), (wl, xh))):
                            last = pe.matmul(E.bank(u % banks, t1 - t0), w[:, panel % 2, k, :], xp[:, k, t0:t1],
                                             start=(k == 0 and i == 0), stop=(k == kt - 1 and i == 2))
                last.then_inc(full, 1)

        def part_of_x(eng, me):
            for k in range(kt):
                if me == "act":
                    eng.activation(xh[:, k, :], x[:, k, 0:T], ACT.Copy).then_inc(x_high, 1)
                else:
                    eng.wait_ge(x_high, k + 1)
                    eng.tensor_tensor(xl[:, k, :], x[:, k, 0:T], xh[:, k, :].bitcast(FP), ALU.subtract).then_inc(x_low, 1)

        def part_of_panel(eng, me, p):
            if p >= len(panels):
                return
            j, n0, _ = panels[p]
            w = tile(j)[:, :, n0:n0 + P]
            if me == "act":
                eng.wait_ge(loaded[j % slots], 16 * (j // slots + 1))
                if p >= 2:
                    eng.wait_ge(full, panels[p - 2][2])
                eng.activation(wh[:, p % 2], w, ACT.Copy).then_inc(w_high, 1)
            else:
                eng.wait_ge(w_high, p + 1)
                eng.tensor_tensor(wl[:, p % 2], w, wh[:, p % 2].bitcast(FP), ALU.subtract).then_inc(w_low, 1)

        def evacuate(eng, me):
            if split:
                part_of_panel(eng, me, 0)
                part_of_x(eng, me)
                part_of_panel(eng, me, 1)
            for u, (j, (_, who, ev, _)) in enumerate(units):
                if who == me:
                    eng.wait_ge(full, u + 1)
                    ev(eng, u % banks).then_inc(freed[me], 1)
                p = panel_of[u]
                if p is not None and panels[p][2] == u + 1:
                    part_of_panel(eng, me, p + 2)

        @block.scalar
        def _(act):
            evacuate(act, "act")

        @block.vector
        def _(dve):
            evacuate(dve, "dve")


def kn(w):
    return w.rearrange("(k p) n -> p k n", p=P)


def feature_unit(E, x, n0, m, t0, t1, who, ev, kt=KT):
    def mms(w, b):
        return [(E.bank(b, t1 - t0, m), w[:, k, n0:n0 + m], x[:, k, t0:t1]) for k in range(kt)]
    return (mms, who, lambda eng, b: ev(eng, E.bank(b, t1 - t0, m)), (n0, t0, t1) if m == P else None)


def token_unit(E, x, t0, n, who, ev, kt=KT, pick=None):
    def mms(w, b):
        return [(E.bank(b, n), x[:, k, t0:t0 + P], pick(w, k) if pick else w[:, k, 0:n]) for k in range(kt)]
    return (mms, who, lambda eng, b: ev(eng, E.bank(b, n)), None)


def act_copy(dst, func=ACT.Copy, scale=1.0):
    return lambda eng, ps: eng.activation(dst, ps, func, scale=scale)


def dve_copy(dst):
    return lambda eng, ps: eng.tensor_copy(dst, ps)


def norm(E, name, src, dst, kt, width, T, scale, shift=None, segs=None):
    nc, sem = E.nc, E.sem
    segs = segs or [(0, T)]
    parts = [(0, min(T, BANK))] + ([(BANK, T)] if T > BANK else [])
    squared, summed, rooted, scaled = (sem(f"{name}_{x}") for x in ("squared", "summed", "rooted", "scaled"))
    with nc.sbuf_tensor(f"{name}_sq", [P, 2, T], FP) as sq, nc.sbuf_tensor(f"{name}_rstd", [P, T], FP) as rstd, \
            nc.Block() as block:
        @block.scalar
        def _(act):
            for k in range(kt):
                if k >= 2:
                    act.wait_ge(summed, k - 1)
                act.activation(sq[:, k % 2, :], src[:, k, 0:T], ACT.Square).then_inc(squared, 1)
            act.wait_ge(summed, kt)
            act.activation(rstd[:], E.ps[:, 0:T], ACT.Ln, scale=1.0 / width, bias=EPS).then_inc(rooted, 1)
            act.wait_ge(rooted, 1)
            act.activation(rstd[:], rstd[:], ACT.Exp, scale=-0.5).then_inc(rooted, 1)
            if shift:
                for k in range(kt):
                    act.wait_ge(scaled, (k + 1) * len(segs))
                    for s, (a, b) in enumerate(segs):
                        act.activation(dst[:, k, a:b], dst[:, k, a:b], ACT.Identity, bias=shift(k, s))

        @block.tensor
        def _(pe):
            for k in range(kt):
                pe.wait_ge(squared, k + 1)
                for a, b in parts:
                    last = pe.matmul(E.ps[:, a:b], E.ones, sq[:, k % 2, a:b], start=(k == 0), stop=(k == kt - 1))
                last.then_inc(summed, 1)

        @block.vector
        def _(dve):
            dve.wait_ge(rooted, 2)
            for k in range(kt):
                for s, (a, b) in enumerate(segs):
                    dve.scalar_tensor_tensor(out=dst[:, k, a:b], in0=src[:, k, a:b], scalar=scale(k, s),
                                             in1=rstd[:, a:b], op0=ALU.mult, op1=ALU.mult).then_inc(scaled, 1)


def gated_norm(E, name, o, dst, tiles, T, width, summer, scale, gate, gate_T=None):
    nc, sem = E.nc, E.sem
    squared, summed, rooted, scaled = (sem(f"{name}_{x}") for x in ("squared", "summed", "rooted", "scaled"))
    per = -(-T // BANK)
    parts = [(0, min(T, BANK))] + ([(BANK, T)] if T > BANK else [])
    with nc.sbuf_tensor(f"{name}_sq", [P, 2, T], FP) as sq, nc.sbuf_tensor(f"{name}_rstd", [P, tiles, T], FP) as rstd, \
            nc.Block() as block:
        @block.scalar
        def _(act):
            for k in range(tiles):
                if k >= 2:
                    act.wait_ge(summed, k - 1)
                act.activation(sq[:, k % 2, :], o[:, k, 0:T], ACT.Square).then_inc(squared, 1)
            act.wait_ge(summed, tiles)
            for k in range(tiles):
                act.activation(rstd[:, k, :], E.ps[:, k * per * BANK:k * per * BANK + T], ACT.Ln,
                               scale=1.0 / width, bias=EPS).then_inc(rooted, 1)
            act.wait_ge(rooted, tiles)
            for k in range(tiles):
                act.activation(rstd[:, k, :], rstd[:, k, :], ACT.Exp, scale=-0.5).then_inc(rooted, 1)

        @block.tensor
        def _(pe):
            for k in range(tiles):
                pe.wait_ge(squared, k + 1)
                for a, b in parts:
                    last = pe.matmul(E.ps[:, k * per * BANK + a:k * per * BANK + b], summer, sq[:, k % 2, a:b],
                                     start=True, stop=True)
                last.then_inc(summed, 1)

        @block.vector
        def _(dve):
            for k in range(tiles):
                dve.wait_ge(rooted, tiles + k + 1)
                dve.scalar_tensor_tensor(out=dst[:, k, 0:T], in0=o[:, k, 0:T], scalar=scale(k), in1=rstd[:, k, :],
                                         op0=ALU.mult, op1=ALU.mult).then_inc(scaled, 1)

        @block.gpsimd
        def _(pool):
            for k in range(tiles):
                pool.wait_ge(scaled, k + 1)
                pool.tensor_tensor(dst[:, k, 0:T], dst[:, k, 0:T], gate[:, k, 0:T], ALU.mult)


def turn(E, name, jobs):
    turned, act_out, dve_out = (E.sem(f"{name}_{x}") for x in ("turned", "act_out", "dve_out"))
    with E.nc.Block() as block:
        @block.tensor
        def _(pe):
            for u, (srcs, _) in enumerate(jobs):
                if u >= 8:
                    pe.wait_ge(act_out if u % 2 == 0 else dve_out, (u - 8) // 2 + 1)
                for i, s in enumerate(srcs):
                    last = pe.transpose(E.bank(u % 8)[:, i * P:(i + 1) * P], s, E.ident)
                last.then_inc(turned, 1)

        @block.scalar
        def _(act):
            for u, (srcs, dst) in enumerate(jobs):
                if u % 2 == 0:
                    act.wait_ge(turned, u + 1)
                    act.activation(dst, E.bank(u % 8, len(srcs) * P), ACT.Copy).then_inc(act_out, 1)

        @block.vector
        def _(dve):
            for u, (srcs, dst) in enumerate(jobs):
                if u % 2 == 1:
                    dve.wait_ge(turned, u + 1)
                    dve.tensor_copy(dst, E.bank(u % 8, len(srcs) * P)).then_inc(dve_out, 1)


def load(E, name, pairs, eng="sync"):
    done = E.sem(f"{name}_loaded")
    with E.nc.Block() as block:
        @block.sync
        def _(sp):
            for dst, src in pairs:
                sp.dma_start(dst, src).then_inc(done, 16)
            sp.wait_ge(done, 16 * len(pairs))


def attention_and_hgrn(E):
    nc, d, sem = E.nc, E.d, E.sem
    hT, aT = E.hT, E.aT
    with ExitStack() as c:
        sb = lambda n, s: c.enter_context(nc.sbuf_tensor(n, s, FP))
        qT, kT, V = sb("a_qT", [P, 4, S]), sb("a_kT", [P, 4, S]), sb("a_V", [P, 4, S])
        hq, hf, hi, hg = sb("h_q", [P, 4, S]), sb("h_f", [P, 4, S]), sb("h_i", [P, 4, S]), sb("h_gate", [P, 4, S])
        w = d["w_in"][0]
        ahead = c.enter_context(ExitStack())
        with nc.sbuf_tensor("x_rows", [P, 4, D], FP) as xr:
            load(E, "x", [(xr[:], d["x"][0].rearrange("(t p) n -> p t n", p=P))])
            turn(E, "xturn", [([xr[:, t, k * P:(k + 1) * P] for t in range(4)], hT[:, k, 0:S]) for k in range(KT)])
        ring = ring_of(E, ahead, "proj1", [kn(w[:, g * S:(g + 1) * S]) for g in range(7)])
        norm(E, "n1", hT, aT, KT, D, S, lambda k, s: E.v("norm1_g", k))

        def group(g, kind, dst, ev):
            units = []
            for n in range(4):
                who = "act" if ev else ("act" if n % 2 else "dve")
                e = ev(dst[:, n, :]) if ev else (act_copy(dst[:, n, :]) if n % 2 else dve_copy(dst[:, n, :]))
                units.append(feature_unit(E, aT, n * P, P, 0, S, who, e) if kind == "f"
                             else token_unit(E, aT, n * P, S, who, e))
            return dict(w=kn(w[:, g * S:(g + 1) * S]), units=units)
        silu = lambda dst: act_copy(dst, ACT.Silu)
        gemm(E, "proj1", [group(0, "f", qT, lambda dst: act_copy(dst, scale=0.125)), group(1, "f", kT, None),
                          group(2, "t", V, None), group(3, "f", hq, silu), group(4, "f", hf, None),
                          group(5, "t", hi, None), group(6, "f", hg, silu)], split=(aT, KT, S), ahead=ring)
        ahead.close()
        dilated(E, qT, kT, V)
        hgrn(E, hq, hf, hi, hg)
    resid_gemm(E, "wout1", d["w_out"][0], aT, S, None)


def resid_gemm(E, name, w, x, T, gate):
    segs = [(0, S)] + ([(S, T)] if T > S else [])

    def ev(n, s, a, b):
        def run(dve, ps):
            if gate is None:
                return dve.tensor_tensor(E.hT[:, n, a:b], E.hT[:, n, a:b], ps, ALU.add)
            return dve.scalar_tensor_tensor(out=E.hT[:, n, a:b], in0=ps, scalar=gate(n, s), in1=E.hT[:, n, a:b],
                                            op0=ALU.mult, op1=ALU.add)
        return run
    gemm(E, name, [dict(w=kn(w[:, g * 512:(g + 1) * 512]),
                        units=[feature_unit(E, x, n * P, P, a, b, "dve", ev(4 * g + n, s, a, b))
                               for n in range(4) for s, (a, b) in enumerate(segs)]) for g in range(2)],
         split=(x, KT, T))


def dilated(E, qT, kT, V):
    nc = E.nc
    with ExitStack() as c:
        sb = lambda nm, s: c.enter_context(nc.sbuf_tensor(nm, s, FP))
        O = sb("dil_o", [P, 4, 512])
        dilated_units(E, qT, kT, V, O)
        oT = sb("dil_oT", [P, 4, 512])
        turn(E, "dil_oturn", [([O[:, i, k * P:(k + 1) * P] for i in range(4)], oT[:, k, :]) for k in range(4)])
        norm(E, "dil_norm", oT, E.aT, 4, 512, S, lambda k, s: E.v("attn_norm_g", k))


def dilated_units(E, qT, kT, V, O):
    nc, d, sem = E.nc, E.d, E.sem
    units = [(h, i) for h in range(HEADS) for i in range(4)]
    n = len(units)
    cst_in, scored, biased, maxed, exped, weighted, turned, evac, summed, done = (
        sem(f"dil_{x}") for x in ("cst", "scored", "biased", "maxed", "exped", "weighted", "turned", "evac",
                                  "summed", "done"))
    with ExitStack() as c:
        sb = lambda nm, s: c.enter_context(nc.sbuf_tensor(nm, s, FP))
        dist, mult = sb("dist", [P, 512]), sb("mult", [P, 512])
        sc, pr, pm, pT = (sb(x, [P, 2, 512]) for x in ("dil_sc", "dil_pr", "dil_pm", "dil_pT"))
        neg, tot, inv = (sb(x, [P, n]) for x in ("dil_neg", "dil_tot", "dil_inv"))
        block = c.enter_context(nc.Block())

        @block.sync
        def _(sp):
            sp.dma_start(dist[:], E.cst("dist")).then_inc(cst_in, 16)
            sp.dma_start(mult[:], E.cst("mult")).then_inc(cst_in, 16)

        @block.tensor
        def _(pe):
            for t in range(n + 3):
                if t < n:
                    h, i = units[t]
                    if t >= 2:
                        pe.wait_ge(biased, t - 1)
                    lo = 64 * (h % 2)
                    pe.matmul(E.bank(t % 2, (i + 1) * P), qT[lo:lo + 64, h // 2, i * P:(i + 1) * P],
                              kT[lo:lo + 64, h // 2, 0:(i + 1) * P], start=True, stop=True).then_inc(scored, 1)
                if 2 <= t <= n + 1:
                    u = t - 2
                    h, i = units[u]
                    pe.wait_ge(weighted, u + 1)
                    if u >= 2:
                        pe.wait_ge(evac, u - 1)
                    for j in range(i + 1):
                        last = pe.transpose(E.bank(2 + u % 2)[:, j * P:(j + 1) * P], pm[:, u % 2, j * P:(j + 1) * P],
                                            E.ident)
                    last.then_inc(turned, 1)
                if t >= 3:
                    u = t - 3
                    h, i = units[u]
                    pe.wait_ge(evac, u + 1)
                    if u >= 2:
                        pe.wait_ge(done, u - 1)
                    for j in range(i + 1):
                        last = pe.matmul(E.bank(4 + u % 2, 64), pT[:, u % 2, j * P:(j + 1) * P],
                                         V[:, j, h * 64:(h + 1) * 64], start=(j == 0), stop=(j == i))
                    last.then_inc(summed, 1)

        @block.scalar
        def _(act):
            for t in range(n + 2):
                if t < n:
                    L = (units[t][1] + 1) * P
                    act.wait_ge(maxed, t + 1)
                    if t >= 2:
                        act.wait_ge(weighted, t - 1)
                    act.activation(pr[:, t % 2, 0:L], sc[:, t % 2, 0:L], ACT.Exp, bias=neg[:, t:t + 1]).then_inc(exped, 1)
                if t >= 2:
                    u = t - 2
                    L = (units[u][1] + 1) * P
                    act.wait_ge(turned, u + 1)
                    if u >= 2:
                        act.wait_ge(summed, u - 1)
                    act.activation(pT[:, u % 2, 0:L], E.bank(2 + u % 2, L), ACT.Copy).then_inc(evac, 1)

        @block.vector
        def _(dve):
            dve.wait_ge(cst_in, 32)
            for t in range(n + 4):
                if t < n:
                    h, i = units[t]
                    L, off = (i + 1) * P, (3 - i) * P
                    dve.wait_ge(scored, t + 1)
                    if t >= 2:
                        dve.wait_ge(exped, t - 1)
                    dve.scalar_tensor_tensor(out=sc[:, t % 2, 0:L], in0=dist[:, off:512], scalar=-2.0 ** -(h + 1),
                                             in1=E.bank(t % 2, L), op0=ALU.mult, op1=ALU.add).then_inc(biased, 1)
                    dve.wait_ge(biased, t + 1)
                    dve.tensor_reduce(neg[:, t:t + 1], sc[:, t % 2, 0:L], AX.X, ALU.max, negate=True).then_inc(maxed, 1)
                if 1 <= t <= n:
                    u = t - 1
                    h, i = units[u]
                    L, off = (i + 1) * P, (3 - i) * P
                    dve.wait_ge(exped, u + 1)
                    if u >= 2:
                        dve.wait_ge(turned, u - 1)
                    dve.tensor_tensor_reduce(pm[:, u % 2, 0:L], pr[:, u % 2, 0:L], mult[:, off:512], 1.0, 0.0,
                                             ALU.mult, ALU.add, tot[:, u:u + 1]).then_inc(weighted, 1)
                    dve.wait_ge(weighted, u + 1)
                    dve.reciprocal(inv[:, u:u + 1], tot[:, u:u + 1])
                if t >= 4:
                    u = t - 4
                    h, i = units[u]
                    dve.wait_ge(summed, u + 1)
                    dve.tensor_scalar(O[:, i, h * 64:(h + 1) * 64], E.bank(4 + u % 2, 64), inv[:, u:u + 1], None,
                                      ALU.mult).then_inc(done, 1)


def hgrn(E, hq, hf, hi, gate):
    nc, d, sem = E.nc, E.d, E.sem
    C, NC = 32, S // 32
    pt = [P, 4, S]
    with ExitStack() as c:
        sb = lambda nm, s: c.enter_context(nc.sbuf_tensor(nm, s, FP))
        reset, mask, lb, omlb, dec = sb("hg_reset", [P, S]), sb("hg_mask", [P, P]), sb("hg_lb", [P, 4]), \
            sb("hg_omlb", [P, 4]), sb("hg_dec", [P, 4, NC])
        key, b, e1, k_in, k_end = sb("hg_key", pt), sb("hg_b", pt), sb("hg_e", pt), sb("hg_k_in", pt), sb("hg_k_end", pt)
        cst_in, a, v = sem("hg_cst"), sem("hg_act"), sem("hg_dve")
        with nc.Block() as block:
            @block.sync
            def _(sp):
                sp.dma_start(reset[:], E.cst("reset32")).then_inc(cst_in, 16)
                sp.dma_start(mask[:], E.cst("hg_mask")).then_inc(cst_in, 16)

            @block.scalar
            def _(act):
                act.activation(e1[:], hf[:], ACT.Sigmoid).then_inc(a, 1)
                act.activation(key[:], hf[:], ACT.Sigmoid, scale=-1.0).then_inc(a, 1)
                act.wait_ge(v, 1)
                act.activation(lb[:], lb[:], ACT.Exp).then_inc(a, 1)
                act.wait_ge(v, 5)
                act.activation(e1[:], e1[:], ACT.Ln).then_inc(a, 1)
                act.wait_ge(v, 11)
                act.activation(k_in[:], b[:], ACT.Exp, scale=-1.0).then_inc(a, 1)
                act.activation(b[:], b[:], ACT.Exp).then_inc(a, 1)
                act.activation(k_end[:], k_end[:], ACT.Exp).then_inc(a, 1)
                act.activation(dec[:], dec[:], ACT.Exp).then_inc(a, 1)

            @block.vector
            def _(dve):
                g = VEC_AT["hgrn_gamma"]
                dve.tensor_tensor(lb[:], E.vcol[:, g + 4:g + 8], E.vcol[:, g:g + 4], ALU.subtract).then_inc(v, 1)
                dve.wait_ge(a, 3)
                dve.tensor_scalar(lb[:], lb[:], 1.0, None, ALU.add).then_inc(v, 1)
                dve.wait_ge(v, 2)
                dve.reciprocal(lb[:], lb[:]).then_inc(v, 1)
                dve.wait_ge(v, 3)
                dve.tensor_scalar(omlb[:], lb[:], -1.0, 1.0, ALU.mult, ALU.add).then_inc(v, 1)
                dve.wait_ge(v, 4)
                for j in range(4):
                    ins = dve.tensor_scalar(e1[:, j, :], e1[:, j, :], omlb[:, j:j + 1], lb[:, j:j + 1], ALU.mult, ALU.add)
                ins.then_inc(v, 1)
                for j in range(4):
                    ins = dve.tensor_scalar(key[:, j, :], key[:, j, :], omlb[:, j:j + 1], None, ALU.mult)
                ins.then_inc(v, 1)
                dve.wait_ge(cst_in, 32)
                dve.wait_ge(a, 4)
                for j in range(4):
                    dve.tensor_tensor_scan(b[:, j, :], reset[:], e1[:, j, :], 0.0, ALU.mult, ALU.add).then_inc(v, 1)
                dve.wait_ge(v, 10)
                bc = b[:].rearrange("p j (c t) -> p (j c) t", t=C)
                dve.tensor_copy(dec[:].rearrange("p j c -> p (j c)"), bc[:, :, C - 1])
                dve.tensor_tensor(k_end[:].rearrange("p j (c t) -> p (j c) t", t=C),
                                  bc[:, :, C - 1:C].to_broadcast([P, 4 * NC, C]), bc, ALU.subtract).then_inc(v, 1)
                dve.wait_ge(a, 7)
                dve.tensor_tensor(k_in[:], k_in[:], key[:], ALU.mult)
                dve.tensor_tensor(k_end[:], k_end[:], key[:], ALU.mult)
                dve.tensor_tensor(hq[:], hq[:], b[:], ALU.mult)
        kt = key
        turn(E, "hg_kturn", [([k_end[:, j, i * P:(i + 1) * P] for j in range(4)],
                              kt[:, i, :]) for i in range(4)])
        Sall = sb("hg_states", [P, 4, 64, NC])
        dS, decx = sb("hg_dS", [P, 64, NC]), sb("hg_decx", [P, 64, NC])
        gains, out, decd, scanned = (sem(f"hg_{x}") for x in ("gains", "gains_out", "decay_spread", "scanned"))
        with nc.Block() as block:
            @block.tensor
            def _(pe):
                for j in range(4):
                    if j >= 2:
                        pe.wait_ge(out, j - 1)
                    for ch in range(NC):
                        t, r = ch // 4, ch % 4
                        for h2 in range(2):
                            col, at = (2 * j + h2) * 64, (4 * (j % 2) + r) * BANK + 64 * t
                            last = pe.matmul(E.ps[64 * h2:64 * h2 + 64, at:at + 64], kt[32 * r:32 * r + 32, t, col:col + 64],
                                             hi[32 * r:32 * r + 32, t, col:col + 64], start=True, stop=True)
                    last.then_inc(gains, 1)

            @block.scalar
            def _(act):
                for j in range(4):
                    if j >= 1:
                        act.wait_ge(scanned, j)
                    act.wait_ge(gains, j + 1)
                    for r in range(4):
                        last = act.activation(dS[:].rearrange("p v (t r) -> p r t v", r=4)[:, r],
                                              E.bank(4 * (j % 2) + r, 256).rearrange("p (t v) -> p t v", v=64), ACT.Copy)
                    last.then_inc(out, 1)

            @block.vector
            def _(dve):
                for j in range(4):
                    dve.tensor_copy(decx[:], dec[:, j:j + 1, :].to_broadcast([P, 64, NC])).then_inc(decd, 1)
                    dve.wait_ge(decd, 2 * j + 1)
                    dve.memset(decx[:, :, 0:1], 0.0).then_inc(decd, 1)
                    dve.wait_ge(decd, 2 * j + 2)
                    dve.wait_ge(out, j + 1)
                    dve.tensor_tensor_scan(Sall[:, j].rearrange("p v c -> p (v c)"), decx[:].rearrange("p v c -> p (v c)"),
                                           dS[:].rearrange("p v c -> p (v c)"), 0.0, ALU.mult, ALU.add).then_inc(scanned, 1)
                    dve.wait_ge(scanned, j + 1)
        AT = sb("hg_AT", [P, 2, 2, P])
        oT = k_end
        scored, masked, summed, taken = (sem(f"hg_{x}") for x in ("scored", "masked", "summed", "taken"))
        with nc.Block() as block:
            units = [(j, t) for j in range(4) for t in range(4)]

            @block.tensor
            def _(pe):
                for n in range(17):
                    if n < 16:
                        j, t = units[n]
                        if n >= 2:
                            pe.wait_ge(masked, n - 1)
                        for h2 in range(2):
                            lo = 64 * h2
                            last = pe.matmul(E.bank(2 * (n % 2) + h2, P), k_in[lo:lo + 64, j, t * P:(t + 1) * P],
                                             hq[lo:lo + 64, j, t * P:(t + 1) * P], start=True, stop=True)
                        last.then_inc(scored, 1)
                    if n >= 1:
                        j, t = units[n - 1]
                        pe.wait_ge(masked, n)
                        if n >= 3:
                            pe.wait_ge(taken, n - 2)
                        for h2 in range(2):
                            lo, col = 64 * h2, (2 * j + h2) * 64
                            o = E.ps[lo:lo + 64, (4 + (n - 1) % 2) * BANK:(4 + (n - 1) % 2) * BANK + P]
                            pe.matmul(o, hi[:, t, col:col + 64], AT[:, (n - 1) % 2, h2, :], start=True, stop=False,
                                      skip_group_check=True)
                            for ci in range(4):
                                ch = 4 * t + ci
                                if ch:
                                    last = pe.matmul(o[:, 32 * ci:32 * ci + 32], Sall[lo:lo + 64, j, :, ch - 1],
                                                     hq[lo:lo + 64, j, 32 * ch:32 * ch + 32], start=False, stop=(ci == 3),
                                                     skip_group_check=True)
                        last.then_inc(summed, 1)

            @block.vector
            def _(dve):
                for n in range(16):
                    dve.wait_ge(scored, n + 1)
                    if n >= 2:
                        dve.wait_ge(summed, n - 1)
                    for h2 in range(2):
                        last = dve.tensor_tensor(AT[:, n % 2, h2, :], mask[:], E.bank(2 * (n % 2) + h2, P), ALU.mult)
                    last.then_inc(masked, 1)

            @block.scalar
            def _(act):
                for n in range(16):
                    j, t = units[n]
                    act.wait_ge(summed, n + 1)
                    act.activation(oT[:, j, t * P:(t + 1) * P], E.bank(4 + n % 2, P), ACT.Copy).then_inc(taken, 1)
        gated_norm(E, "hg_norm", oT, E.aT[:, 4:8, :], 4, S, 64, E.blk64, lambda k: E.v("hgrn_norm_g", k), gate)


N_EXP, N_GRP, D_EXP = 32, 4, 512


SLOTS = 64
PAIRS = N_EXP // 2


def route(E, R):
    nc, d, sem = E.nc, E.d, E.sem
    with ExitStack() as c:
        sb = lambda n, s, dt=FP: c.enter_context(nc.sbuf_tensor(n, s, dt))
        wr, brow = sb("r_w", [P, KT, 36]), sb("r_bias", [1, 36])
        L, grp, m8, g8, iota = sb("r_L", [P, 4, 36]), sb("r_grp", [P, 4, 8]), sb("r_m8", [P, 4, 8]), sb("r_g8", [P, 4, 8]), \
            sb("r_iota", [P, 8])
        idx, idf = sb("r_idx", [P, 4, 8], mybir.dt.uint32), sb("r_idf", [P, 4, 8])
        m8b, idxb, idfb = sb("r_m8b", [P, 4, 8]), sb("r_idxb", [P, 4, 8], mybir.dt.uint32), sb("r_idfb", [P, 4, 8])
        ex, ohg, sel, tmp = sb("r_ex", [P, 4, 4]), sb("r_ohg", [P, 4, 4]), sb("r_sel", [P, 4, 8]), sb("r_tmp", [P, 4, 8])
        s1, s2, s3, s4 = (sb(f"r_s{i}", [P, 4, 1]) for i in range(4))
        Gt, mem, before = R.gate, sb("r_mem", [P, 4, 32]), sb("r_before", [P, P])
        mem8, fullest, need = sb("r_mem8", [P, 4, 8]), sb("r_fullest", [P, 1]), sb("r_need", [P, 8])
        loaded, logits, v, a, ranked = (sem(f"route_{x}") for x in ("loaded", "logits", "dve", "act", "ranked"))
        with nc.Block() as block:
            @block.sync
            def _(sp):
                sp.dma_start(wr[:, :, 0:4], kn(d["w_group"][0])).then_inc(loaded, 16)
                sp.dma_start(wr[:, :, 4:36], kn(d["w_router"][0])).then_inc(loaded, 16)
                sp.dma_start(brow[:, 0:4], d["b_group"]).then_inc(loaded, 16)
                sp.dma_start(brow[:, 4:36], d["b_router"]).then_inc(loaded, 16)
                sp.dma_start(iota[:], E.cst("iota")[:, 0:8]).then_inc(loaded, 16)
                sp.dma_start(before[:], E.cst("before")).then_inc(loaded, 16)
                sp.dma_start(R.slot[:], E.cst("iota64")).then_inc(loaded, 16)

            @block.tensor
            def _(pe):
                pe.wait_ge(loaded, 112)
                for t in range(4):
                    pe.matmul(E.bank(t, 36), E.ones[0:1, :], brow[0:1, :], start=True, stop=False)
                    for k in range(KT):
                        last = pe.matmul(E.bank(t, 36), E.aT[:, k, t * P:(t + 1) * P], wr[:, k, :], start=False,
                                         stop=(k == KT - 1))
                    last.then_inc(logits, 1)
                pe.wait_ge(v, 99)
                for t in range(4):
                    for i in range(t):
                        pe.matmul(E.bank(4, P)[:, 32 * t:32 * t + 32], E.ones, mem[:, i, :], start=(i == 0), stop=False)
                    pe.matmul(E.bank(4, P)[:, 32 * t:32 * t + 32], before[:], mem[:, t, :], start=(t == 0), stop=True)
                for t in range(4):
                    last = pe.matmul(E.bank(5, 32), E.ones, mem[:, t, :], start=(t == 0), stop=(t == 3))
                last.then_inc(ranked, 1)

            @block.scalar
            def _(act):
                act.wait_ge(v, 11)
                act.activation(ex[:], ex[:], ACT.Exp).then_inc(a, 1)
                act.wait_ge(v, 25)
                act.activation(s2[:], s2[:], ACT.Exp).then_inc(a, 1)

            @block.vector
            def _(dve):
                n = [0]

                def done(ins, upto=None):
                    k = (upto or n[0] + 1) - n[0]
                    ins.then_inc(v, k)
                    n[0] += k
                    dve.wait_ge(v, n[0])
                dve.wait_ge(logits, 4)
                dve.wait_ge(loaded, 112)
                done(dve.memset(grp[:], -3e38))
                done(dve.tensor_copy(L[:], E.ps[:].rearrange("p (b n) -> p b n", n=BANK)[:, 0:4, 0:36]))
                done(dve.tensor_copy(grp[:, :, 0:4], L[:, :, 0:4]))
                for t in range(4):
                    last = dve.max(m8[:, t, :], grp[:, t, :])
                done(last)
                for t in range(4):
                    last = dve.max_index(idx[:, t, :], m8[:, t, :], grp[:, t, :])
                done(last)
                done(dve.tensor_copy(idf[:], idx[:]))
                done(dve.tensor_tensor(ohg[:], iota[:, 0:4].unsqueeze(1).to_broadcast([P, 4, 4]),
                                       idf[:, :, 0:1].to_broadcast([P, 4, 4]), ALU.is_equal))
                done(dve.tensor_tensor(ex[:], L[:, :, 0:4], m8[:, :, 0:1].to_broadcast([P, 4, 4]), ALU.subtract), 11)
                done(dve.tensor_tensor(sel[:], L[:, :, 4:12], ohg[:, :, 0:1].to_broadcast([P, 4, 8]), ALU.mult))
                for g in range(1, 4):
                    done(dve.tensor_tensor(tmp[:], L[:, :, 4 + 8 * g:12 + 8 * g], ohg[:, :, g:g + 1].to_broadcast([P, 4, 8]),
                                           ALU.mult))
                    done(dve.tensor_tensor(sel[:], sel[:], tmp[:], ALU.add))
                for t in range(4):
                    last = dve.max(m8b[:, t, :], sel[:, t, :])
                done(last)
                for t in range(4):
                    last = dve.max_index(idxb[:, t, :], m8b[:, t, :], sel[:, t, :])
                done(last)
                done(dve.tensor_copy(idfb[:], idxb[:]))
                done(dve.tensor_tensor(s2[:], m8b[:, :, 1:2], m8b[:, :, 0:1], ALU.subtract), 25)
                dve.wait_ge(a, 2)
                done(dve.tensor_reduce(s1[:], ex[:], AX.X, ALU.add))
                done(dve.tensor_scalar(s3[:], s2[:], 1.0, None, ALU.add))
                done(dve.tensor_tensor(s1[:], s1[:], s3[:], ALU.mult))
                done(dve.reciprocal(s1[:], s1[:]))
                done(dve.tensor_tensor(s2[:], s2[:], s1[:], ALU.mult))
                iob = iota[:, 0:8].unsqueeze(1).to_broadcast([P, 4, 8])
                for which, g in ((0, s1), (1, s2)):
                    done(dve.tensor_tensor(tmp[:], iob, idfb[:, :, which:which + 1].to_broadcast([P, 4, 8]), ALU.is_equal))
                    if which == 0:
                        done(dve.tensor_copy(mem8[:], tmp[:]))
                        done(dve.tensor_tensor(g8[:], tmp[:], g[:].to_broadcast([P, 4, 8]), ALU.mult))
                    else:
                        done(dve.tensor_tensor(mem8[:], mem8[:], tmp[:], ALU.add))
                        done(dve.tensor_tensor(tmp[:], tmp[:], g[:].to_broadcast([P, 4, 8]), ALU.mult))
                done(dve.tensor_tensor(g8[:], g8[:], tmp[:], ALU.add))
                for g in range(4):
                    of_group = ohg[:, :, g:g + 1].to_broadcast([P, 4, 8])
                    dve.tensor_tensor(Gt[:, :, 8 * g:8 * g + 8], g8[:], of_group, ALU.mult)
                    last = dve.tensor_tensor(mem[:, :, 8 * g:8 * g + 8], mem8[:], of_group, ALU.mult)
                done(last, 99)
                dve.wait_ge(ranked, 1)
                done(dve.tensor_scalar(R.key[:].rearrange("p t e -> p (t e)"), E.bank(4, P), 1.0, None, ALU.add))
                done(dve.tensor_tensor(R.key[:], R.key[:], mem[:], ALU.mult))
                done(dve.tensor_scalar(R.key[:], R.key[:], -1.0, None, ALU.add))
                done(dve.tensor_reduce(fullest[:], E.bank(5, 32), AX.X, ALU.max))
                done(dve.tensor_scalar(need[:], iota[:], float(SLOTS), None, ALU.mult))
                done(dve.tensor_tensor(need[:], need[:], fullest[:].to_broadcast([P, 8]), ALU.is_lt))
                done(dve.tensor_reduce(fullest[:], need[:], AX.X, ALU.add))
                done(dve.tensor_copy(R.passes[:], fullest[:]))


def token_rows(E, R):
    turned, high, low = (E.sem(f"rows_{x}") for x in ("turned", "high", "low"))
    with E.nc.Block() as block:
        units = [(t, half) for t in range(4) for half in range(2)]

        @block.tensor
        def _(pe):
            for u, (t, half) in enumerate(units):
                for i in range(4):
                    last = pe.transpose(E.bank(u)[:, i * P:(i + 1) * P], E.aT[:, 4 * half + i, t * P:(t + 1) * P], E.ident)
                last.then_inc(turned, 1)

        @block.scalar
        def _(act):
            for u, (t, half) in enumerate(units):
                act.wait_ge(turned, u + 1)
                act.activation(R.xh[:, t, half * BANK:(half + 1) * BANK], E.bank(u), ACT.Copy).then_inc(high, 1)

        @block.vector
        def _(dve):
            for u, (t, half) in enumerate(units):
                dve.wait_ge(high, u + 1)
                cols = slice(half * BANK, (half + 1) * BANK)
                dve.tensor_tensor(R.xl[:, t, cols], E.bank(u), R.xh[:, t, cols].bitcast(FP), ALU.subtract).then_inc(low, 1)


def experts(E, R):
    nc, d, sem = E.nc, E.d, E.sem
    FT = D_EXP // P
    FR = mybir.dt.float32r
    with ExitStack() as c:
        sb = lambda n, s, dt=FP: c.enter_context(nc.sbuf_tensor(n, s, dt))
        sel, back = sb("e_sel", [P, 4, P], FR), sb("e_back", [P, S], FR)
        xg, sg, hid, hidT = sb("e_xg", [P, KT, P]), sb("e_silu", [P, D_EXP]), sb("e_hid", [P, D_EXP]), sb("e_hidT", [P, FT, P])
        yh, yl, weight = sb("e_y_high", [P, D], FR), sb("e_y_low", [P, D], FR), sb("e_weight", [P, 1])
        wg, wu, wd, in_g, in_u, in_d = R.wg, R.wu, R.wd, R.in_g, R.in_u, R.in_d
        (selected, gathered, xg_act, xg_dve, gates, silus, ups, hids, hid_turned, hid_out, sel_turned, back_out, weight_out,
         downs, y_high, y_low, scattered, added, cleared, keyed) = (sem(f"exp_{n}") for n in (
             "selected", "gathered", "xg_act", "xg_dve", "gate_done", "silu", "up_done", "hidden", "hid_turned", "hid_out",
             "sel_turned", "back_out", "weight_out", "down_done", "y_high", "y_low", "scattered", "added", "cleared",
             "keyed"))

        with nc.Block() as block:
            @block.tensor
            def _(pe):
                n_pass = pe.value_load(R.passes[0:1, 0:1], min_val=1, max_val=S // SLOTS)
                with pe.Fori(0, n_pass) as p, pe.Fori(0, PAIRS) as i:
                    q = pe.snap(p * PAIRS + i)
                    pe.wait_ge(selected, q + 1)
                    pe.wait_ge(back_out, q + 1)
                    pe.wait_ge(weight_out, q + 1)
                    for k in range(KT):
                        for t in range(4):
                            for x in (R.xh, R.xl):
                                last = pe.matmul(E.bank(4 + k // 4)[:, (k % 4) * P:(k % 4 + 1) * P], x[:, t, k * P:(k + 1) * P],
                                                 sel[:, t, :], start=(t == 0 and x is R.xh), stop=(t == 3 and x is R.xl))
                        if k % 4 == 3:
                            last.then_inc(gathered, 1)
                    pe.wait_ge(in_g, 16 * q + 16)
                    pe.wait_ge(hid_out, q + 1)
                    pe.wait_ge(xg_act, q + 1)
                    for k in range(KT):
                        if k == KT // 2:
                            pe.wait_ge(xg_dve, q + 1)
                        for s in range(2):
                            last = pe.matmul(E.ps[SLOTS * s:SLOTS * (s + 1), 0:BANK], xg[:, k, s * SLOTS:(s + 1) * SLOTS],
                                             wg[:, s, k, :], start=(k == 0), stop=(k == KT - 1))
                    last.then_inc(gates, 1)
                    pe.wait_ge(in_u, 16 * q + 16)
                    pe.wait_ge(hids, q + 1)
                    pe.wait_ge(y_high, 2 * q + 2)
                    pe.wait_ge(y_low, 2 * q + 2)
                    for k in range(KT):
                        for s in range(2):
                            last = pe.matmul(E.ps[SLOTS * s:SLOTS * (s + 1), BANK:2 * BANK], xg[:, k, s * SLOTS:(s + 1) * SLOTS],
                                             wu[:, s, k, :], start=(k == 0), stop=(k == KT - 1))
                        if k == KT - 1:
                            last.then_inc(ups, 1)
                        pe.wait_ge(added, 8 * q + k + 1)
                        pe.matmul(E.bank(6 + k % 2), yh[:, k * P:(k + 1) * P], back[:], start=True, stop=False)
                        pe.matmul(E.bank(6 + k % 2), yl[:, k * P:(k + 1) * P], back[:], start=False, stop=True)\
                          .then_inc(scattered, 1)
                    for t in range(4):
                        pe.transpose(E.bank(4)[:, t * P:(t + 1) * P], sel[:, t, :].bitcast(FP), E.ident)
                    for t in range(4):
                        last = pe.matmul(E.bank(5, 2), sel[:, t, :].bitcast(FP), R.gate[:, t, bass.ds(2 * i, 2)],
                                         start=(t == 0), stop=(t == 3))
                    last.then_inc(sel_turned, 1)
                    pe.wait_ge(hids, q + 2)
                    for f in range(FT):
                        last = pe.transpose(E.bank(0)[:, f * P:(f + 1) * P], hid[:, f * P:(f + 1) * P], E.ident)
                    last.then_inc(hid_turned, 1)
                    pe.wait_ge(in_d, 16 * q + 16)
                    pe.wait_ge(hid_out, q + 2)
                    for half in range(2):
                        for f in range(FT):
                            for s in range(2):
                                last = pe.matmul(E.ps[SLOTS * s:SLOTS * (s + 1), (2 + half) * BANK:(3 + half) * BANK],
                                                 hidT[:, f, s * SLOTS:(s + 1) * SLOTS],
                                                 wd[:, s, f, half * BANK:(half + 1) * BANK], start=(f == 0), stop=(f == FT - 1))
                        last.then_inc(downs, 1)

            @block.scalar
            def _(act):
                n_pass = act.value_load(R.passes[0:1, 0:1], min_val=1, max_val=S // SLOTS)
                act.wait_ge(cleared, 3)
                act.sem_inc(y_high, 2)
                act.sem_inc(hid_out, 1)

                def turn_(q, i):
                    act.wait_ge(gathered, 2 * q + 1)
                    act.activation(xg[:, 0:4, :], E.bank(4).rearrange("p (k n) -> p k n", k=4), ACT.Copy).then_inc(xg_act, 1)
                    act.wait_ge(gates, q + 1)
                    if i is not None:
                        act.dma_start(wg[:], pair(d["w_gate"], i)).then_inc(in_g, 16)
                    act.activation(sg[:], E.bank(0), ACT.Silu).then_inc(silus, 1)
                    act.wait_ge(ups, q + 1)
                    if i is not None:
                        act.dma_start(wu[:], pair(d["w_up"], i)).then_inc(in_u, 16)
                    act.wait_ge(hid_turned, q + 1)
                    act.activation(hidT[:], E.bank(0).rearrange("p (f n) -> p f n", f=FT), ACT.Copy).then_inc(hid_out, 1)
                    act.wait_ge(weight_out, q + 2)
                    for half in range(2):
                        act.wait_ge(downs, 2 * q + half + 1)
                        if half == 1 and i is not None:
                            act.dma_start(wd[:], pair(d["w_down"], i)).then_inc(in_d, 16)
                        act.activation(yh[:, half * BANK:(half + 1) * BANK], E.bank(2 + half), ACT.Copy, scale=weight[:])\
                           .then_inc(y_high, 1)
                with act.Fori(0, n_pass) as p:
                    with act.Fori(0, PAIRS - 1) as i:
                        turn_(act.snap(p * PAIRS + i), i + 1)
                    turn_(act.snap(p * PAIRS + PAIRS - 1), None)
                    with act.If(p + 1 < n_pass):
                        act.dma_start(wg[:], pair(d["w_gate"], 0)).then_inc(in_g, 16)
                        act.dma_start(wu[:], pair(d["w_up"], 0)).then_inc(in_u, 16)
                        act.dma_start(wd[:], pair(d["w_down"], 0)).then_inc(in_d, 16)
                    act.nop()

            @block.vector
            def _(dve):
                n_pass = dve.value_load(R.passes[0:1, 0:1], min_val=1, max_val=S // SLOTS)
                dve.memset(sg[:], 0.0).then_inc(cleared, 1)
                dve.memset(hid[:], 0.0).then_inc(cleared, 1)
                dve.wait_ge(cleared, 2)
                dve.tensor_copy(back[:], sg[:])
                for half in range(2):
                    dve.tensor_copy(yh[:, half * BANK:(half + 1) * BANK], sg[:])
                    last = dve.tensor_copy(yl[:, half * BANK:(half + 1) * BANK], hid[:])
                last.then_inc(cleared, 1)
                dve.wait_ge(cleared, 3)
                dve.sem_inc(y_low, 2)
                dve.sem_inc(back_out, 1)
                dve.sem_inc(weight_out, 1)
                dve.sem_inc(hids, 1)
                dve.sem_inc(added, 2)
                dve.sem_inc(keyed, 1)

                def select(i):
                    dve.tensor_tensor(sel[:].rearrange("p t (e s) -> p t e s", e=2),
                                      R.slot[:].unsqueeze(1).unsqueeze(1).to_broadcast([P, 4, 2, SLOTS]),
                                      R.key[:, :, bass.ds(2 * i, 2)].unsqueeze(3).to_broadcast([P, 4, 2, SLOTS]),
                                      ALU.is_equal).then_inc(selected, 1)

                def turn_(q, p, i):
                    dve.wait_ge(gathered, 2 * q + 2)
                    dve.tensor_copy(xg[:, 4:8, :], E.bank(5).rearrange("p (k n) -> p k n", k=4)).then_inc(xg_dve, 1)
                    for n in range(KT):
                        dve.wait_ge(scattered, 8 * q + n + 1)
                        dve.tensor_tensor(E.hT[:, n, 0:S], E.hT[:, n, 0:S], E.bank(6 + n % 2), ALU.add).then_inc(added, 1)
                    dve.wait_ge(silus, q + 1)
                    dve.wait_ge(ups, q + 1)
                    dve.tensor_tensor(hid[:], sg[:], E.bank(1), ALU.mult).then_inc(hids, 1)
                    dve.wait_ge(sel_turned, q + 1)
                    dve.tensor_copy(back[:], E.bank(4)).then_inc(back_out, 1)
                    for s in range(2):
                        last = dve.tensor_copy(weight[SLOTS * s:SLOTS * (s + 1), :], E.ps[SLOTS * s:SLOTS * (s + 1), 5 * BANK + s:5 * BANK + s + 1])
                    last.then_inc(weight_out, 1)
                    if i is None:
                        dve.wait_ge(selected, q + 1)
                        dve.tensor_scalar(R.key[:], R.key[:], -float(SLOTS), None, ALU.add).then_inc(keyed, 1)
                        dve.wait_ge(keyed, p + 2)
                    select(0 if i is None else i)
                    dve.wait_ge(weight_out, q + 2)
                    for half in range(2):
                        dve.wait_ge(y_high, 2 * q + half + 3)
                        cols = slice(half * BANK, (half + 1) * BANK)
                        dve.scalar_tensor_tensor(out=yl[:, cols], in0=E.bank(2 + half), scalar=weight[:],
                                                 in1=yh[:, cols].bitcast(FP), op0=ALU.mult, op1=ALU.subtract).then_inc(y_low, 1)
                select(0)
                with dve.Fori(0, n_pass) as p:
                    with dve.Fori(0, PAIRS - 1) as i:
                        turn_(dve.snap(p * PAIRS + i), p, i + 1)
                    turn_(dve.snap(p * PAIRS + PAIRS - 1), p, None)
        last_in, last_out = sem("exp_last_scattered"), sem("exp_last_added")
        with nc.Block() as block:
            @block.tensor
            def _(pe):
                for n in range(KT):
                    pe.matmul(E.bank(n), yh[:, n * P:(n + 1) * P], back[:], start=True, stop=False)
                    pe.matmul(E.bank(n), yl[:, n * P:(n + 1) * P], back[:], start=False, stop=True).then_inc(last_in, 1)

            @block.vector
            def _(dve):
                for n in range(KT):
                    dve.wait_ge(last_in, n + 1)
                    dve.tensor_tensor(E.hT[:, n, 0:S], E.hT[:, n, 0:S], E.bank(n), ALU.add).then_inc(last_out, 1)


def pair(w, i):
    return w[0][bass.ds(2 * i, 2)].rearrange("e (k p) n -> p (e k) n", p=P).rearrange("p (e k) n -> p e k n", e=2)


def moe(E):
    nc, d, sem = E.nc, E.d, E.sem
    with ExitStack() as c:
        sb = lambda n, s, dt=FP: c.enter_context(nc.sbuf_tensor(n, s, dt))
        R = Parts()
        R.wg, R.wu, R.wd = sb("e_wg", [P, 2, KT, D_EXP]), sb("e_wu", [P, 2, KT, D_EXP]), sb("e_wd", [P, 2, D_EXP // P, D])
        R.in_g, R.in_u, R.in_d = (sem(f"exp_{n}_loaded") for n in ("gate", "up", "down"))
        with nc.Block() as block:
            @block.scalar
            def _(act):
                act.dma_start(R.wg[:], pair(d["w_gate"], 0)).then_inc(R.in_g, 16)
                act.dma_start(R.wu[:], pair(d["w_up"], 0)).then_inc(R.in_u, 16)
                act.dma_start(R.wd[:], pair(d["w_down"], 0)).then_inc(R.in_d, 16)
        norm(E, "n2", E.hT, E.aT, KT, D, S, lambda k, s: E.v("norm2_g", k))
        R.gate, R.key, R.slot = sb("r_gate", [P, 4, N_EXP]), sb("r_key", [P, 4, N_EXP]), sb("r_slot", [P, SLOTS])
        R.passes = sb("r_passes", [P, 1], mybir.dt.int32)
        route(E, R)
        R.xh, R.xl = sb("e_xh", [P, 4, D], mybir.dt.float32r), sb("e_xl", [P, 4, D], mybir.dt.float32r)
        token_rows(E, R)
        experts(E, R)
    norm(E, "nf", E.hT, E.hT, KT, D, S, lambda k, s: E.v("norm_f_g", k))


N_MOD, D_FF = 6, 4 * D


def modulation(E):
    nc, d, sem = E.nc, E.d, E.sem
    turns = N_MOD * D // 512 // 2
    loaded = [sem(f"ada_w_loaded{i}") for i in range(2)]
    cleared, silus, full, copied, folded, biased = (sem(f"ada_{x}") for x in (
        "cleared", "silu", "full", "copied", "folded", "biased"))
    with nc.sbuf_tensor("ada_c", [P, KT, 32], FP) as cs, nc.sbuf_tensor("ada_ring", [P, 2, KT, 512], FP) as ring, \
            nc.sbuf_tensor("ada_rows", [P, 2, 512], FP) as rows, nc.Block() as block:
        ada = [d["ada_w_2"][l].rearrange("(k p) (g n) -> g p k n", p=P, n=512) for l in range(2)]
        b0 = VEC_AT["ada_b_2"]

        @block.scalar
        def _(act):
            for s in range(2):
                act.dma_start(ring[:, s], ada[0][s]).then_inc(loaded[s], 16)
            act.wait_ge(cleared, 1)
            for s, name in enumerate(("c_2", "c_ctx_2")):
                last = act.activation(cs[:, :, s], E.vcol[:, VEC_AT[name]:VEC_AT[name] + KT], ACT.Silu)
            last.then_inc(silus, 1)

            def take(i, layer, s, fetch):
                act.wait_ge(full, 2 * i + 2 * turns * layer + s + 1)
                if fetch is not None:
                    act.dma_start(ring[:, s], fetch).then_inc(loaded[s], 16)
                act.activation(rows[:, s], E.bank(s), ACT.Copy).then_inc(copied, 1)
            for layer in range(2):
                with act.Fori(0, turns - 1) as i:
                    for s in range(2):
                        take(i, layer, s, ada[layer][bass.ds(2 * i + s + 2, 1)].rearrange("o p k n -> p (o k) n"))
                for s in range(2):
                    take(turns - 1, layer, s, ada[1][s] if layer == 0 else None)

        @block.tensor
        def _(pe):
            pe.wait_ge(silus, 1)
            with pe.Fori(0, 2 * turns) as i:
                for s in range(2):
                    pe.wait_ge(loaded[s], 16 * i + 16)
                    for k in range(KT):
                        g = 32 * (k % 4)
                        last = pe.matmul(E.ps[g:g + 32, s * BANK:(s + 1) * BANK], cs[:, k, :], ring[:, s, k, :], start=(k < 4),
                                         stop=(k >= 4), tile_position=(0, g))
                    last.then_inc(full, 1)
                for s in range(2):
                    pe.wait_ge(copied, 2 * i + s + 1)
                    pe.wait_ge(biased, 2 * i + 1)
                    for n in range(4):
                        last = pe.matmul(E.bank(2 + s)[:, 2 * n:2 * n + 2], rows[:, s, n * P:(n + 1) * P], E.fold,
                                         start=True, stop=True)
                    last.then_inc(folded, 1)

        @block.vector
        def _(dve):
            dve.memset(cs[:], 0.0).then_inc(cleared, 1)
            flat = E.mod[:].rearrange("p l m s -> p (l m) s")
            dve.sem_inc(biased, 1)
            with dve.Fori(0, 2 * turns) as i:
                for s in range(2):
                    dve.wait_ge(folded, 2 * i + s + 1)
                    dve.tensor_tensor(flat[:, bass.ds(8 * i + 4 * s, 4), :], E.bank(2 + s, 8).rearrange("p (n s) -> p n s", s=2),
                                      E.vcol[:, bass.ds(8 * i + b0 + 4 * s, 4)].unsqueeze(2).to_broadcast([P, 4, 2]), ALU.add)\
                       .then_inc(biased, 1)
            dve.wait_ge(biased, 4 * turns + 1)
            for layer in range(2):
                for which, (name, m) in enumerate((("norm1_w_2", 1), ("norm2_w_2", 4))):
                    w = E.vcol[:, VEC_AT[name] + 8 * layer:VEC_AT[name] + 8 * layer + 8].unsqueeze(2).to_broadcast([P, 8, 2])
                    dve.scalar_tensor_tensor(out=E.nw[:, layer, which], in0=E.mod[:, layer, 8 * m:8 * m + 8, :], scalar=1.0,
                                             in1=w, op0=ALU.add, op1=ALU.mult)


def modulated_norm(E, name, layer, which, T):
    segs = [(0, S)] + ([(S, T)] if T > S else [])
    m = 0 if which == 0 else 3
    norm(E, name, E.hT, E.aT, KT, D, T, lambda k, s: E.nw[:, layer, which, k, s:s + 1],
         shift=lambda k, s: E.mod[:, layer, 8 * m + k, s:s + 1], segs=segs)


FR = mybir.dt.float32r
MW = 256
CHUNKS = 4


def mlp(E, layer, T):
    nc, d, sem = E.nc, E.d, E.sem
    name = f"mlp{layer}"
    segs = [(0, S)] + ([(S, T)] if T > S else [])
    ns = len(segs)
    CW = D_FF // CHUNKS
    HT, ST, NT = CW // P, CW // MW, MW // P
    STEPS = 2 * ST * CHUNKS
    U = NT * ns
    unit = [(n, s, a, b) for n in range(NT) for s, (a, b) in enumerate(segs)]
    w1, w2 = d["mlp_w1_2"][layer], d["mlp_w2_2"][layer]

    def weight(g):
        chunk, st = g // (2 * ST), g % (2 * ST)
        if st < ST:
            return kn(w1[:, chunk * CW + st * MW:chunk * CW + (st + 1) * MW])
        return kn(w2[chunk * CW:(chunk + 1) * CW, (st - ST) * MW:(st - ST + 1) * MW])
    with ExitStack() as c:
        sb = lambda n, s, dt=FP: c.enter_context(nc.sbuf_tensor(f"{name}_{n}", s, dt))
        ring = ring_of(E, c, name, [weight(g) for g in range(STEPS)])
        ring, loaded = ring.ring[:].rearrange("p s (k n) -> p s k n", k=KT), ring.loaded
        modulated_norm(E, f"{name}_norm", layer, 1, T)
        wh, wl = sb("w_high", [P, 2, KT, MW], FR), sb("w_low", [P, 2, KT, MW], FR)
        xh, xl = sb("x_high", [P, KT, T], FR), sb("x_low", [P, KT, T], FR)
        hh, hl = sb("h_high", [P, HT, T], FR), sb("h_low", [P, HT, T], FR)
        r, sq = sb("relu", [P, NT, T]), sb("square", [P, NT, T])
        (w_high, w_low, x_high, x_low, full, relus, squares, h_high, h_low, added) = (sem(f"{name}_{x}") for x in (
            "w_high", "w_low", "x_high", "x_low", "full", "relu", "squared", "h_high", "h_low", "added"))
        bank = lambda st, n, s, w: E.bank(4 * (st % 2) + 2 * n + s, w)

        with nc.Block() as block:
            @block.sync
            def _(sp):
                for g in range(2, STEPS):
                    sp.wait_ge(w_low, g - 1)
                    sp.dma_start(ring[:, g % 2], weight(g)).then_inc(loaded[g % 2], 16)

            @block.tensor
            def _(pe):
                with pe.Fori(0, CHUNKS) as chunk:
                    for st in range(2 * ST):
                        up, i = st < ST, st % ST
                        high, low = (xh, xl) if up else (hh, hl)
                        pe.wait_ge(w_low, 2 * ST * chunk + st + 1)
                        for u, (n, s, a, b) in enumerate(unit):
                            if up == (i >= 2):
                                pe.wait_ge(relus, U * (ST * chunk + (i - 2) % ST) + u + 1)
                            else:
                                pe.wait_ge(added, U * (ST * chunk + i + 2) + u + 1)
                            for k in range(KT):
                                if u == 0 and i == 0:
                                    pe.wait_ge(x_low, k + 1) if up else pe.wait_ge(h_low, NT + HT * chunk + k + 1)
                                for p, (w, x) in enumerate(((wh, high), (wh, low), (wl, high))):
                                    last = pe.matmul(bank(st, n, s, b - a), w[:, st % 2, k, n * P:(n + 1) * P], x[:, k, a:b],
                                                     start=(k == 0 and p == 0), stop=(k == KT - 1 and p == 2))
                            last.then_inc(full, 1)

            @block.scalar
            def _(act):
                act.sem_inc(squares, NT)
                act.sem_inc(h_high, NT)

                def split(slot, count):
                    act.wait_ge(loaded[slot], 16 * count)
                    act.activation(wh[:, slot], ring[:, slot], ACT.Copy).then_inc(w_high, 1)
                split(0, 1)
                for k in range(KT):
                    act.activation(xh[:, k, :], E.aT[:, k, 0:T], ACT.Copy).then_inc(x_high, 1)
                split(1, 1)

                def steps(chunk, last_st):
                    for st in range(2 * ST):
                        done = U * (2 * ST * chunk + st)
                        if st < ST:
                            tiles = NT * (ST * chunk + st)
                            for u, (n, s, a, b) in enumerate(unit):
                                act.wait_ge(full, done + u + 1)
                                if s == 0:
                                    act.wait_ge(squares, tiles + n + 1)
                                    act.wait_ge(h_high, tiles + n + 1)
                                act.activation(r[:, n, a:b], bank(st, n, s, b - a), ACT.Relu).then_inc(relus, 1)
                            for n in range(NT):
                                act.wait_ge(relus, ns * (tiles + n + 1))
                                act.activation(hh[:, NT * st + n, :], r[:, n, :], ACT.Square).then_inc(h_high, 1)
                        else:
                            act.wait_ge(full, done + U)
                        if st + 2 <= last_st:
                            split(st % 2, ST * chunk + st // 2 + 2)
                with act.Fori(0, CHUNKS - 1) as chunk:
                    steps(chunk, 2 * ST + 1)
                steps(CHUNKS - 1, 2 * ST - 1)

            @block.vector
            def _(dve):
                dve.sem_inc(added, ST * U)
                dve.sem_inc(h_low, NT)

                def split(g, slot):
                    dve.wait_ge(w_high, g + 1)
                    dve.tensor_tensor(wl[:, slot], ring[:, slot], wh[:, slot].bitcast(FP), ALU.subtract).then_inc(w_low, 1)
                split(0, 0)
                for k in range(KT):
                    dve.wait_ge(x_high, k + 1)
                    dve.tensor_tensor(xl[:, k, :], E.aT[:, k, 0:T], xh[:, k, :].bitcast(FP), ALU.subtract).then_inc(x_low, 1)
                split(1, 1)

                def steps(chunk, last_st):
                    for st in range(2 * ST):
                        done = U * (2 * ST * chunk + st)
                        if st < ST:
                            tiles = NT * (ST * chunk + st)
                            for n in range(NT):
                                dve.wait_ge(relus, ns * (tiles + n + 1))
                                dve.wait_ge(h_low, tiles + n + 1)
                                dve.tensor_tensor(sq[:, n, :], r[:, n, :], r[:, n, :], ALU.mult).then_inc(squares, 1)
                            for n in range(NT):
                                dve.wait_ge(squares, tiles + NT + n + 1)
                                dve.wait_ge(h_high, tiles + NT + n + 1)
                                dve.tensor_tensor(hl[:, NT * st + n, :], sq[:, n, :], hh[:, NT * st + n, :].bitcast(FP),
                                                  ALU.subtract).then_inc(h_low, 1)
                        else:
                            for u, (n, s, a, b) in enumerate(unit):
                                dve.wait_ge(full, done + u + 1)
                                k = NT * (st - ST) + n
                                dve.wait_ge(added, U * (ST * chunk + st - ST) + u + 1)
                                dve.scalar_tensor_tensor(out=E.hT[:, k, a:b], in0=bank(st, n, s, b - a),
                                                         scalar=E.mod[:, layer, 40 + k, s:s + 1], in1=E.hT[:, k, a:b],
                                                         op0=ALU.mult, op1=ALU.add).then_inc(added, 1)
                        if st + 2 <= last_st:
                            split(2 * ST * chunk + st + 2, st % 2)
                with dve.Fori(0, CHUNKS - 1) as chunk:
                    steps(chunk, 2 * ST + 1)
                steps(CHUNKS - 1, 2 * ST - 1)


def even_mixer(E):
    nc, d, sem = E.nc, E.d, E.sem
    w = d["even_w_in_2"][0]
    aT = E.aT
    segs = [(0, S), (S, TT)]
    with ExitStack() as c:
        sb = lambda n, s: c.enter_context(nc.sbuf_tensor(n, s, FP))
        cq, ckv, kpe = sb("cq", [P, 3, TT]), sb("ckv", [P, 2, TT]), sb("kpe", [P, TT])
        gq, gk, gv, gg, glow = sb("gq", [P, 2, TT]), sb("gk", [P, 2, TT]), sb("gv", [P, 6, 512]), sb("gg", [P, 4, TT]), \
            sb("glow", [32, TT])

        ws = [kn(w[:, a:b]) for a, b in ((0, 384), (384, 672), (672, 1184), (1184, 1696), (1696, 2240))]
        ahead = c.enter_context(ExitStack())
        ring = ring_of(E, ahead, "proj2", ws)
        modulated_norm(E, "even_norm", 0, 0, TT)

        def feats(n0, tiles, dst, func=ACT.Copy, scale=1.0):
            return [feature_unit(E, aT, n0 + n * P, P, a, b, "act", act_copy(dst[:, n, a:b], func, scale))
                    if func != ACT.Copy or n % 2 or scale != 1.0 else
                    feature_unit(E, aT, n0 + n * P, P, a, b, "dve", dve_copy(dst[:, n, a:b]))
                    for n in range(tiles) for a, b in segs]

        def kpe_unit(a, b):
            def mms(wt, bank):
                return [(E.ps[64:96, bank * BANK:bank * BANK + b - a], wt[:, k, 256:288], aT[:, k, a:b]) for k in range(KT)]
            return (mms, "dve", lambda eng, bank: eng.tensor_copy(kpe[64:96, a:b], E.ps[64:96, bank * BANK:bank * BANK + b - a]),
                    None)
        gemm(E, "proj2", [
            dict(w=ws[0], units=feats(0, 3, cq)),
            dict(w=ws[1], units=feats(0, 2, ckv) + [kpe_unit(a, b) for a, b in segs]),
            dict(w=ws[2], units=feats(0, 2, gq, scale=0.125) + feats(256, 2, gk)),
            dict(w=ws[3], units=[token_unit(E, aT, t * P, 512, "act" if t % 2 else "dve",
                                                          (act_copy if t % 2 else dve_copy)(gv[:, t, :])) for t in range(6)]),
            dict(w=ws[4], units=feats(0, 4, gg, func=ACT.Silu) + [
                feature_unit(E, aT, 512, 32, a, b, "dve", dve_copy(glow[:, a:b])) for a, b in segs]),
        ], split=(aT, KT, TT), ahead=ring)
        ahead.close()
        gla(E, gq, gk, gv, gg, glow)
        mla(E, cq, ckv, kpe)
    resid_gemm(E, "wout2", d["even_w_out_2"][0], aT, TT, lambda n, s: E.mod[:, 0, 16 + n, s:s + 1])


def mla(E, cq, ckv, kpe):
    nc, d, sem = E.nc, E.d, E.sem
    segs = [(0, S), (S, TT)]
    norm(E, "cq_norm", cq, cq, 3, 384, TT, lambda k, s: E.v("mla_q_norm_2", k))
    norm(E, "ckv_norm", ckv, ckv, 2, 256, TT, lambda k, s: E.v("mla_kv_norm_2", k))
    QK = 96
    with ExitStack() as c:
        sb = lambda n, s: c.enter_context(nc.sbuf_tensor(n, s, FP))
        O = sb("mla_o", [P, 6, 512])
        with ExitStack() as c2:
            sb2 = lambda n, s: c2.enter_context(nc.sbuf_tensor(n, s, FP))
            qh, kh, V = sb2("mla_q", [P, HEADS, TT]), sb2("mla_k", [P, HEADS, TT]), sb2("mla_v", [P, 6, 512])
            gemm(E, "mla_up", [
                dict(w=kn(d["mla_w_uq_2"][0]), units=[
                    feature_unit(E, cq, QK * h, QK, a, b, "act", act_copy(qh[0:QK, h, a:b], scale=QK ** -0.5), kt=3)
                    for h in range(HEADS) for a, b in segs]),
                dict(w=kn(d["mla_w_ukv_2"][0]), units=[
                    feature_unit(E, ckv, P * h, 64, a, b, "dve", dve_copy(kh[0:64, h, a:b]), kt=2)
                    for h in range(HEADS) for a, b in segs] + [
                    token_unit(E, ckv, t * P, 512, "act", act_copy(V[:, t, :]), kt=2,
                               pick=lambda wt, k: wt[:, k, :].rearrange("p (h x) -> p h x", x=P)[:, :, 64:128])
                    for t in range(6)])])
            rope(E, qh, kh, kpe)
            mla_units(E, qh, kh, V, O)
        turn(E, "mla_oturn", [([O[:, i, k * P:(k + 1) * P] for i in ts], E.aT[:, k, ts[0] * P:(ts[-1] + 1) * P])
                              for k in range(4) for ts in ((0, 1, 2, 3), (4, 5))])


def rope(E, qh, kh, kpe):
    nc, sem = E.nc, E.sem
    with ExitStack() as c:
        sb = lambda n, s: c.enter_context(nc.sbuf_tensor(n, s, FP))
        cos, sin, rot, part = sb("cos", [P, S]), sb("sin", [P, S]), sb("rot", [P, 32]), sb("rope_part", [P, 2, S])
        loaded, swapped, own, part_s, done = (sem(f"rope_{x}") for x in ("loaded", "swapped", "own", "partner", "done"))
        items = [kpe[64:96, 0:S]] + [qh[64:96, h, 0:S] for h in range(HEADS)]
        with nc.Block() as block:
            @block.sync
            def _(sp):
                sp.dma_start(cos[64:96, :], E.cst("cos")[64:96, 0:S]).then_inc(loaded, 16)
                sp.dma_start(sin[64:96, :], E.cst("sin")[64:96, 0:S]).then_inc(loaded, 16)
                sp.dma_start(rot[64:96, :], E.cst("rot")[64:96, :]).then_inc(loaded, 16)

            @block.tensor
            def _(pe):
                pe.wait_ge(loaded, 48)
                for i, x in enumerate(items):
                    if i >= 2:
                        pe.wait_ge(part_s, i - 1)
                    pe.matmul(E.ps[64:96, (i % 2) * BANK:(i % 2) * BANK + S], rot[64:96, :], x, start=True, stop=True)\
                      .then_inc(swapped, 1)

            @block.vector
            def _(dve):
                dve.wait_ge(loaded, 48)
                for i, x in enumerate(items):
                    dve.wait_ge(swapped, i + 1)
                    dve.tensor_tensor(part[64:96, i % 2, :], sin[64:96, :], E.ps[64:96, (i % 2) * BANK:(i % 2) * BANK + S],
                                      ALU.mult).then_inc(part_s, 1)
                    dve.tensor_tensor(x, x, cos[64:96, :], ALU.mult).then_inc(own, 1)
                    dve.wait_ge(own, i + 1)
                    dve.wait_ge(part_s, i + 1)
                    dve.tensor_tensor(x, x, part[64:96, i % 2, :], ALU.add).then_inc(done, 1)

            @block.scalar
            def _(act):
                act.wait_ge(done, 1)
                for h in range(HEADS):
                    act.activation(kh[64:96, h, :], kpe[64:96, :], ACT.Copy)


def mla_units(E, qh, kh, V, O):
    nc, sem = E.nc, E.sem
    QK = 96
    units = [(h, i, 0, TT) if i < 4 else (h, i, S, TT) for h in range(HEADS) for i in range(6)]
    n = len(units)
    scored, maxed, exped, turned, evac_a, evac_v, summed, done = (
        sem(f"mla_{x}") for x in ("scored", "maxed", "exped", "turned", "evac_a", "evac_v", "summed", "done"))
    with ExitStack() as c:
        sb = lambda nm, s: c.enter_context(nc.sbuf_tensor(nm, s, FP))
        pr, pT = sb("mla_pr", [P, 2, TT]), sb("mla_pT", [P, 2, TT])
        neg, tot, inv = (sb(x, [P, n]) for x in ("mla_neg", "mla_tot", "mla_inv"))
        block = c.enter_context(nc.Block())
        score = lambda u, L: E.ps[:, (u % 2) * 2 * BANK:(u % 2) * 2 * BANK + L]

        @block.tensor
        def _(pe):
            for t in range(n + 3):
                if t < n:
                    h, i, k0, k1 = units[t]
                    if t >= 2:
                        pe.wait_ge(exped, t - 1)
                    for a in range(0, k1 - k0, BANK):
                        b = min(a + BANK, k1 - k0)
                        last = pe.matmul(score(t, b)[:, a:b], qh[0:QK, h, i * P:(i + 1) * P], kh[0:QK, h, k0 + a:k0 + b],
                                         start=True, stop=True)
                    last.then_inc(scored, 1)
                if 2 <= t <= n + 1:
                    u = t - 2
                    h, i, k0, k1 = units[u]
                    pe.wait_ge(exped, u + 1)
                    if u >= 1:
                        pe.wait_ge(evac_a, u)
                        pe.wait_ge(evac_v, u)
                    for j in range((k1 - k0) // P):
                        last = pe.transpose(E.ps[:, 4 * BANK + j * P:4 * BANK + (j + 1) * P], pr[:, u % 2, j * P:(j + 1) * P],
                                            E.ident)
                    last.then_inc(turned, 1)
                if t >= 3:
                    u = t - 3
                    h, i, k0, k1 = units[u]
                    pe.wait_ge(evac_a, u + 1)
                    pe.wait_ge(evac_v, u + 1)
                    if u >= 2:
                        pe.wait_ge(done, u - 1)
                    J = (k1 - k0) // P
                    for j in range(J):
                        last = pe.matmul(E.bank(6 + u % 2, 64), pT[:, u % 2, j * P:(j + 1) * P],
                                         V[:, k0 // P + j, h * 64:(h + 1) * 64], start=(j == 0), stop=(j == J - 1))
                    last.then_inc(summed, 1)

        @block.scalar
        def _(act):
            for t in range(n + 2):
                if t < n:
                    L = units[t][3] - units[t][2]
                    act.wait_ge(maxed, t + 1)
                    if t >= 2:
                        act.wait_ge(turned, t - 1)
                    act.activation(pr[:, t % 2, 0:L], score(t, L), ACT.Exp, bias=neg[:, t:t + 1],
                                   accum_out=tot[:, t:t + 1]).then_inc(exped, 1)
                if t >= 2:
                    u = t - 2
                    L = min(BANK, units[u][3] - units[u][2])
                    act.wait_ge(turned, u + 1)
                    if u >= 2:
                        act.wait_ge(summed, u - 1)
                    act.activation(pT[:, u % 2, 0:L], E.bank(4, L), ACT.Copy).then_inc(evac_a, 1)

        @block.vector
        def _(dve):
            for t in range(n + 4):
                if t < n:
                    L = units[t][3] - units[t][2]
                    dve.wait_ge(scored, t + 1)
                    dve.tensor_reduce(neg[:, t:t + 1], score(t, L), AX.X, ALU.max, negate=True).then_inc(maxed, 1)
                if 2 <= t <= n + 1:
                    u = t - 2
                    L = units[u][3] - units[u][2]
                    dve.wait_ge(turned, u + 1)
                    if u >= 2:
                        dve.wait_ge(summed, u - 1)
                    if L > BANK:
                        dve.tensor_copy(pT[:, u % 2, BANK:L], E.bank(5, L - BANK)).then_inc(evac_v, 1)
                        dve.reciprocal(inv[:, u:u + 1], tot[:, u:u + 1])
                    else:
                        dve.reciprocal(inv[:, u:u + 1], tot[:, u:u + 1]).then_inc(evac_v, 1)
                if t >= 4:
                    u = t - 4
                    h, i, _, _ = units[u]
                    dve.wait_ge(summed, u + 1)
                    dve.tensor_scalar(O[:, i, h * 64:(h + 1) * 64], E.bank(6 + u % 2, 64), inv[:, u:u + 1], None,
                                      ALU.mult).then_inc(done, 1)


GLA_C = 64
NCH = TT // GLA_C


def step_of(z, ch):
    return (ch + 4 if ch < 8 else ch - 8) if z == 0 else 11 - ch


def gla(E, gq, gk, gv, gg, glow):
    nc, d, sem = E.nc, E.d, E.sem
    C = GLA_C
    full = [P, 4, TT]
    with ExitStack() as c:
        sb = lambda n, s: c.enter_context(nc.sbuf_tensor(n, s, FP))
        gate_up, reset, masks = sb("gla_gate_up", [32, 2, 256]), sb("gla_reset", [P, TT]), sb("gla_masks", [P, 2, P])
        dec = sb("gla_dec", [P, 4, NCH])
        lg, B, qd, ki = sb("gla_lg", full), sb("gla_B", full), sb("gla_qd", full), sb("gla_ki", full)
        zeroed, loaded, logits, biased, a, v = (sem(f"gla_{x}") for x in ("zeroed", "loaded", "logits", "biased", "act", "dve"))
        with nc.Block() as block:
            @block.gpsimd
            def _(pool):
                pool.memset(gate_up[:], 0.0).then_inc(zeroed, 1)

            @block.sync
            def _(sp):
                sp.dma_start(reset[:], E.cst("reset64")).then_inc(loaded, 16)
                sp.dma_start(masks[:, 0, :], E.cst("fwd64")).then_inc(loaded, 16)
                sp.dma_start(masks[:, 1, :], E.cst("bwd64")).then_inc(loaded, 16)
                sp.wait_ge(zeroed, 1)
                for z in range(2):
                    sp.dma_start(gate_up[16 * z:16 * z + 16, z, :], d["gla_gate_up_2"][0, z]).then_inc(loaded, 16)

            @block.tensor
            def _(pe):
                pe.wait_ge(loaded, 80)
                for q in range(4):
                    for b, (t0, t1) in enumerate(((0, S), (S, TT))):
                        last = pe.matmul(E.bank(2 * q + b, t1 - t0), gate_up[:, q // 2, (q % 2) * P:(q % 2 + 1) * P],
                                         glow[:, t0:t1], start=True, stop=True)
                    last.then_inc(logits, 1)

            @block.scalar
            def _(act):
                for q in range(4):
                    act.wait_ge(logits, q + 1)
                    act.activation(lg[:, q, :], E.ps[:, 2 * q * BANK:2 * q * BANK + TT], ACT.Identity,
                                   bias=E.v("gla_gate_bias_2", q)).then_inc(biased, 1)
                act.wait_ge(v, 1)
                act.activation(B[:], B[:], ACT.Exp).then_inc(a, 1)
                act.wait_ge(a, 1)
                act.activation(B[:], B[:], ACT.Ln, bias=1.0).then_inc(a, 1)
                act.wait_ge(v, 7)
                act.activation(qd[:], B[:], ACT.Exp, scale=1 / 16).then_inc(a, 1)
                act.activation(ki[:], B[:], ACT.Exp, scale=-1 / 16).then_inc(a, 1)
                act.wait_ge(v, 8)
                act.activation(lg[:], lg[:], ACT.Exp, scale=1 / 16).then_inc(a, 1)
                act.activation(dec[:], dec[:], ACT.Exp, scale=1 / 16).then_inc(a, 1)

            @block.vector
            def _(dve):
                dve.wait_ge(biased, 4)
                dve.scalar_tensor_tensor(out=B[:], in0=lg[:], scalar=-1.0, in1=lg[:], op0=ALU.mult, op1=ALU.min).then_inc(v, 1)
                dve.wait_ge(a, 2)
                dve.scalar_tensor_tensor(out=lg[:], in0=lg[:], scalar=0.0, in1=B[:], op0=ALU.min, op1=ALU.subtract)\
                   .then_inc(v, 1)
                dve.wait_ge(loaded, 80)
                dve.wait_ge(v, 2)
                for q in range(4):
                    last = dve.tensor_tensor_scan(B[:, q, :], reset[:], lg[:, q, :], 0.0, ALU.mult, ALU.add)
                last.then_inc(v, 1)
                dve.wait_ge(v, 3)
                ch = lambda x: x.rearrange("p q (c t) -> p q c t", t=C)
                flat = lambda x: x.rearrange("p q (c t) -> p (q c) t", t=C)
                dve.tensor_copy(dec[:], ch(B[:])[:, :, :, C - 1]).then_inc(v, 1)
                dve.wait_ge(v, 4)
                tot = dec[:].rearrange("p q c -> p (q c)").unsqueeze(2)
                dve.tensor_tensor(lg[:, 2:4, :], lg[:, 2:4, :], B[:, 2:4, :], ALU.subtract).then_inc(v, 1)
                dve.wait_ge(v, 5)
                dve.tensor_tensor(flat(B[:, 2:4, :]), flat(lg[:, 2:4, :]), tot[:, 24:48].to_broadcast([P, 24, C]), ALU.add)\
                   .then_inc(v, 2)
                dve.wait_ge(v, 7)
                dve.tensor_tensor(flat(lg[:]), tot.to_broadcast([P, 48, C]), flat(B[:]), ALU.subtract).then_inc(v, 1)
                dve.wait_ge(a, 5)
                for z in range(2):
                    dve.tensor_tensor(qd[:, 2 * z:2 * z + 2, :], qd[:, 2 * z:2 * z + 2, :], gq[:], ALU.mult)
                    dve.tensor_tensor(ki[:, 2 * z:2 * z + 2, :], ki[:, 2 * z:2 * z + 2, :], gk[:], ALU.mult)
                    dve.tensor_tensor(lg[:, 2 * z:2 * z + 2, :], lg[:, 2 * z:2 * z + 2, :], gk[:], ALU.mult)
        kt = B[:].rearrange("p q t -> p (q t)").rearrange("p (i n) -> p i n", n=512)
        turn(E, "gla_kturn", [([lg[:, q, i * P:(i + 1) * P] for q in range(4)], kt[:, i, :]) for i in range(6)])
        St = sb("gla_states", [P, 4, P, NCH])
        gains, out, decd, scanned = (sem(f"gla_{x}") for x in ("gains", "gains_out", "decay_spread", "scanned"))
        with ExitStack() as c2:
            dS, decx = (c2.enter_context(nc.sbuf_tensor(n, [P, P, NCH], FP)) for n in ("gla_dS", "gla_decx"))
            block = c2.enter_context(nc.Block())

            def place(z, t):
                return (0, t if z == 0 else 3 - t) if t < 4 else (1, t - 4 if z == 0 else 5 - t)

            @block.tensor
            def _(pe):
                for q in range(4):
                    z, j = q // 2, q % 2
                    if q >= 2:
                        pe.wait_ge(out, q - 1)
                    for t in range(6):
                        for r in range(2):
                            half, slot = place(z, t)
                            at = (4 * (q % 2) + 2 * r + half) * BANK + P * slot
                            for h2 in range(2):
                                last = pe.matmul(E.ps[64 * h2:64 * h2 + 64, at:at + P],
                                                 kt[64 * r:64 * r + 64, t, q * P + 64 * h2:q * P + 64 * h2 + 64],
                                                 gv[64 * r:64 * r + 64, t, (2 * j + h2) * P:(2 * j + h2 + 1) * P],
                                                 start=True, stop=True)
                    last.then_inc(gains, 1)

            @block.scalar
            def _(act):
                for q in range(4):
                    z = q // 2
                    act.wait_ge(gains, q + 1)
                    if q >= 1:
                        act.wait_ge(scanned, q)
                    for r in range(2):
                        for half, n, first in ((0, 4, 4 + r if z == 0 else 5 - r), (1, 2, r if z == 0 else 1 - r)):
                            last = act.activation(dS[:, :, first:first + 2 * n - 1:2].rearrange("p v s -> p s v"),
                                                  E.bank(4 * (q % 2) + 2 * r + half, n * P).rearrange("p (s v) -> p s v", v=P),
                                                  ACT.Copy)
                    last.then_inc(out, 1)

            @block.vector
            def _(dve):
                m = 0
                for q in range(4):
                    for ch in range(NCH):
                        last = dve.tensor_copy(decx[:, :, step_of(q // 2, ch):step_of(q // 2, ch) + 1],
                                               dec[:, q:q + 1, ch:ch + 1].to_broadcast([P, P, 1]))
                    last.then_inc(decd, 1)
                    dve.wait_ge(decd, 2 * q + 1)
                    dve.memset(decx[:, :, 0:1], 0.0).then_inc(decd, 1)
                    dve.wait_ge(decd, 2 * q + 2)
                    dve.wait_ge(out, q + 1)
                    dve.tensor_tensor_scan(St[:, q].rearrange("p v s -> p (v s)"), decx[:].rearrange("p v s -> p (v s)"),
                                           dS[:].rearrange("p v s -> p (v s)"), 0.0, ALU.mult, ALU.add).then_inc(scanned, 1)
                    dve.wait_ge(scanned, q + 1)
        AT = sb("gla_AT", [P, 2, 2, P])
        oT = lg
        scored, masked, summed, taken = (sem(f"gla_{x}") for x in ("scored", "masked", "summed", "taken"))
        units = [(h, t) for h in range(4) for t in range(6)]
        n = len(units)
        with nc.Block() as block:
            @block.tensor
            def _(pe):
                for u in range(n + 1):
                    if u < n:
                        h, t = units[u]
                        lo, j = 64 * (h % 2), h // 2
                        if u >= 2:
                            pe.wait_ge(masked, u - 1)
                        for z in range(2):
                            last = pe.matmul(E.bank(u % 2, 2 * P)[:, z * P:(z + 1) * P], ki[lo:lo + 64, 2 * z + j, t * P:(t + 1) * P],
                                             qd[lo:lo + 64, 2 * z + j, t * P:(t + 1) * P], start=True, stop=True)
                        last.then_inc(scored, 1)
                    if u >= 1:
                        w = u - 1
                        h, t = units[w]
                        lo, j = 64 * (h % 2), h // 2
                        pe.wait_ge(masked, w + 1)
                        if w >= 2:
                            pe.wait_ge(taken, w - 1)
                        o = E.bank(2 + w % 2, P)
                        for z in range(2):
                            last = pe.matmul(o, gv[:, t, h * P:(h + 1) * P], AT[:, w % 2, z, :], start=(z == 0), stop=False,
                                             skip_group_check=True)
                        for z in range(2):
                            for r in range(2):
                                st = step_of(z, 2 * t + r)
                                if st:
                                    last = pe.matmul(o[:, 64 * r:64 * r + 64], St[lo:lo + 64, 2 * z + j, :, st - 1],
                                                     qd[lo:lo + 64, 2 * z + j, (2 * t + r) * 64:(2 * t + r + 1) * 64],
                                                     start=False, stop=(z == 1 and r == 1), skip_group_check=True)
                        last.then_inc(summed, 1)

            @block.vector
            def _(dve):
                for u in range(n):
                    dve.wait_ge(scored, u + 1)
                    if u >= 2:
                        dve.wait_ge(summed, u - 1)
                    dve.tensor_tensor(AT[:, u % 2], masks[:], E.bank(u % 2, 2 * P).rearrange("p (z t) -> p z t", z=2),
                                      ALU.mult).then_inc(masked, 1)

            @block.scalar
            def _(act):
                for u, (h, t) in enumerate(units):
                    act.wait_ge(summed, u + 1)
                    act.activation(oT[:, h, t * P:(t + 1) * P], E.bank(2 + u % 2, P), ACT.Copy).then_inc(taken, 1)
        gated_norm(E, "gla_norm", oT, E.aT[:, 4:8, :], 4, TT, P, E.ones, lambda k: E.v("gla_o_norm_2", 0), gg)


def odd_mixer(E):
    nc, d, sem = E.nc, E.d, E.sem
    w = d["gdn_w_in_2"][0]
    gate_dram = nc.dram_tensor("gdn_gate", [P, KT, S], FP).ap()
    ab_dram = nc.dram_tensor("gdn_ab", [2, 16, TT], FP).ap()
    with ExitStack() as c:
        sb = lambda n, s: c.enter_context(nc.sbuf_tensor(n, s, FP))
        gate, la, be = sb("gdn_gate_sb", [P, KT, S]), sb("gdn_la_rows", [16, TT]), sb("gdn_be_rows", [16, TT])
        silu = lambda dst: act_copy(dst, ACT.Silu)
        ws = [kn(w[:, a:b]) for a, b in ((2048, 2560), (2560, 3072), (3072, 3104))]
        ahead = c.enter_context(ExitStack())
        ring = ring_of(E, ahead, "proj3", ws)
        modulated_norm(E, "odd_norm", 1, 0, TT)
        gemm(E, "proj3", [dict(w=ws[g],
                               units=[feature_unit(E, E.aT, n * P, P, 0, S, "act", silu(gate[:, 4 * g + n, :]))
                                      for n in range(4)]) for g in range(2)] + [
            dict(w=ws[2], units=[feature_unit(E, E.aT, 16 * i, 16, a, b, "dve", dve_copy(x[:, a:b]))
                                               for i, x in enumerate((la, be)) for a, b in ((0, S), (S, TT))])],
             split=(E.aT, KT, S), ahead=ring)
        ahead.close()
        decay_and_beta(E, gate, la, be, gate_dram, ab_dram)
    with ExitStack() as c:
        sb = lambda n, s: c.enter_context(nc.sbuf_tensor(n, s, FP))
        G = Parts()
        raw = sb("gdn_raw", [P, 4 * (S + 3 * TT)])
        q, k = raw[:, 0:4 * S].rearrange("a (p t) -> a p t", p=4), raw[:, 4 * S:4 * (S + TT)].rearrange("a (p t) -> a p t", p=4)
        vc = raw[:, 4 * (S + TT):4 * (S + 3 * TT)].rearrange("a (p c h t) -> a p c h t", p=4, c=NCH, h=2)
        G.K = E.aT[:].rearrange("p k t -> p (k t)").rearrange("p (c q n) -> p c q n", c=NCH, q=4)
        G.LA, G.BE, G.GC, G.EGL, G.GE, G.BEG = (sb(f"gdn_{n}", [P, 2, 4, NCH])
                                                for n in ("LA", "BE", "GC", "EGL", "GE", "BEG"))
        with ExitStack() as c2:
            FR = mybir.dt.float32r
            short_conv(E, w, q, k, vc, *(c2.enter_context(nc.sbuf_tensor(f"conv_{n}", shape, FR)) for n, shape in (
                ("x_high", [P, KT, TT]), ("x_low", [P, KT, TT]), ("w_parts", [P, 2, 2, KT, P]))))
        G.KT, G.QT, G.V = sb("gdn_KT", [P, NCH, 4, P]), sb("gdn_QT", [P, 8, 4, P]), sb("gdn_V", [P, NCH, 4, P])
        l2_blocks(E, G, q, k)
        turn(E, "gdn_vturn", [([vc[:, p, ch].rearrange("a h t -> a (h t)") for p in range(4)],
                               G.V[:, ch].rearrange("a p n -> a (p n)")) for ch in range(NCH)])
        turn(E, "gdn_kturn2", [([G.KT[:, ch, p, :] for p in range(4)], G.K[:, ch].rearrange("a p n -> a (p n)"))
                               for ch in range(NCH)])
        chunk_scalars(E, G, ab_dram)
        O = raw[:, 0:KT * S].rearrange("a (k t) -> a k t", k=KT)
        delta(E, G, O, raw[:, KT * S:])
        load(E, "gdn_gate_back", [(G.V[:].rearrange("a c p n -> a (c p n)")[:, 0:KT * S],
                                   gate_dram.rearrange("p k t -> p (k t)"))])
        gate = G.V[:].rearrange("a c p n -> a (c p n)")[:, 0:KT * S].rearrange("a (k t) -> a k t", t=S)
        gated_norm(E, "gdn_norm", O, E.aT, KT, S, P, E.ones, lambda k: E.v("gdn_o_norm_2", 0), gate)
    resid_gemm(E, "wout3", d["gdn_w_out_2"][0], E.aT, S, lambda n, s: E.mod[:, 1, 16 + n, s:s + 1])


def decay_and_beta(E, gate, la, be, gate_dram, ab_dram):
    nc, d, sem = E.nc, E.d, E.sem
    with ExitStack() as c:
        col, e = c.enter_context(nc.sbuf_tensor("gdn_cols", [16, 2], FP)), c.enter_context(nc.sbuf_tensor("gdn_e", [16, TT], FP))
        loaded, stored, a, v = (sem(f"ab_{x}") for x in ("loaded", "stored", "act", "dve"))
        with nc.Block() as block:
            @block.sync
            def _(sp):
                sp.dma_start(col[:, 0:1], d["gdn_dt_bias_2"].rearrange("o z (h i) -> (o z h) i", i=1)).then_inc(loaded, 16)
                sp.dma_start(col[:, 1:2], d["gdn_a_log_2"].rearrange("o z (h i) -> (o z h) i", i=1)).then_inc(loaded, 16)
                sp.dma_start(gate_dram, gate[:]).then_inc(stored, 16)
                sp.wait_ge(v, 8)
                sp.dma_start(ab_dram[0], la[:]).then_inc(stored, 16)
                sp.dma_start(ab_dram[1], be[:]).then_inc(stored, 16)
                sp.wait_ge(stored, 48)

            @block.scalar
            def _(act):
                act.wait_ge(loaded, 32)
                act.activation(col[:, 1:2], col[:, 1:2], ACT.Exp).then_inc(a, 1)
                act.activation(be[:], be[:], ACT.Exp, scale=-1.0).then_inc(a, 1)
                act.wait_ge(v, 2)
                act.activation(e[:], e[:], ACT.Exp).then_inc(a, 1)
                act.wait_ge(a, 3)
                act.activation(e[:], e[:], ACT.Ln, bias=1.0).then_inc(a, 1)

            @block.vector
            def _(dve):
                dve.wait_ge(loaded, 32)
                dve.tensor_scalar(la[:], la[:], col[:, 0:1], None, ALU.add).then_inc(v, 1)
                dve.wait_ge(v, 1)
                dve.scalar_tensor_tensor(out=e[:], in0=la[:], scalar=-1.0, in1=la[:], op0=ALU.mult, op1=ALU.min)\
                   .then_inc(v, 1)
                dve.wait_ge(a, 4)
                dve.tensor_scalar(be[:], be[:], 1.0, None, ALU.add).then_inc(v, 1)
                dve.scalar_tensor_tensor(out=la[:], in0=la[:], scalar=0.0, in1=e[:], op0=ALU.max, op1=ALU.add).then_inc(v, 1)
                dve.wait_ge(v, 4)
                dve.reciprocal(be[:], be[:]).then_inc(v, 1)
                dve.tensor_scalar(la[:], la[:], col[:, 1:2], -1.0, ALU.mult, ALU.mult).then_inc(v, 3)


def short_conv(E, w, q, k, vc, xh, xl, wp):
    nc, d, sem = E.nc, E.d, E.sem
    tiles = 16
    cols = 256
    with ExitStack() as c:
        sb = lambda n, s: c.enter_context(nc.sbuf_tensor(n, s, FP))
        ring, x, y = sb("conv_ring", [P, 2, KT, cols]), sb("conv_x", [P, 2, TT + 3]), sb("conv_y", [P, 2, TT + 1])
        loaded = [sem(f"conv_w_loaded{i}") for i in range(2)]
        zeroed, full, padded, v, out, w_high, w_low, x_high, x_low = (sem(f"conv_{n}") for n in (
            "zeroed", "full", "padded", "dve", "out", "w_high", "w_low", "x_high", "x_low"))
        panel = lambda n: ring[:, (n // 2) % 2, :, (n % 2) * P:(n % 2 + 1) * P]
        cw = VEC_AT["gdn_conv_w_2"]
        with nc.Block() as block:
            @block.sync
            def _(sp):
                for g in range(tiles // 2):
                    if g >= 2:
                        sp.wait_ge(w_low, 2 * (g - 1))
                    sp.dma_start(ring[:, g % 2], kn(w[:, g * cols:(g + 1) * cols])).then_inc(loaded[g % 2], 16)

            @block.tensor
            def _(pe):
                for n in range(tiles):
                    pe.wait_ge(w_low, n + 1)
                    if n >= 4:
                        pe.wait_ge(padded, n - 3)
                    for half, (a, b) in enumerate(((0, S), (S, TT)) if n >= 4 else ((0, S),)):
                        for kk in range(KT):
                            if n == 0:
                                pe.wait_ge(x_low, kk + 1)
                            for i, (part, xp) in enumerate(((0, xh), (0, xl), (1, xh))):
                                last = pe.matmul(E.bank(2 * (n % 4) + half, b - a), wp[:, part, n % 2, kk, :], xp[:, kk, a:b],
                                                 start=(kk == 0 and i == 0), stop=(kk == KT - 1 and i == 2))
                    last.then_inc(full, 1)

            @block.scalar
            def _(act):
                def high(n):
                    act.wait_ge(loaded[(n // 2) % 2], 16 * (n // 4 + 1))
                    act.activation(wp[:, 0, n % 2], panel(n), ACT.Copy).then_inc(w_high, 1)
                high(0)
                for kk in range(KT):
                    act.activation(xh[:, kk, :], E.aT[:, kk, :], ACT.Copy).then_inc(x_high, 1)
                high(1)
                act.wait_ge(zeroed, 1)
                for n in range(tiles + 1):
                    if n < tiles:
                        act.wait_ge(full, n + 1)
                        if n >= 2:
                            act.wait_ge(v, 3 * (n - 1))
                        last = act.activation(x[:, n % 2, 1:S + 1], E.bank(2 * (n % 4)), ACT.Copy)
                        if n >= 4:
                            last = act.activation(x[:, n % 2, S + 2:TT + 2], E.bank(2 * (n % 4) + 1, CTX), ACT.Copy)
                        last.then_inc(padded, 1)
                        if n + 2 < tiles:
                            high(n + 2)
                    if n >= 1:
                        m = n - 1
                        act.wait_ge(v, 3 * m + 3)
                        lat, ctx_ = y[:, m % 2, 0:S], y[:, m % 2, S + 1:TT + 1]
                        if m < 4:
                            last = act.activation(q[:, m, :], lat, ACT.Silu)
                        elif m < 8:
                            act.activation(k[:, m - 4, 0:S], lat, ACT.Silu)
                            last = act.activation(k[:, m - 4, S:TT], ctx_, ACT.Silu)
                        else:
                            h = m - 8
                            act.activation(vc[:, h // 2, 0:8, h % 2, :], lat.rearrange("p (c t) -> p c t", t=64), ACT.Silu)
                            last = act.activation(vc[:, h // 2, 8:12, h % 2, :], ctx_.rearrange("p (c t) -> p c t", t=64),
                                                  ACT.Silu)
                        last.then_inc(out, 1)

            @block.gpsimd
            def _(pool):
                pool.memset(x[:], 0.0).then_inc(zeroed, 1)

            @block.vector
            def _(dve):
                def low(n):
                    dve.wait_ge(w_high, n + 1)
                    dve.tensor_tensor(wp[:, 1, n % 2], panel(n), wp[:, 0, n % 2].bitcast(FP), ALU.subtract).then_inc(w_low, 1)
                low(0)
                for kk in range(KT):
                    dve.wait_ge(x_high, kk + 1)
                    dve.tensor_tensor(xl[:, kk, :], E.aT[:, kk, :], xh[:, kk, :].bitcast(FP), ALU.subtract).then_inc(x_low, 1)
                low(1)
                for n in range(tiles):
                    dve.wait_ge(padded, n + 1)
                    if n + 2 < tiles:
                        low(n + 2)
                    if n >= 2:
                        dve.wait_ge(out, n - 1)
                    L = TT + 1 if n >= 4 else S
                    xs, ys = x[:, n % 2], y[:, n % 2, 0:L]
                    tap = lambda j: E.vcol[:, cw + 16 * j + n:cw + 16 * j + n + 1]
                    dve.tensor_scalar(ys, xs[:, 1:L + 1], tap(1), None, ALU.mult).then_inc(v, 1)
                    dve.wait_ge(v, 3 * n + 1)
                    dve.scalar_tensor_tensor(out=ys, in0=xs[:, 0:L], scalar=tap(0), in1=ys, op0=ALU.mult, op1=ALU.add)\
                       .then_inc(v, 1)
                    dve.wait_ge(v, 3 * n + 2)
                    dve.scalar_tensor_tensor(out=ys, in0=xs[:, 2:L + 2], scalar=tap(2), in1=ys, op0=ALU.mult, op1=ALU.add)\
                       .then_inc(v, 1)


def l2_blocks(E, G, q, k):
    nc, sem = E.nc, E.sem
    items = [("k", p) for p in range(4)] + [("q", p) for p in range(4)]
    zeroed, squared, summed, rooted, used = (sem(f"l2_{x}") for x in ("zeroed", "squared", "summed", "rooted", "used"))
    with ExitStack() as c:
        sb = lambda n, s: c.enter_context(nc.sbuf_tensor(n, s, FP))
        sq, rstd = sb("l2_sq", [P, 2, TT]), sb("l2_rstd", [P, 4, TT])
        with nc.Block() as block:
            @block.gpsimd
            def _(pool):
                pool.memset(G.KT[:], 0.0)
                pool.memset(G.QT[:], 0.0).then_inc(zeroed, 1)
            @block.scalar
            def _(act):
                for rnd, (x, T, scale) in enumerate(((k, TT, 1.0), (q, S, 64.0))):
                    for p in range(4):
                        n = 4 * rnd + p
                        if n >= 2:
                            act.wait_ge(summed, n - 1)
                        act.activation(sq[:, n % 2, 0:T], x[:, p, 0:T], ACT.Square).then_inc(squared, 1)
                    act.wait_ge(summed, 4 * rnd + 4)
                    for p in range(4):
                        if rnd == 1:
                            act.wait_ge(used, 2 * p + 2)
                        act.activation(rstd[:, p, 0:T], E.ps[:, 2 * p * BANK:2 * p * BANK + T], ACT.Ln, scale=scale,
                                       bias=scale * EPS).then_inc(rooted, 1)
                    act.wait_ge(rooted, 8 * rnd + 4)
                    for p in range(4):
                        act.activation(rstd[:, p, 0:T], rstd[:, p, 0:T], ACT.Exp, scale=-0.5).then_inc(rooted, 1)

            @block.tensor
            def _(pe):
                for rnd, T in enumerate((TT, S)):
                    if rnd == 1:
                        pe.wait_ge(rooted, 4)
                    for p in range(4):
                        n = 4 * rnd + p
                        pe.wait_ge(squared, n + 1)
                        for a, b in ((0, S), (S, TT))[:2 if T == TT else 1]:
                            last = pe.matmul(E.ps[:, 2 * p * BANK + a:2 * p * BANK + b], E.blk64, sq[:, n % 2, a:b],
                                             start=True, stop=True)
                        last.then_inc(summed, 1)

            @block.vector
            def _(dve):
                dve.wait_ge(zeroed, 1)
                for rnd, (x, dst, nch) in enumerate(((k, G.KT, NCH), (q, G.QT, 8))):
                    for p in range(4):
                        dve.wait_ge(rooted, 8 * rnd + 5 + p)
                        for h2 in range(2):
                            lo = 64 * h2
                            ch = lambda t: t.rearrange("a (c t) -> a c t", t=64)
                            dve.tensor_tensor(dst[lo:lo + 64, :, p, lo:lo + 64], ch(x[lo:lo + 64, p, :]),
                                              ch(rstd[lo:lo + 64, p, 0:nch * 64]), ALU.mult).then_inc(used, 1)


def chunk_scalars(E, G, ab_dram):
    nc, sem = E.nc, E.sem
    with ExitStack() as c:
        sb = lambda n, s: c.enter_context(nc.sbuf_tensor(n, s, FP))
        rows, U, G.EG = sb("gdn_rows", [96, 2, P]), sb("gdn_U0", [P, 2, P]), sb("gdn_EG", [P, 96])
        loaded, turned, copied, cum, v, a = (sem(f"sc_{x}") for x in ("loaded", "turned", "copied", "cum", "dve", "act"))
        f = lambda x: x[:].rearrange("a z p c -> a (z p c)")
        with nc.Block() as block:
            @block.sync
            def _(sp):
                for i in range(2):
                    for zp in range(8):
                        sp.dma_start(rows[12 * zp:12 * zp + 12, i, :].rearrange("c (h t) -> c h t", h=2),
                                     ab_dram[i, 2 * zp:2 * zp + 2, :].rearrange("h (c t) -> c h t", t=64)).then_inc(loaded, 16)
                sp.dma_start(U[:, 0, :], E.cst("fwd64")).then_inc(loaded, 16)
                sp.dma_start(U[:, 1, :], E.cst("bwd64")).then_inc(loaded, 16)

            @block.tensor
            def _(pe):
                pe.wait_ge(loaded, 18 * 16)
                for i in range(2):
                    last = pe.transpose(E.bank(i, 96), rows[:, i, :], E.ident[0:96, 0:96])
                last.then_inc(turned, 1)
                pe.wait_ge(copied, 1)
                for z in range(2):
                    pe.matmul(E.bank(2, 96)[:, 48 * z:48 * z + 48], U[:, z, :], f(G.LA)[:, 48 * z:48 * z + 48],
                              start=True, stop=True)
                pe.matmul(E.bank(3, 96), E.blk64, f(G.LA), start=True, stop=True).then_inc(cum, 1)

            @block.vector
            def _(dve):
                dve.wait_ge(turned, 1)
                dve.tensor_copy(f(G.LA), E.bank(0, 96))
                dve.tensor_copy(f(G.BE), E.bank(1, 96)).then_inc(copied, 1)
                dve.wait_ge(cum, 1)
                dve.tensor_copy(f(G.GC), E.bank(2, 96)).then_inc(v, 1)
                dve.wait_ge(v, 1)
                dve.tensor_tensor(f(G.EGL), E.bank(3, 96), f(G.GC), ALU.subtract).then_inc(v, 1)
                dve.wait_ge(a, 3)
                dve.tensor_tensor(f(G.BEG), f(G.BE), G.EG[:], ALU.mult)

            @block.scalar
            def _(act):
                act.wait_ge(v, 2)
                act.activation(f(G.GE), E.bank(3, 96), ACT.Exp).then_inc(a, 1)
                act.activation(f(G.EGL), f(G.EGL), ACT.Exp).then_inc(a, 1)
                act.activation(G.EG[:], f(G.GC), ACT.Exp).then_inc(a, 1)


LEVELS = 6
STEPS = NCH


def chunk_at(z, s):
    return (s + 8 if s < 4 else s - 4) if z == 0 else 11 - s


def steps_of(lat):
    up = [f"{x}{l}" for l in range(1, LEVELS) for x in ("M", "X", "T")][:-1]
    return {
        "pe": ["Gj", "KK"] + (["KQ"] if lat else []) + ["T0"] + up + ["U", "W", "WS"] + (["OS"] if lat else []) + ["DS"] +
              (["O"] if lat else []),
        "act": ["D"] + (["DT", "E"] if lat else []) + [f"{x}{l}" for l in range(1, LEVELS) for x in ("M", "T")][:-1] + ["u", "w"],
        "dve": ["t1", "t2"] + (["t3"] if lat else []) + ["N"] + (["qk"] if lat else []) + [f"T{l}" for l in range(LEVELS)] +
               ["vn", "S"] + (["O"] if lat else []),
        "pool": ["LU", "ke", "Vb", "Kb", "Dbeta"] + (["DTmask", "qd"] if lat else []) + ["N0", "I0"] +
                [f"N{l}" for l in range(1, LEVELS)],
    }


def delta(E, G, O, room):
    nc, sem = E.nc, E.sem
    sems = {e: [sem(f"delta_{e}{z}_done") for z in range(2)] for e in ("pe", "act", "dve", "pool")}

    def done(e, s, label):
        before = sum(len(steps_of(t >= 4)[e]) for t in range(s))
        return before + steps_of(s >= 4)[e].index(label) + 1

    with ExitStack() as c:
        sb = lambda n, s: c.enter_context(nc.sbuf_tensor(n, s, FP))
        U, lev = sb("gdn_U", [P, 2, P]), sb("gdn_levels", [P, LEVELS, 2, P])
        Z = []
        for z in range(2):
            B = Parts()
            (B.LU, B.t1, B.D, B.DT, B.Na, B.Nb, B.T, B.Tt, B.M, B.Vb, B.Kb, B.ke, B.vn, B.S) = (
                sb(f"gdn{z}_{n}", [P, 4, P]) if z else room[:, 4 * P * i:4 * P * (i + 1)].rearrange("a (p n) -> a p n", p=4)
                for i, n in enumerate(("LU", "t1", "D", "DT", "Na", "Nb", "T", "Tt", "M", "Vb", "Kb", "ke", "vn", "S")))
            Z.append(B)
            Z[z].Nl = (Z[z].Na, Z[z].Nb)
        cst_in, ready = sem("delta_cst"), sem("delta_ready")
        bank = lambda z, b: E.bank(4 * z + b).rearrange("a (p n) -> a p n", p=4)
        ident4 = E.ident.unsqueeze(1).to_broadcast([P, 4, P])
        mask4 = lambda m: m.unsqueeze(1).to_broadcast([P, 4, P])
        col4 = lambda x, z, ch: x[:, z, :, ch:ch + 1].to_broadcast([P, 4, P])

        def wait(eng, e, z, s, label):
            if s >= 0:
                eng.wait_ge(sems[e][z], done(e, s, label))

        with nc.Block() as block:
            @block.sync
            def _(sp):
                sp.dma_start(U[:, 0, :], E.cst("fwd64")).then_inc(cst_in, 16)
                sp.dma_start(U[:, 1, :], E.cst("bwd64")).then_inc(cst_in, 16)
                sp.dma_start(lev[:].rearrange("a l z n -> a (l z n)"), E.cst("levels")).then_inc(cst_in, 16)

            @block.tensor
            def _(pe):
                def each(z, b, lhsT, rhs, start=True, stop=True):
                    for p in range(4):
                        last = pe.matmul(bank(z, b)[:, p, :], lhsT(p), rhs(p), start=start, stop=stop, skip_group_check=True)
                    return last
                pe.wait_ge(ready, 1)
                for s in range(STEPS):
                    lat = s >= 4
                    for label in steps_of(lat)["pe"]:
                        for z in range(2):
                            B, ch = Z[z], chunk_at(z, s)
                            w = lambda e, l, t=s: wait(pe, e, z, t, l)
                            if label == "Gj":
                                w("pool", "LU")
                                w("dve", "t1", s - 1)
                                if s > 4:
                                    w("dve", "qk", s - 1)
                                last = pe.matmul(E.bank(4 * z), E.ones, B.LU[:].rearrange("a p n -> a (p n)"),
                                                 start=True, stop=True)
                            elif label == "KK":
                                w("act", "u", s - 1)
                                if s > 4:
                                    w("dve", "O", s - 1)
                                last = each(z, 1, lambda p: G.KT[:, ch, p, :], lambda p: G.KT[:, ch, p, :])
                            elif label == "KQ":
                                w("dve", "t1")
                                w("act", "E")
                                last = each(z, 0, lambda p: G.KT[:, ch, p, :], lambda p: G.QT[:, ch, p, :])
                            elif label == "T0":
                                w("pool", "N0")
                                w("dve", "vn", s - 1)
                                for p in range(4):
                                    last = pe.transpose(bank(z, 2)[:, p, :], B.Nl[0][:, p, :], E.ident)
                            elif label[0] == "M":
                                l = int(label[1])
                                w("pool", f"N{l}")
                                w("dve", f"T{l - 1}")
                                if l > 1:
                                    w("act", f"T{l - 1}")
                                last = each(z, 2, lambda p: B.Nl[l % 2][:, p, :], lambda p: B.Tt[:, p, :])
                            elif label[0] == "X":
                                l = int(label[1])
                                w("act", f"M{l}")
                                w("pool", "I0")
                                if l == 1:
                                    w("dve", "S", s - 1)
                                last = each(z, 3, lambda p: B.T[:, p, :], lambda p: B.M[:, p, :])
                            elif label[0] == "T":
                                w("dve", label)
                                for p in range(4):
                                    last = pe.transpose(bank(z, 2)[:, p, :], B.Tt[:, p, :], E.ident)
                            elif label == "U":
                                w("dve", "T5")
                                w("pool", "Kb")
                                last = each(z, 1, lambda p: B.Tt[:, p, :], lambda p: B.Vb[:, p, :])
                            elif label == "W":
                                last = each(z, 3, lambda p: B.Kb[:, p, :], lambda p: B.Tt[:, p, :])
                            elif label == "WS":
                                w("act", "w")
                                w("dve", "S", s - 1)
                                last = each(z, 2, lambda p: B.Kb[:, p, :], lambda p: B.S[:, p, :])
                            elif label == "OS":
                                w("pool", "qd")
                                for p in range(4):
                                    last = pe.matmul(bank(z, 1)[:, p, :], B.S[:, p, :], B.LU[:, p, :], start=(p == 0),
                                                     stop=False, skip_group_check=True)
                            elif label == "DS":
                                w("dve", "vn")
                                last = each(z, 3, lambda p: B.ke[:, p, :], lambda p: B.vn[:, p, :])
                            elif label == "O":
                                last = each(z, 1, lambda p: B.vn[:, p, :], lambda p: B.DT[:, p, :], start=False)
                            last.then_inc(sems["pe"][z], 1)

            @block.scalar
            def _(act):
                for s in range(STEPS):
                    lat = s >= 4
                    for label in steps_of(lat)["act"]:
                        for z in range(2):
                            B, ch = Z[z], chunk_at(z, s)
                            w = lambda e, l, t=s: wait(act, e, z, t, l)
                            if label == "D":
                                w("dve", "t2")
                                last = act.activation(B.D[:], B.D[:], ACT.Exp, scale=-1.0)
                            elif label == "DT":
                                w("dve", "t3")
                                last = act.activation(B.DT[:], B.DT[:], ACT.Exp)
                            elif label == "E":
                                w("pe", "Gj")
                                last = act.activation(B.t1[:], bank(z, 0), ACT.Exp)
                            elif label[0] == "M":
                                w("pe", label)
                                if label == "M1":
                                    w("pe", "X5", s - 1)
                                last = act.activation(B.M[:], bank(z, 2), ACT.Copy)
                            elif label[0] == "T":
                                w("pe", label)
                                last = act.activation(B.T[:], bank(z, 2), ACT.Copy)
                            elif label == "u":
                                w("pe", "U")
                                last = act.activation(B.Vb[:], bank(z, 1), ACT.Copy)
                            elif label == "w":
                                w("pe", "W")
                                last = act.activation(B.Kb[:], bank(z, 3), ACT.Copy)
                            last.then_inc(sems["act"][z], 1)

            @block.vector
            def _(dve):
                for z in range(2):
                    dve.memset(Z[z].S[:], 0.0)
                dve.memset(O[:], 0.0).then_inc(ready, 1)
                dve.wait_ge(ready, 1)
                for s in range(STEPS):
                    lat = s >= 4
                    for label in steps_of(lat)["dve"]:
                        for z in range(2):
                            B, ch = Z[z], chunk_at(z, s)
                            w = lambda e, l, t=s: wait(dve, e, z, t, l)
                            if label == "t1":
                                w("pe", "Gj")
                                if s > 4:
                                    w("pool", "qd", s - 1)
                                last = dve.tensor_tensor(B.t1[:], bank(z, 0), col4(G.GC, z, ch), ALU.subtract)
                            elif label == "t2":
                                w("dve", "t1")
                                w("pool", "N5", s - 1)
                                last = dve.tensor_scalar(B.D[:], B.t1[:], 0.0, None, ALU.max)
                            elif label == "t3":
                                if s > 4:
                                    w("pe", "O", s - 1)
                                last = dve.tensor_scalar(B.DT[:], B.t1[:], 0.0, None, ALU.min)
                            elif label == "N":
                                w("pool", "Dbeta")
                                w("pe", "KK")
                                last = dve.tensor_tensor(B.D[:], B.D[:], bank(z, 1), ALU.mult)
                            elif label == "qk":
                                w("pool", "DTmask")
                                w("pe", "KQ")
                                last = dve.tensor_tensor(B.DT[:], B.DT[:], bank(z, 0), ALU.mult)
                            elif label == "T0":
                                w("pe", "T0")
                                w("pe", "W", s - 1)
                                last = dve.tensor_tensor(B.Tt[:], ident4, bank(z, 2), ALU.subtract)
                            elif label[0] == "T":
                                w("pe", "X" + label[1])
                                w("dve", f"T{int(label[1]) - 1}")
                                last = dve.tensor_tensor(B.Tt[:], B.Tt[:], bank(z, 3), ALU.subtract)
                            elif label == "vn":
                                w("pe", "WS")
                                w("act", "u")
                                w("pe", "O" if s > 4 else "DS", s - 1)
                                last = dve.tensor_tensor(B.vn[:], B.Vb[:], bank(z, 2), ALU.subtract)
                            elif label == "S":
                                w("pe", "DS")
                                w("dve", "S", s - 1)
                                for p in range(4):
                                    last = dve.scalar_tensor_tensor(out=B.S[:, p, :], in0=B.S[:, p, :],
                                                                    scalar=G.GE[:, z, p, ch:ch + 1], in1=bank(z, 3)[:, p, :],
                                                                    op0=ALU.mult, op1=ALU.add)
                            elif label == "O":
                                w("pe", "O")
                                if z == 1:
                                    wait(dve, "dve", 0, s, "O")
                                elif s > 4:
                                    wait(dve, "dve", 1, s - 1, "O")
                                o = O[:, :, 64 * ch:64 * ch + 64]
                                last = dve.tensor_tensor(o, o, E.bank(4 * z + 1).rearrange("a (h t) -> a h t", t=64), ALU.add)
                            last.then_inc(sems["dve"][z], 1)

            @block.gpsimd
            def _(pool):
                pool.wait_ge(cst_in, 48)
                for s in range(STEPS):
                    lat = s >= 4
                    for label in steps_of(lat)["pool"]:
                        for z in range(2):
                            B, ch = Z[z], chunk_at(z, s)
                            w = lambda e, l, t=s: wait(pool, e, z, t, l)
                            tt = lambda out, a, b: pool.tensor_tensor(out, a, b, ALU.mult)
                            if label == "LU":
                                w("pe", "O" if s > 4 else "Gj", s - 1)
                                last = tt(B.LU[:], mask4(U[:, z, :]), col4(G.LA, z, ch))
                            elif label == "ke":
                                w("pe", "DS", s - 1)
                                last = tt(B.ke[:], G.K[:, ch], col4(G.EGL, z, ch))
                            elif label == "Vb":
                                w("dve", "vn", s - 1)
                                last = tt(B.Vb[:], G.V[:, ch], col4(G.BE, z, ch))
                            elif label == "Kb":
                                w("pe", "WS", s - 1)
                                last = tt(B.Kb[:], G.K[:, ch], col4(G.BEG, z, ch))
                            elif label == "Dbeta":
                                w("act", "D")
                                last = tt(B.D[:], B.D[:], col4(G.BE, z, ch))
                            elif label == "DTmask":
                                w("act", "DT")
                                last = tt(B.DT[:], B.DT[:], mask4(U[:, z, :]))
                            elif label == "qd":
                                w("act", "E")
                                w("pe", "Gj")
                                last = tt(B.LU[:], G.QT[:, ch], B.t1[:])
                            elif label == "I0":
                                w("pool", "N0")
                                w("pe", "X5", s - 1)
                                last = pool.tensor_tensor(B.T[:], ident4, B.Nl[0][:], ALU.subtract)
                            else:
                                l = int(label[1])
                                w("dve", "N")
                                if l == 0:
                                    w("pe", "M4", s - 1)
                                elif l == 1:
                                    w("pe", "M5", s - 1)
                                elif l == 2:
                                    w("pe", "T0")
                                    w("pool", "I0")
                                else:
                                    w("pe", f"M{l - 2}")
                                last = tt(B.Nl[l % 2][:], B.D[:], mask4(lev[:, l, 1 - z, :]))
                            last.then_inc(sems["pool"][z], 1)


def build_program(nc, d, out):
    with ExitStack() as ctx:
        E = setup(nc, ctx, d)
        with nc.sbuf_tensor("ctx_rows", [P, 2, D], FP) as cr:
            load(E, "ctx", [(cr[:], d["ctx_2"][0].rearrange("(t p) n -> p t n", p=P))])
            turn(E, "cturn", [([cr[:, t, k * P:(k + 1) * P] for t in range(2)], E.hT[:, k, S:TT]) for k in range(KT)])
        for part in (lambda: attention_and_hgrn(E), lambda: moe(E), lambda: modulation(E), lambda: even_mixer(E),
                     lambda: mlp(E, 0, TT), lambda: odd_mixer(E), lambda: mlp(E, 1, S), lambda: put_out(E, out)):
            with nc.cleanup_on_exit():
                part()


def put_out(E, out):
    nc = E.nc
    norm(E, "last_norm", E.hT, E.aT, KT, D, S, lambda k, s: E.v("final_norm_2", k))
    with nc.sbuf_tensor("out_rows", [P, 4, D], FP) as rows:
        turn(E, "out_turn", [([E.aT[:, k, t * P:(t + 1) * P] for k in ks], rows[:, t, ks[0] * P:(ks[-1] + 1) * P])
                             for t in range(4) for ks in ((0, 1, 2, 3), (4, 5, 6, 7))])
        stored = E.sem("out_stored")
        with nc.Block() as block:
            @block.sync
            def _(sp):
                sp.dma_start(out[0].rearrange("(t p) n -> p t n", p=P), rows[:]).then_inc(stored, 16)
                sp.wait_ge(stored, 16)


WHOLE = ["x", "w_in", "w_out", "w_group", "b_group", "w_router", "b_router", "w_gate", "w_up", "w_down", "ctx_2",
         "ada_w_2", "mlp_w1_2", "mlp_w2_2", "even_w_in_2", "mla_w_uq_2", "mla_w_ukv_2", "gla_gate_up_2",
         "even_w_out_2", "gdn_w_in_2", "gdn_a_log_2", "gdn_dt_bias_2", "gdn_w_out_2"]


def kernel(**inputs):
    import numpy as _np
    import concourse.bacc as _bacc
    from concourse import mybir as _mybir
    from concourse.bass_utils import run_bass_kernel_spmd as _run

    nc = _bacc.Bacc("TRN2", target_bir_lowering=False, num_devices=1)
    host = {name: _np.ascontiguousarray(inputs[name]) for name in WHOLE}
    host["vec"] = _np.concatenate([_np.asarray(inputs[name]).reshape(-1, P) for name, _ in VEC_ROWS])
    host["cst"] = constants()
    arrays, d = {}, {}
    for name, a in host.items():
        arrays[f"in_{name}_dram"] = a
        d[name] = nc.dram_tensor(f"in_{name}_dram", a.shape, _mybir.dt.from_np(a.dtype), kind="ExternalInput").ap()
    out = nc.dram_tensor("out_0_dram", (1, S, D), FP, kind="ExternalOutput").ap()
    build_program(nc, d, out)
    r = _run(nc, [arrays], core_ids=[0])
    return r.results[0]["out_0_dram"]
```
